# Optimizing a Trainium2 kernel written in Bass

```python
import math
import jax, jax.numpy as jnp
from jax import lax
import numpy as np

D_MODEL = 1024
BATCH = 1
SEQ = 256
DEPTH = 2

N_HEADS_A = 8
HEAD_DIM_A = 64
D_A = N_HEADS_A * HEAD_DIM_A
ATTN_PATTERNS = ((128, 1), (512, 4), (2048, 16))
ATTN_BLOCK = 128
NUM_BUCKETS = 32
MAX_DISTANCE = 2048
N_HEADS_M = 4
HEAD_DIM_M = 128
D_M = N_HEADS_M * HEAD_DIM_M
CONV_K = 4
MLSTM_CHUNK = 128
P_IN = 3 * D_A + 2 * D_M
D_FF = 2816
N_EXPERTS = 8
TOP_K = 2
D_FF_E = 3584
N_DENSE = (DEPTH + 1) // 2
N_MOE = DEPTH // 2
ALPHA = (2.0 * DEPTH) ** 0.25
BETA = (8.0 * DEPTH) ** -0.25
LN_EPS = 1e-5


def layer_norm(x, g, b):
    xf = x.astype(jnp.float32)
    mu = xf.mean(-1, keepdims=True)
    var = jnp.square(xf - mu).mean(-1, keepdims=True)
    return ((xf - mu) * lax.rsqrt(var + LN_EPS) * g.astype(jnp.float32) + b.astype(jnp.float32)).astype(x.dtype)

def rel_bucket(dist):
    exact = NUM_BUCKETS // 2
    d = jnp.maximum(dist, exact).astype(jnp.float32)
    log_b = exact + (jnp.log(d / exact) / math.log(MAX_DISTANCE / exact) * (NUM_BUCKETS - exact)).astype(jnp.int32)
    return jnp.where(dist < exact, dist, jnp.minimum(log_b, NUM_BUCKETS - 1))

def strided_window_attention(q, k, v, rel_bias, window, dilation):
    B, S, H, hd = q.shape
    L = S // dilation
    W = window // dilation
    blk = ATTN_BLOCK
    nb = -(-L // blk)
    Lp = nb * blk

    def to_classes(t):
        t = t.reshape(B, L, dilation, H, hd).transpose(0, 2, 1, 3, 4).reshape(B * dilation, L, H, hd)
        return jnp.pad(t, ((0, 0), (0, Lp - L), (0, 0), (0, 0)))

    qc, kc, vc = to_classes(q), to_classes(k), to_classes(v)
    qb = qc.reshape(B * dilation, nb, blk, H, hd)

    def band(t):
        t = jnp.pad(t, ((0, 0), (blk, 0), (0, 0), (0, 0))).reshape(B * dilation, nb + 1, blk, H, hd)
        return jnp.concatenate([t[:, :-1], t[:, 1:]], axis=2)

    kb, vb = band(kc), band(vc)
    qi = jnp.arange(blk)[:, None]
    kj = jnp.arange(2 * blk)[None, :]
    rel = qi + blk - kj
    bias = rel_bias[rel_bucket(jnp.maximum(rel, 0) * dilation)]
    bias = bias.transpose(2, 0, 1).astype(jnp.float32)
    key_pos = jnp.arange(nb)[:, None] * blk - blk + kj
    mask = ((rel >= 0) & (rel <= W))[None] & (key_pos >= 0)[:, None, :]

    logits = jnp.einsum('bnqhd,bnkhd->bnhqk', qb.astype(jnp.float32), kb.astype(jnp.float32)) * (hd ** -0.5) + bias
    logits = jnp.where(mask[None, :, None], logits, -jnp.inf)
    m = logits.max(-1, keepdims=True)
    p = jnp.exp(logits - m)
    denom = p.sum(-1, keepdims=True)
    o = jnp.einsum('bnhqk,bnkhd->bnqhd', p / denom, vb.astype(jnp.float32))
    lse = (m + jnp.log(denom))[..., 0].transpose(0, 1, 3, 2)

    def from_classes(t):
        t = t.reshape((B * dilation, Lp) + t.shape[3:])[:, :L]
        t = t.reshape((B, dilation, L) + t.shape[2:])
        t = jnp.moveaxis(t, 1, 2)
        return t.reshape((B, S) + t.shape[3:])

    return from_classes(o), from_classes(lse)

def dilated_attention(q, k, v, rel_bias):
    outs, lses = [], []
    for window, dilation in ATTN_PATTERNS:
        o, lse = strided_window_attention(q, k, v, rel_bias, window, dilation)
        outs.append(o)
        lses.append(lse)
    wts = jax.nn.softmax(jnp.stack(lses), axis=0)
    return jnp.einsum('pbsh,pbshd->bshd', wts, jnp.stack(outs))

def mlstm_chunkwise(q, k, v, i_pre, log_f):
    B, S, H, hd = q.shape
    L = MLSTM_CHUNK
    nc = S // L
    k = k * (hd ** -0.5)
    tri = jnp.tril(jnp.ones((L, L), dtype=bool))

    def chunks(t):
        return jnp.moveaxis(t.reshape((B, nc, L) + t.shape[2:]), 1, 0)

    def step(carry, xs):
        C, n, m = carry
        qc, kc, vc, ic, fc = xs
        b = jnp.cumsum(fc, axis=1).transpose(0, 2, 1)
        ic = ic.transpose(0, 2, 1)
        Dm = jnp.where(tri, b[..., :, None] - b[..., None, :] + ic[..., None, :], -jnp.inf)
        inter = b + m[..., None]
        m_loc = jnp.maximum(inter, Dm.max(-1))
        Dexp = jnp.exp(Dm - m_loc[..., None])
        inter_w = jnp.exp(inter - m_loc)
        s = jnp.einsum('blhd,bshd->bhls', qc, kc) * Dexp
        num = inter_w[..., None] * jnp.einsum('blhd,bhde->bhle', qc, C) + jnp.einsum('bhls,bshe->bhle', s, vc)
        nq = inter_w * jnp.einsum('blhd,bhd->bhl', qc, n) + s.sum(-1)
        h = num / jnp.maximum(jnp.abs(nq), jnp.exp(-m_loc))[..., None]
        bL = b[..., -1]
        g = bL[..., None] - b + ic
        m_new = jnp.maximum(bL + m, g.max(-1))
        decay = jnp.exp(bL + m - m_new)
        w = jnp.exp(g - m_new[..., None])
        C = decay[..., None, None] * C + jnp.einsum('bhs,bshd,bshe->bhde', w, kc, vc)
        n = decay[..., None] * n + jnp.einsum('bhs,bshd->bhd', w, kc)
        return (C, n, m_new), h.transpose(0, 2, 1, 3)

    init = (jnp.zeros((B, H, hd, hd), jnp.float32), jnp.zeros((B, H, hd), jnp.float32),
            jnp.zeros((B, H), jnp.float32))
    _, hs = lax.scan(step, init, (chunks(q), chunks(k), chunks(v), chunks(i_pre), chunks(log_f)))
    return jnp.moveaxis(hs, 0, 1).reshape(B, S, H, hd)

def causal_conv(x, w, b):
    out = lax.conv_general_dilated(x, w[:, None, :].astype(x.dtype), window_strides=(1,),
                                   padding=[(CONV_K - 1, 0)], dimension_numbers=('NWC', 'WIO', 'NWC'),
                                   feature_group_count=x.shape[-1])
    return out + b

def token_mixer(x, rel_bias, w_in, w_gate, b_gate, conv_w, conv_b, w_qk_m, w_v_m, w_if, b_if,
                m_norm_g, w_br_a, w_br_m, w_o):
    B, S, _ = x.shape
    proj = x @ w_in
    q_a, k_a, v_a, x_m, z_m = jnp.split(proj, [D_A, 2 * D_A, 3 * D_A, 3 * D_A + D_M], axis=-1)

    ha = lambda t: t.reshape(B, S, N_HEADS_A, HEAD_DIM_A)
    y_a = dilated_attention(ha(q_a), ha(k_a), ha(v_a), rel_bias).reshape(B, S, D_A).astype(x.dtype)

    hm = lambda t: t.reshape(B, S, N_HEADS_M, HEAD_DIM_M)
    x_c = jax.nn.silu(causal_conv(x_m, conv_w, conv_b))
    q_m = jnp.einsum('bshd,hde->bshe', hm(x_c), w_qk_m[0])
    k_m = jnp.einsum('bshd,hde->bshe', hm(x_c), w_qk_m[1])
    v_m = jnp.einsum('bshd,hde->bshe', hm(x_m), w_v_m)
    qkv = jnp.concatenate([q_m.reshape(B, S, D_M), k_m.reshape(B, S, D_M), v_m.reshape(B, S, D_M)], axis=-1)
    gates = (qkv @ w_if + b_if).astype(jnp.float32)
    i_pre, f_pre = jnp.split(gates, 2, axis=-1)
    f32 = lambda t: t.astype(jnp.float32)
    h = mlstm_chunkwise(f32(q_m), f32(k_m), f32(v_m), i_pre, jax.nn.log_sigmoid(f_pre))
    mu = h.mean(-1, keepdims=True)
    var = jnp.square(h - mu).mean(-1, keepdims=True)
    h = ((h - mu) * lax.rsqrt(var + LN_EPS)).reshape(B, S, D_M) * m_norm_g.astype(jnp.float32)
    y_m = (jax.nn.sigmoid(f32(z_m)) * h).astype(x.dtype)

    g_a, g_m = jnp.split(jax.nn.sigmoid(x @ w_gate + b_gate), 2, axis=-1)
    merged = g_a * (y_a @ w_br_a) + g_m * (y_m @ w_br_m)
    return merged @ w_o

def swiglu(x, w13, w2):
    a, g = jnp.split(x @ w13, 2, axis=-1)
    return (jax.nn.silu(a) * g) @ w2

def moe_ffn(x, router_w, router_b, w13, w2):
    logits = (x @ router_w).astype(jnp.float32) + router_b.astype(jnp.float32)
    top_v, top_i = lax.top_k(logits, TOP_K)
    wts = jax.nn.softmax(top_v, axis=-1)
    gate = jnp.einsum('bsk,bske->bse', wts, jax.nn.one_hot(top_i, N_EXPERTS, dtype=jnp.float32)).astype(x.dtype)
    y = jnp.zeros_like(x)
    for e in range(N_EXPERTS):
        y = y + gate[..., e:e + 1] * swiglu(x, w13[e], w2[e])
    return y

def first_inputs(seed: int = 0) -> dict:
    key = jax.random.key(seed)
    ks = jax.random.split(key, 24)
    nrm = lambda k, shape, scale: jax.random.normal(k, shape, jnp.float32) * scale
    b_if = jnp.concatenate([nrm(ks[10], (DEPTH, N_HEADS_M), 0.1),
                            3.0 + 3.0 * jax.random.uniform(ks[11], (DEPTH, N_HEADS_M), jnp.float32)], axis=-1)
    return {
        "x": nrm(ks[0], (BATCH, SEQ, D_MODEL), 1.0),
        "rel_bias": nrm(ks[1], (NUM_BUCKETS, N_HEADS_A), 0.2),
        "w_in": nrm(ks[2], (DEPTH, D_MODEL, P_IN), D_MODEL ** -0.5),
        "w_gate": nrm(ks[3], (DEPTH, D_MODEL, 2 * D_MODEL), D_MODEL ** -0.5),
        "b_gate": nrm(ks[4], (DEPTH, 2 * D_MODEL), 0.02),
        "conv_w": nrm(ks[5], (DEPTH, CONV_K, D_M), CONV_K ** -0.5),
        "conv_b": nrm(ks[6], (DEPTH, D_M), 0.02),
        "w_qk_m": nrm(ks[7], (DEPTH, 2, N_HEADS_M, HEAD_DIM_M, HEAD_DIM_M), HEAD_DIM_M ** -0.5),
        "w_v_m": nrm(ks[8], (DEPTH, N_HEADS_M, HEAD_DIM_M, HEAD_DIM_M), HEAD_DIM_M ** -0.5),
        "w_if": nrm(ks[9], (DEPTH, 3 * D_M, 2 * N_HEADS_M), (3 * D_M) ** -0.5),
        "b_if": b_if,
        "m_norm_g": 1.0 + nrm(ks[12], (DEPTH, D_M), 0.02),
        "w_br_a": nrm(ks[13], (DEPTH, D_A, D_MODEL), D_A ** -0.5),
        "w_br_m": nrm(ks[14], (DEPTH, D_M, D_MODEL), D_M ** -0.5),
        "w_o": nrm(ks[15], (DEPTH, D_MODEL, D_MODEL), BETA * D_MODEL ** -0.5),
        "ln_g": 1.0 + nrm(ks[16], (DEPTH, 2, D_MODEL), 0.02),
        "ln_b": nrm(ks[17], (DEPTH, 2, D_MODEL), 0.02),
        "ffn_w13": nrm(ks[18], (N_DENSE, D_MODEL, 2 * D_FF), D_MODEL ** -0.5),
        "ffn_w2": nrm(ks[19], (N_DENSE, D_FF, D_MODEL), BETA * D_FF ** -0.5),
        "router_w": nrm(ks[20], (N_MOE, D_MODEL, N_EXPERTS), D_MODEL ** -0.5),
        "router_b": nrm(ks[21], (N_MOE, N_EXPERTS), 0.01),
        "exp_w13": nrm(ks[22], (N_MOE, N_EXPERTS, D_MODEL, 2 * D_FF_E), D_MODEL ** -0.5),
        "exp_w2": nrm(ks[23], (N_MOE, N_EXPERTS, D_FF_E, D_MODEL), BETA * D_FF_E ** -0.5),
    }

def first_block(x, rel_bias, w_in, w_gate, b_gate, conv_w, conv_b, w_qk_m, w_v_m, w_if, b_if, m_norm_g,
              w_br_a, w_br_m, w_o, ln_g, ln_b, ffn_w13, ffn_w2, router_w, router_b, exp_w13, exp_w2):
    for l in range(DEPTH):
        y = token_mixer(x, rel_bias, w_in[l], w_gate[l], b_gate[l], conv_w[l], conv_b[l], w_qk_m[l],
                        w_v_m[l], w_if[l], b_if[l], m_norm_g[l], w_br_a[l], w_br_m[l], w_o[l])
        x = layer_norm(ALPHA * x + y, ln_g[l, 0], ln_b[l, 0])
        j = l // 2
        if l % 2 == 0:
            y = swiglu(x, ffn_w13[j], ffn_w2[j])
        else:
            y = moe_ffn(x, router_w[j], router_b[j], exp_w13[j], exp_w2[j])
        x = layer_norm(ALPHA * x + y, ln_g[l, 1], ln_b[l, 1])
    return x


CONV_CH = D_MODEL // 4
CONV_WIDTH = 31
MOBA_HEADS = 4
MOBA_HEAD_DIM = D_MODEL // 16
MOBA_WIDTH = MOBA_HEADS * MOBA_HEAD_DIM
MOBA_BLOCK = 256
MOBA_TOPK = 3
MOBA_Q_CHUNK = 64
GLA_HEADS = 4
GLA_WIDTH = D_MODEL // 2
GLA_DV = GLA_WIDTH // GLA_HEADS
GLA_DK = GLA_DV // 2
GLA_GATE_RANK = 16
GLA_TAU = 16.0
GLA_CHUNK = 32
MIX_WIDTH = CONV_CH + MOBA_WIDTH + GLA_WIDTH
FFN_CONV_WIDTH = 3
NORM_EPS = 1e-6
NEG_INF = -1e30

COL_A = 2 * CONV_CH
COL_B = 3 * MOBA_WIDTH
COL_C_Q = GLA_HEADS * GLA_DK
COL_C_K = GLA_HEADS * GLA_DK
COL_C_V = GLA_WIDTH
COL_C_G = GLA_GATE_RANK
COL_C_R = GLA_WIDTH
COL_C = COL_C_Q + COL_C_K + COL_C_V + COL_C_G + COL_C_R
IN_COLS = COL_A + COL_B + COL_C


def rms_norm(x, g, eps=NORM_EPS):
    xf = x.astype(jnp.float32)
    y = xf * lax.rsqrt(jnp.mean(xf * xf, axis=-1, keepdims=True) + eps)
    return (y * g.astype(jnp.float32)).astype(x.dtype)

def head_rms_norm(x, g, n_heads):
    B, S, W = x.shape
    xf = x.astype(jnp.float32).reshape(B, S, n_heads, W // n_heads)
    y = xf * lax.rsqrt(jnp.mean(xf * xf, axis=-1, keepdims=True) + NORM_EPS)
    return (y.reshape(B, S, W) * g.astype(jnp.float32)).astype(x.dtype)

def layer_norm_2(x, g, b, eps=1e-5):
    xf = x.astype(jnp.float32)
    mu = jnp.mean(xf, axis=-1, keepdims=True)
    var = jnp.mean(jnp.square(xf - mu), axis=-1, keepdims=True)
    y = (xf - mu) * lax.rsqrt(var + eps)
    return (y * g.astype(jnp.float32) + b.astype(jnp.float32)).astype(x.dtype)

def causal_depthwise_conv(x, w, b):
    W = w.shape[0]
    y = lax.conv_general_dilated(
        x, w[:, None, :].astype(x.dtype), window_strides=(1,), padding=[(W - 1, 0)],
        dimension_numbers=("NWC", "WIO", "NWC"), feature_group_count=x.shape[-1])
    return y + b.astype(x.dtype)

def conformer_conv(a_val, a_gate, conv_w, conv_b, ln_g, ln_b):
    h = a_val * jax.nn.sigmoid(a_gate)
    h = causal_depthwise_conv(h, conv_w, conv_b)
    h = layer_norm_2(h, ln_g, ln_b)
    return jax.nn.silu(h)

def moba_attention(q, k, v):
    B, S, H, dh = q.shape
    s_pad = ((S + MOBA_BLOCK - 1) // MOBA_BLOCK) * MOBA_BLOCK
    pad = [(0, 0), (0, s_pad - S), (0, 0), (0, 0)]
    qp = jnp.pad(q, pad).transpose(0, 2, 1, 3)
    kp = jnp.pad(k, pad).transpose(0, 2, 1, 3)
    vp = jnp.pad(v, pad).transpose(0, 2, 1, 3)
    nb = s_pad // MOBA_BLOCK
    topk = min(MOBA_TOPK, nb)
    kb = kp.reshape(B, H, nb, MOBA_BLOCK, dh)
    vb = vp.reshape(B, H, nb, MOBA_BLOCK, dh)
    k_mean = jnp.mean(kb.astype(jnp.float32), axis=3)
    nq = s_pad // MOBA_Q_CHUNK
    q_chunks = qp.reshape(B, H, nq, MOBA_Q_CHUNK, dh).transpose(2, 0, 1, 3, 4)
    scale = 1.0 / math.sqrt(dh)
    chunks_per_block = MOBA_BLOCK // MOBA_Q_CHUNK
    gather_blocks = jax.vmap(jax.vmap(lambda t, i: t[i]))

    def one_chunk(args):
        c, qc = args
        own = c // chunks_per_block
        q_pos = c * MOBA_Q_CHUNK + jnp.arange(MOBA_Q_CHUNK)
        gate = jnp.einsum("bhqd,bhnd->bhqn", qc.astype(jnp.float32), k_mean)
        gate = jnp.where(jnp.arange(nb) < own, gate, NEG_INF)
        _, idx = lax.top_k(gate, topk)
        valid = idx < own
        ks = gather_blocks(kb, idx)
        vs = gather_blocks(vb, idx)
        l_sel = jnp.einsum("bhqd,bhqtkd->bhqtk", qc, ks).astype(jnp.float32) * scale
        l_sel = jnp.where(valid[..., None], l_sel, NEG_INF).reshape(B, H, MOBA_Q_CHUNK, topk * MOBA_BLOCK)
        k_own = lax.dynamic_index_in_dim(kb, own, axis=2, keepdims=False)
        v_own = lax.dynamic_index_in_dim(vb, own, axis=2, keepdims=False)
        k_pos = own * MOBA_BLOCK + jnp.arange(MOBA_BLOCK)
        l_own = jnp.einsum("bhqd,bhkd->bhqk", qc, k_own).astype(jnp.float32) * scale
        l_own = jnp.where(k_pos[None, :] <= q_pos[:, None], l_own, NEG_INF)
        p = jax.nn.softmax(jnp.concatenate([l_sel, l_own], axis=-1), axis=-1)
        p_sel = p[..., : topk * MOBA_BLOCK].reshape(B, H, MOBA_Q_CHUNK, topk, MOBA_BLOCK).astype(vs.dtype)
        p_own = p[..., topk * MOBA_BLOCK:].astype(v_own.dtype)
        return (jnp.einsum("bhqtk,bhqtkd->bhqd", p_sel, vs)
                + jnp.einsum("bhqk,bhkd->bhqd", p_own, v_own))

    out = lax.map(one_chunk, (jnp.arange(nq), q_chunks))
    out = out.transpose(1, 0, 3, 2, 4).reshape(B, s_pad, H, dh)
    return out[:, :S].astype(q.dtype)

def gla_chunked(q, k, v, log_a):
    B, S, H, DK = q.shape
    DV = v.shape[-1]
    C = GLA_CHUNK
    nc = S // C

    def to_chunks(t):
        return t.astype(jnp.float32).reshape(B, nc, C, H, t.shape[-1]).transpose(0, 3, 1, 2, 4)

    qc, kc, vc, gc = to_chunks(q), to_chunks(k), to_chunks(v), to_chunks(log_a)
    G = jnp.cumsum(gc, axis=3)
    gamma = G[:, :, :, -1:, :]
    qg = qc * jnp.exp(G)
    kg = kc * jnp.exp(-G)
    kd = kc * jnp.exp(gamma - G)
    tril = jnp.tril(jnp.ones((C, C), dtype=bool))
    attn = jnp.where(tril, jnp.einsum("bhnid,bhnjd->bhnij", qg, kg), 0.0)
    o_intra = jnp.einsum("bhnij,bhnje->bhnie", attn, vc)
    d_state = jnp.einsum("bhnjd,bhnje->bhnde", kd, vc)
    decay = jnp.exp(gamma[:, :, :, 0, :])

    def step(state, inp):
        d, ds = inp
        return d[..., None] * state + ds, state

    _, s_prev = lax.scan(step, jnp.zeros((B, H, DK, DV), jnp.float32),
                         (jnp.moveaxis(decay, 2, 0), jnp.moveaxis(d_state, 2, 0)))
    s_prev = jnp.moveaxis(s_prev, 0, 2)
    o = o_intra + jnp.einsum("bhnid,bhnde->bhnie", qg, s_prev)
    return o.transpose(0, 2, 3, 1, 4).reshape(B, S, H, DV).astype(v.dtype)

def second_inputs(seed: int = 0) -> dict:
    key = jax.random.key(seed)
    ks = jax.random.split(key, 20)
    f32 = jnp.float32
    n = lambda k, shape, s: jax.random.normal(k, shape, f32) * s
    return {
        "x": n(ks[0], (BATCH, SEQ, D_MODEL), 1.0),
        "norm_mix_g": 1.0 + n(ks[1], (DEPTH, D_MODEL), 0.05),
        "w_in": n(ks[2], (DEPTH, D_MODEL, IN_COLS), D_MODEL ** -0.5),
        "conv_w": n(ks[3], (DEPTH, CONV_WIDTH, CONV_CH), CONV_WIDTH ** -0.5),
        "conv_b": n(ks[4], (DEPTH, CONV_CH), 0.02),
        "conv_ln_g": 1.0 + n(ks[5], (DEPTH, CONV_CH), 0.05),
        "conv_ln_b": n(ks[6], (DEPTH, CONV_CH), 0.02),
        "moba_out_g": 1.0 + n(ks[7], (DEPTH, MOBA_WIDTH), 0.05),
        "gla_gate_w": n(ks[8], (DEPTH, GLA_GATE_RANK, GLA_HEADS * GLA_DK), GLA_GATE_RANK ** -0.5),
        "gla_gate_b": n(ks[9], (DEPTH, GLA_HEADS * GLA_DK), 0.1),
        "gla_out_g": 1.0 + n(ks[10], (DEPTH, GLA_WIDTH), 0.05),
        "w_out": n(ks[11], (DEPTH, MIX_WIDTH, D_MODEL), MIX_WIDTH ** -0.5),
        "norm_ffn_g": 1.0 + n(ks[12], (DEPTH, D_MODEL), 0.05),
        "ffn_w_up": n(ks[13], (DEPTH, D_MODEL, 2 * D_FF), D_MODEL ** -0.5),
        "ffn_conv_w": n(ks[14], (DEPTH, FFN_CONV_WIDTH, 2 * D_FF), FFN_CONV_WIDTH ** -0.5),
        "ffn_conv_b": n(ks[15], (DEPTH, 2 * D_FF), 0.02),
        "ffn_w_down": n(ks[16], (DEPTH, D_FF, D_MODEL), D_FF ** -0.5),
        "final_g": 1.0 + n(ks[17], (D_MODEL,), 0.05),
    }

def second_block(x, norm_mix_g, w_in, conv_w, conv_b, conv_ln_g, conv_ln_b, moba_out_g,
              gla_gate_w, gla_gate_b, gla_out_g, w_out, norm_ffn_g, ffn_w_up, ffn_conv_w,
              ffn_conv_b, ffn_w_down, final_g):
    B, S, _ = x.shape
    o1 = COL_A
    o2 = o1 + COL_B
    o3 = o2 + COL_C_Q
    o4 = o3 + COL_C_K
    o5 = o4 + COL_C_V
    o6 = o5 + COL_C_G
    for l in range(DEPTH):
        h = rms_norm(x, norm_mix_g[l])
        p = h @ w_in[l].astype(h.dtype)
        y_a = conformer_conv(p[..., :CONV_CH], p[..., CONV_CH:o1],
                             conv_w[l], conv_b[l], conv_ln_g[l], conv_ln_b[l])
        qkv = p[..., o1:o2].reshape(B, S, 3, MOBA_HEADS, MOBA_HEAD_DIM)
        y_b = moba_attention(qkv[:, :, 0], qkv[:, :, 1], qkv[:, :, 2]).reshape(B, S, MOBA_WIDTH)
        y_b = head_rms_norm(y_b, moba_out_g[l], MOBA_HEADS)
        q_c = p[..., o2:o3].reshape(B, S, GLA_HEADS, GLA_DK) * (GLA_DK ** -0.5)
        k_c = p[..., o3:o4].reshape(B, S, GLA_HEADS, GLA_DK)
        v_c = p[..., o4:o5].reshape(B, S, GLA_HEADS, GLA_DV)
        gate_logit = (p[..., o5:o6] @ gla_gate_w[l].astype(p.dtype)).astype(jnp.float32) \
            + gla_gate_b[l].astype(jnp.float32)
        log_a = (jax.nn.log_sigmoid(gate_logit) / GLA_TAU).reshape(B, S, GLA_HEADS, GLA_DK)
        y_c = gla_chunked(q_c, k_c, v_c, log_a).reshape(B, S, GLA_WIDTH)
        y_c = head_rms_norm(y_c, gla_out_g[l], GLA_HEADS) * jax.nn.silu(p[..., o6:])
        y = jnp.concatenate([y_a, y_b, y_c], axis=-1) @ w_out[l].astype(x.dtype)
        x = x + y
        h = rms_norm(x, norm_ffn_g[l])
        u = causal_depthwise_conv(h @ ffn_w_up[l].astype(h.dtype), ffn_conv_w[l], ffn_conv_b[l])
        x = x + (jax.nn.silu(u[..., :D_FF]) * u[..., D_FF:]) @ ffn_w_down[l].astype(x.dtype)
    return rms_norm(x, final_g)


def setup_inputs(seed=0):
    out = dict(first_inputs(seed))
    for name, value in second_inputs(seed + 1).items():
        if name != "x":
            out[name + "_2"] = value
    return out


def reference(
    x, rel_bias, w_in, w_gate, b_gate, conv_w, conv_b, w_qk_m, w_v_m, w_if, b_if, m_norm_g,
    w_br_a, w_br_m, w_o, ln_g, ln_b, ffn_w13, ffn_w2, router_w, router_b, exp_w13, exp_w2,
    norm_mix_g_2, w_in_2, conv_w_2, conv_b_2, conv_ln_g_2, conv_ln_b_2, moba_out_g_2,
    gla_gate_w_2, gla_gate_b_2, gla_out_g_2, w_out_2, norm_ffn_g_2, ffn_w_up_2, ffn_conv_w_2,
    ffn_conv_b_2, ffn_w_down_2, final_g_2,
):
    x = first_block(
        x, rel_bias, w_in, w_gate, b_gate, conv_w, conv_b, w_qk_m, w_v_m, w_if, b_if, m_norm_g,
        w_br_a, w_br_m, w_o, ln_g, ln_b, ffn_w13, ffn_w2, router_w, router_b, exp_w13, exp_w2,
    )
    return second_block(
        x, norm_mix_g_2, w_in_2, conv_w_2, conv_b_2, conv_ln_g_2, conv_ln_b_2, moba_out_g_2,
        gla_gate_w_2, gla_gate_b_2, gla_out_g_2, w_out_2, norm_ffn_g_2, ffn_w_up_2,
        ffn_conv_w_2, ffn_conv_b_2, ffn_w_down_2, final_g_2,
    )


_drawn_inputs = setup_inputs


def setup_inputs(seed=0):
    import zlib

    import numpy as np

    out = dict(_drawn_inputs(seed))
    spreads = {}
    factors = {'b_gate': 8.0,
     'conv_b': 2.947,
     'm_norm_g': 6.485,
     'router_b': 7.921,
     'conv_b_2': 2.705,
     'conv_ln_b_2': 6.216,
     'gla_gate_b_2': 2.734,
     'ffn_conv_b_2': 3.057}
    for name, (base, spread) in spreads.items():
        noise = np.random.default_rng([zlib.crc32(name.encode()), seed]).standard_normal(out[name].shape)
        drawn = base * np.exp(spread * noise) if base else spread * noise
        out[name] = __import__('jax').numpy.asarray(drawn.astype(out[name].dtype))
    for name, factor in factors.items():
        out[name] = (out[name] * factor).astype(out[name].dtype)
    return out
```

```python
from contextlib import ExitStack

import numpy as np

import concourse.bass as bass
from concourse import mybir

ALU = mybir.AluOpType
ACT = mybir.ActivationFunctionType
F32 = mybir.dt.float32
F32R = mybir.dt.float32r
BF16 = mybir.dt.bfloat16
I32 = mybir.dt.int32
AX_X = mybir.AxisListType.X

P = 128
TT = 2
S = TT * P
D = 1024
KC = D // P
HALF = 512
NEG = -1e30
ALPHA = 4.0 ** 0.25
LN_EPS = 1e-5
RMS_EPS = 1e-6

HA, HDA = 8, 64
DA = HA * HDA
HM, HDM = 4, 128
DM = HM * HDM
CONV_K = 4
BUCKETS = 32
D_FF = 2816
E_N, D_FF_E = 8, 3584
CW = 31
HB, HDB = 4, 64
GH, GDK, GDV = 4, 64, 128
GCH = 32
NCH = S // GCH
TAU = 16.0

RAW = 6
SPL = 3
AHEAD = 2
UW = KC * 256
STEP = 3
FFC = 256

MIX1_UNITS = 27
DENSE_STEPS = D_FF // FFC
MOE_STEPS = D_FF_E // FFC
LAYER1_UNITS = MIX1_UNITS + STEP * DENSE_STEPS
EXPERT_UNITS = STEP * MOE_STEPS
MIX2_UNITS = 15
LAYER2_UNITS = MIX2_UNITS + STEP * DENSE_STEPS
MOE_UNIT0 = LAYER1_UNITS + MIX1_UNITS
BLOCK2_UNIT0 = 2 * MIX1_UNITS + STEP * DENSE_STEPS + E_N * EXPERT_UNITS
assert LAYER1_UNITS % RAW == 0 and LAYER2_UNITS % RAW == 0 and EXPERT_UNITS % RAW == 0

MERGE_UNITS = (("a", 0), ("m", 0), ("ga", 0), ("gm", 0), ("ga", 1), ("gm", 1), ("ga", 2), ("gm", 2), ("a", 1), ("m", 1),
               ("ga", 3), ("gm", 3))
WO_UNITS = ((0, 256), (256, 256), (512, 256), (768, 128), (896, 128))
assert 10 + len(MERGE_UNITS) + len(WO_UNITS) == MIX1_UNITS
IN2_COLS = (0, 256, 512, 768, 1024, 1280, 1536, 1792, 2048, 2320, 2576)
GATE_COL = 2304

CONST = {"ident": P, "ones": P}
CONST1 = {"upto": P, "before": P, "tri": P, "iota": P, "wincount": S, "lower": E_N * E_N}
CONST2 = {"glamask": P, "reset": S, "causal": S}
CONST_INIT = {"winmask": S}
GROUPS = (CONST, CONST1, CONST2, CONST_INIT)
BUCKET_W = 384


def constants():
    parts = {}

    def put(name, value):
        parts[name] = np.ascontiguousarray(np.broadcast_to(value, (P, np.shape(value)[-1] if np.ndim(value) else P)),
                                           dtype=np.float32)

    p = np.arange(P)[:, None]
    j = np.arange(P)[None, :]
    dist = p + P - np.arange(S)[None, :]
    count = (((dist >= 0) & (dist <= 128)).astype(np.float32) + ((dist >= 0) & (dist % 4 == 0))
             + ((dist >= 0) & (dist % 16 == 0)))
    put("ident", p == j)
    put("ones", 1.0)
    put("upto", p <= j)
    put("before", p < j)
    put("tri", np.where(j <= p, 0.0, NEG))
    put("winmask", np.where(count > 0, 0.0, NEG))
    put("wincount", count)
    put("causal", np.where(dist >= 0, 0.0, NEG))
    put("glamask", (p // GCH == j // GCH) & (p <= j))
    put("reset", np.broadcast_to((np.arange(S) % GCH != 0), (P, S)))
    put("iota", np.broadcast_to(j, (P, P)))
    e = np.arange(E_N)
    put("lower", np.broadcast_to((e[None, :] < e[:, None]).reshape(1, -1), (P, E_N * E_N)))
    u = np.maximum(S - 1 - np.arange(BUCKET_W), 0)
    exact = BUCKETS // 2
    log_b = exact + (np.log(np.maximum(u, exact).astype(np.float32) / exact) / np.log(2048 / exact)
                     * (BUCKETS - exact)).astype(np.int32)
    bucket = np.where(u < exact, u, np.minimum(log_b, BUCKETS - 1))
    onehot = (np.arange(BUCKETS)[:, None] == bucket[None, :]).astype(np.float32)
    packed = [np.concatenate([parts[n] for n in g], axis=1) for g in GROUPS]
    assert all(a.shape[1] == sum(g.values()) for a, g in zip(packed, GROUPS))
    return packed, onehot


class Count:

    def __init__(self, const, terms=()):
        self.const, self.terms = const, tuple(terms)

    def __add__(self, n):
        if isinstance(n, Count):
            return Count(self.const + n.const, self.terms + n.terms)
        return Count(self.const + n, self.terms)

    def loop(self, register, step):
        return Count(self.const, self.terms + ((register, step),))

    def value(self, scale=1, plus=0):
        out = self.const * scale + plus
        for register, k in self.terms:
            out = register * (k * scale) + out
        return out

    def turns(self, ring):
        assert all(k % ring == 0 for _, k in self.terms)
        return Count(self.const // ring, [(r, k // ring) for r, k in self.terms])


class Signals(dict):

    def __init__(self, nc, ctx):
        super().__init__()
        self.nc, self.ctx = nc, ctx

    def __getattr__(self, name):
        if name not in self:
            self[name] = self.ctx.enter_context(self.nc.semaphore(name))
        return self[name]


def spread(ap, axis, n):
    ap = ap.unsqueeze(axis)
    shape = list(ap.shape)
    shape[axis] = n
    return ap.to_broadcast(shape)


def build(nc, A, out):
    ctx = ExitStack()
    with ctx:
        def sb(name, shape, dt=F32, scope=None):
            return (scope or ctx).enter_context(nc.sbuf_tensor(name, shape, dt))

        S_ = Signals(nc, ctx)
        bias_rows = nc.dram_tensor("bias_rows", (P * HA * BUCKET_W,), F32, kind="Internal").ap()

        raw = sb("raw", [P, RAW, UW])
        w_hi = sb("w_hi", [P, SPL, UW], F32R)
        w_lo = sb("w_lo", [P, SPL, UW], F32R)
        x = sb("x", [P, TT, D])
        xT_hi = sb("xT_hi", [P, KC, S], F32R)
        xT_lo = sb("xT_lo", [P, KC, S], F32R)
        yA_hi = sb("yA_hi", [P, 4, S], F32R)
        yA_lo = sb("yA_lo", [P, 4, S], F32R)
        with ExitStack() as shared:
            wqk = sb("wqk", [P, 12, HDM], scope=shared)
        yM_hi = sb("yM_hi", [P, 4, S], F32R)
        yM_lo = sb("yM_lo", [P, 4, S], F32R)
        zeros = sb("zeros", [32, HALF], BF16)
        stat = sb("stat", [P, 192])
        norm_gb = sb("norm_gb", [P, 2, D])

        K = {}

        def const_tile(name, group, scope=None):
            t = sb(name, [P, sum(group.values())], scope=scope)
            at = 0
            for n, w in group.items():
                K[n] = t[:, at:at + w]
                at += w
            return t

        cst = const_tile("cst", CONST)
        ident, ones = K["ident"], K["ones"]

        with ExitStack() as b1:
            cst1 = const_tile("cst1", CONST1, b1)
            bias = sb("bias", [P, HA, S], scope=b1)
            with ExitStack() as m1:
                with ExitStack() as s:
                    xmT = sb("xmT", [P, HM, CONV_K - 1 + S], scope=s)
                    xcT = sb("xcT", [P, HM, S], scope=s)
                bg = sb("bg", [P, 2, D], scope=m1)
                sb("bg_pad", [P, HM * (CONV_K - 1)], scope=m1)
                with ExitStack() as s:
                    qT = sb("qT", [P, HM, S], scope=s)
                    kT = sb("kT", [P, HM, S], scope=s)
                    vA = sb("vA", [P, TT, DM], scope=s)
                merged = sb("merged", [P, TT, D], scope=m1)
                vT = sb("vT_place", [P, HM, S], scope=m1)
                zg = sb("zg", [P, TT, DM], scope=m1)
                gain_m = sb("gain_m", [P, DM], scope=m1)
                cols1 = sb("cols1", [P, 20], scope=m1)
                rows1 = sb("rows1", [20, P], scope=m1)
                w_if = sb("w_if", [P, 12, 8], scope=m1)
                b_if = sb("b_if", [P, 8], scope=m1)
                ht = sb("ht", [P, TT, HM, HDM + 1], scope=m1)
                with ExitStack() as s:
                    sc0 = sb("sc0", [P, HA, P], scope=s)
                    sc1 = sb("sc1", [P, HA, S], scope=s)
                    pT1 = sb("pT1", [P, 2, 3, P], scope=s)
                with ExitStack() as s:
                    bvec = sb("bvec", [P, HA, BUCKET_W], scope=s)
                    cst_init = const_tile("cst_init", CONST_INIT, s)
                    onehot_sb = sb("onehot_sb", [BUCKETS, BUCKET_W], scope=s)
                with ExitStack() as s:
                    vme = sb("vme", [P, TT, HM, HDM + 1], scope=s)
                    kw = sb("kw", [P, HM, HDM], scope=s)
                    cn = sb("cn", [P, HM, HDM + 1], scope=s)
                    dm = sb("dm", [P, TT, HM, P], scope=s)
                with ExitStack() as s:
                    ga = sb("ga", [P, TT, FFC], scope=s)
                    gm = sb("gm", [P, TT, FFC], scope=s)
            relb = merged[0:BUCKETS, 0, :].rearrange("p (h m) -> p h m", h=HA)
            relrow = merged[0:BUCKETS, 1, 0:HA]
            with ExitStack() as s:
                sa = sb("sa", [P, 2, HALF], scope=s)
                hf = sb("hf", [P, 2, HALF], scope=s)
                hT_hi = sb("hT_hi", [P, 2, 2, S], F32R, scope=s)
                hT_lo = sb("hT_lo", [P, 2, 2, S], F32R, scope=s)
                gateb = sb("gateb", [P, E_N, S], scope=s)
                rw_raw = sb("rw_raw", [P, KC, E_N], scope=s)
                rw_hi = sb("rw_hi", [P, KC, E_N], F32R, scope=s)
                rw_lo = sb("rw_lo", [P, KC, E_N], F32R, scope=s)
                rb = sb("rb", [P, E_N], scope=s)
                lg = sb("lg", [P, TT, E_N], scope=s)
                cmp2 = sb("cmp2", [P, 2, E_N, E_N], scope=s)
                rt = sb("rt", [P, 6, TT, E_N], scope=s)
        with ExitStack() as b2:
            cst2 = const_tile("cst2", CONST2, b2)
            cols2 = sb("cols2", [P, 250], scope=b2)
            with ExitStack() as s:
                rows2 = sb("rows2", [P, 3, P], scope=s)
            egT = sb("egT", [P, 2, S], scope=b2)
            with ExitStack() as s:
                xn = sb("xn", [P, TT, D], scope=s)
            st8 = sb("st8", [P, NCH, 2, GDV], scope=b2)
            with ExitStack() as m2:
                avT = sb("avT", [P, 2, CW - 1 + S], scope=m2)
                agT = sb("agT", [P, 2, S], scope=m2)
                cvT = sb("cvT", [P, 2, S], scope=m2)
                qcT = sb("qcT", [P, 2, S], scope=m2)
                kcT = sb("kcT", [P, 2, S], scope=m2)
                vc = sb("vc", [P, TT, GH * GDV], scope=m2)
                rT = sb("rT", [P, GH, S], scope=m2)
                gT = sb("gT", [16, S], scope=m2)
                wg = sb("wg", [16, 2 * P], scope=m2)
                w16 = sb("w16", [P, KC, 16], scope=m2)
                gain_b = sb("gain_b", [P, HB * HDB], scope=m2)
                laT = sb("laT", [P, 2, S], scope=m2)
                cumT = sb("cumT", [P, 2, S], scope=m2)
                dec = sb("dec", [P, 2, NCH], scope=m2)
                with ExitStack() as s:
                    qbT = sb("qbT", [P, 2, S], scope=s)
                    kbT = sb("kbT", [P, 2, S], scope=s)
                    vb = sb("vb", [P, TT, HB * HDB], scope=s)
                    sb0 = sb("sb0", [P, HB, P], scope=s)
                    sb1 = sb("sb1", [P, HB, S], scope=s)
                    pT2 = sb("pT2", [P, 2, 3, P], scope=s)
                with ExitStack() as s:
                    kd = sb("kd", [P, TT, 2, P], scope=s)
                    atT = sb("atT", [P, GH, TT, P], scope=s)
                    oc = sb("oc", [P, GH, S], scope=s)
                    rv = sb("rv", [P, GH, S], scope=s)
            with ExitStack() as s:
                u_a = sb("u_a", [P, 2, 2, 2 + S], scope=s)
                u_g = sb("u_g", [P, 2, 2, 2 + S], scope=s)
                c_a = sb("c_a", [P, 2, 2, S], scope=s)
                c_g = sb("c_g", [P, 2, S], scope=s)
                h2f = sb("h2f", [P, 2, HALF], scope=s)
                h2_hi = sb("h2_hi", [P, 2, 2, S], F32R, scope=s)
                h2_lo = sb("h2_lo", [P, 2, 2, S], F32R, scope=s)

        ps = ctx.enter_context(nc.psum_tensor("ps", [P, 8, HALF], F32))
        raw_landed = [ctx.enter_context(nc.semaphore(f"raw_landed{i}")) for i in range(RAW)]
        block = ctx.enter_context(nc.Block())
        gcols = sa[:].rearrange("p b (e t n) -> p b e t n", e=2, t=TT)
        yb, qgT, kgT, kdT, sTm = vb, qcT, laT, cumT, dm
        F1 = {"h": hf, "h_ready": S_.h1_ready, "h_hi_ready": S_.h1_hi_ready, "h_lo_ready": S_.h1_lo_ready}
        F2 = {"h": h2f, "h_ready": S_.h2_ready, "h_hi_ready": S_.h2_hi_ready, "h_lo_ready": S_.h2_lo_ready}

        def bank(b, *shape):
            n = int(np.prod(shape))
            v = ps[:, b:b + -(-n // HALF), :].rearrange("p b n -> p (b n)")[:, 0:n]
            if len(shape) == 2:
                v = v.rearrange("p (a b) -> p a b", a=shape[0])
            if len(shape) == 3:
                v = v.rearrange("p (a b c) -> p a b c", a=shape[0], b=shape[1])
            return v

        @block.sync
        def _(sp):
            def load(u, src, width):
                slot = u.const % RAW
                sp.wait_ge(S_.lo_ready, u.value(plus=1))
                dst = raw[:, slot, 0:width].rearrange("p (k n) -> p k n", k=src.shape[1])
                sp.dma_start(dst, src).then_inc(raw_landed[slot], 16)

            def columns(w, c0, n):
                return w.rearrange("(k p) n -> p k n", p=P)[:, :, c0:c0 + n]

            def feed_forward(u, w13, w2, steps):
                hidden = steps * FFC

                def val(j):
                    return w13[:, 0:hidden].rearrange("(k p) (j n) -> p k j n", p=P, n=FFC)[:, :, j, :]

                def gat(j):
                    return w13[:, hidden:2 * hidden].rearrange("(k p) (j n) -> p k j n", p=P, n=FFC)[:, :, j, :]

                def down(j):
                    return w2.rearrange("(j c p) n -> p j c n", p=P, c=2)[:, j, :, :]

                load(u, val(0), UW)
                load(u + 1, gat(0), UW)
                pairs = (steps - 1) // 2
                with sp.Fori(0, pairs) as i:
                    for q in range(2):
                        at = (u + (2 + STEP * q)).loop(i, 2 * STEP)
                        load(at, val(i * 2 + (1 + q)), UW)
                        load(at + 1, gat(i * 2 + (1 + q)), UW)
                        load(at + 2, down(i * 2 + q), UW)
                for j in range(2 * pairs + 1, steps):
                    at = u + (2 + STEP * (j - 1))
                    load(at, val(j), UW)
                    load(at + 1, gat(j), UW)
                    load(at + 2, down(j - 1), UW)
                load(u + (STEP * steps - 1), down(steps - 1), UW)

            sp.dma_start(cst[:], A["const0"]).then_inc(S_.start_loaded, 16)
            sp.dma_start(cst1[:], A["const1"]).then_inc(S_.start_loaded, 16)
            sp.dma_start(cst_init[:], A["const3"]).then_inc(S_.start_loaded, 16)
            sp.dma_start(onehot_sb[:], A["onehot"]).then_inc(S_.start_loaded, 16)
            sp.dma_start(relrow, A["rel_bias"]).then_inc(S_.start_loaded, 16)
            sp.dma_start(x[:], A["x"][0].rearrange("(t p) d -> p t d", p=P)).then_inc(S_.start_loaded, 16)

            with sp.Fori(0, 2) as L:
                u = Count(0).loop(L, LAYER1_UNITS)
                w_in, w_gate = A["w_in"][L], A["w_gate"][L]
                for n in range(10):
                    load(u + n, columns(w_in, 256 * n, 256), UW)
                br = {"a": A["w_br_a"][L], "m": A["w_br_m"][L]}
                for m, (kind, c) in enumerate(MERGE_UNITS):
                    if kind in br:
                        load(u + (10 + m), columns(br[kind], HALF * c, HALF), UW)
                    else:
                        load(u + (10 + m), columns(w_gate, D * (kind == "gm") + 256 * c, 256), UW)
                for n, (c0, w) in enumerate(WO_UNITS):
                    load(u + (22 + n), columns(A["w_o"][L], c0, w), KC * w)
                with sp.If(L == 0):
                    feed_forward(Count(MIX1_UNITS), A["ffn_w13"][0], A["ffn_w2"][0], DENSE_STEPS)
                with sp.Else():
                    with sp.Fori(0, E_N) as e:
                        feed_forward(Count(MOE_UNIT0).loop(e, EXPERT_UNITS), A["exp_w13"][0][e], A["exp_w2"][0][e],
                                     MOE_STEPS)
            with sp.Fori(0, 2) as L:
                u = Count(BLOCK2_UNIT0).loop(L, LAYER2_UNITS)
                w_in = A["w_in_2"][L]
                for n, c0 in enumerate(IN2_COLS):
                    load(u + n, columns(w_in, c0, 256), UW)
                for n in range(4):
                    load(u + (11 + n), columns(A["w_out_2"][L], 256 * n, 256), UW)
                feed_forward(u + MIX2_UNITS, A["ffn_w_up_2"][L], A["ffn_w_down_2"][L], DENSE_STEPS)
            sp.wait_ge(S_.result_ready, 1)
            sp.dma_start(out[0].rearrange("(t p) d -> p t d", p=P), xn[:]).then_inc(S_.result_stored, 16)
            sp.wait_ge(S_.result_stored, 16)

        @block.gpsimd
        def _(pool):
            def over(v, n):
                return v.partition_broadcast(P)

            pool.wait_ge(S_.bvec_ready, 1)
            pool.dma_start(bias_rows.rearrange("(p n) -> p n", p=P),
                           bvec[:].rearrange("p h n -> p (h n)")).then_inc(S_.bias_stored, 16)
            pool.wait_ge(S_.bias_stored, 16)
            pitch = HA * BUCKET_W - 1
            skew = bias_rows[P - 1:P - 1 + P * pitch].rearrange("(p n) -> p n", n=pitch)
            for h in range(HA):
                pool.dma_start(bias[:, h, :], skew[:, h * BUCKET_W:h * BUCKET_W + S]).then_inc(S_.bias_loaded, 16)

            def norm_params(g, b, before):
                pool.wait_ge(S_.xn_ready, before)
                pool.dma_start(norm_gb[:, 0, :], over(g, D)).then_inc(S_.norm_loaded, 16)
                if b is not None:
                    pool.dma_start(norm_gb[:, 1, :], over(b, D)).then_inc(S_.norm_loaded, 16)

            pool.wait_ge(S_.bias_done, 1)
            with pool.Fori(0, 2) as L:
                pool.wait_ge(S_.xn_ready, L * 2 + 1)
                pool.sem_inc(S_.pool_passed, 1)
                pool.dma_start(rows1[0:16, :], A["conv_w"][L].rearrange("k (c p) -> (k c) p", p=P)).then_inc(S_.p1_loaded, 16)
                pool.dma_start(rows1[16:20, :], A["conv_b"][L].rearrange("(c p) -> c p", p=P)).then_inc(S_.p1_loaded, 16)
                pool.dma_start(wqk[:, 0:8, :], A["w_qk_m"][L].rearrange("a h d e -> d (a h) e")).then_inc(S_.p1_loaded, 16)
                pool.dma_start(wqk[:, 8:12, :], A["w_v_m"][L].rearrange("h d e -> d h e")).then_inc(S_.p1_loaded, 16)
                pool.dma_start(w_if[:], A["w_if"][L].rearrange("(c p) g -> p c g", p=P)).then_inc(S_.p1_loaded, 16)
                pool.dma_start(b_if[:], over(A["b_if"][L], 8)).then_inc(S_.p1_loaded, 16)
                pool.dma_start(gain_m[:], over(A["m_norm_g"][L], DM)).then_inc(S_.p1_loaded, 16)
                pool.dma_start(norm_gb[:, 0, :], over(A["ln_g"][L, 0], D)).then_inc(S_.norm_loaded, 16)
                pool.dma_start(norm_gb[:, 1, :], over(A["ln_b"][L, 0], D)).then_inc(S_.norm_loaded, 16)
                pool.wait_ge(S_.v_m_psum, L + 1)
                pool.sem_inc(S_.pool_passed, 1)
                pool.dma_start(bg[:], over(A["b_gate"][L], 2 * D).rearrange("p (a d) -> p a d", a=2)).then_inc(S_.bg_loaded, 16)
                pool.wait_ge(S_.xn_ready, L * 2 + 2)
                pool.sem_inc(S_.pool_passed, 1)
                pool.dma_start(norm_gb[:, 0, :], over(A["ln_g"][L, 1], D)).then_inc(S_.norm_loaded, 16)
                pool.dma_start(norm_gb[:, 1, :], over(A["ln_b"][L, 1], D)).then_inc(S_.norm_loaded, 16)
                with pool.If(L == 0):
                    pool.nop()
                with pool.Else():
                    pool.dma_start(rw_raw[:], A["router_w"][0].rearrange("(k p) e -> p k e", p=P)).then_inc(S_.router_loaded, 16)
                    pool.dma_start(rb[:], over(A["router_b"][0], E_N)).then_inc(S_.router_loaded, 16)
            pool.wait_ge(S_.xn_ready, 5)
            pool.dma_start(cst2[:], A["const2"]).then_inc(S_.const2_loaded, 16)
            with pool.Fori(0, 2) as L:
                pool.wait_ge(S_.xn_ready, L * 2 + 5)
                pool.sem_inc(S_.pool_passed, 1)
                pool.dma_start(norm_gb[:, 0, :], over(A["norm_mix_g_2"][L], D)).then_inc(S_.norm2_loaded, 16)
                pool.wait_ge(S_.xn_ready, L * 2 + 6)
                pool.sem_inc(S_.pool_passed, 1)
                pool.dma_start(norm_gb[:, 0, :], over(A["norm_ffn_g_2"][L], D)).then_inc(S_.norm2_loaded, 16)
                p2 = lambda dst, src: pool.dma_start(dst, src).then_inc(S_.p2_loaded, 16)
                p2(rows2[0:62, 0, :], A["conv_w_2"][L].rearrange("k (c p) -> (k c) p", p=P))
                p2(rows2[62:64, 0, :], A["conv_b_2"][L].rearrange("(c p) -> c p", p=P))
                p2(rows2[64:66, 0, :], A["conv_ln_g_2"][L].rearrange("(c p) -> c p", p=P))
                p2(rows2[66:68, 0, :], A["conv_ln_b_2"][L].rearrange("(c p) -> c p", p=P))
                p2(rows2[68:70, 0, :], A["gla_gate_b_2"][L].rearrange("(c p) -> c p", p=P))
                p2(rows2[70:74, 0, :], A["gla_out_g_2"][L].rearrange("(c p) -> c p", p=P))
                p2(rows2[0:88, 1, :], A["ffn_conv_w_2"][L, 0:2].rearrange("k (c p) -> (k c) p", p=P))
                p2(rows2[0:44, 2, :], A["ffn_conv_w_2"][L, 2].rearrange("(c p) -> c p", p=P))
                p2(rows2[44:88, 2, :], A["ffn_conv_b_2"][L].rearrange("(c p) -> c p", p=P))
                p2(wg[:], A["gla_gate_w_2"][L])
                p2(gain_b[:], over(A["moba_out_g_2"][L], HB * HDB))
                p2(w16[:], A["w_in_2"][L].rearrange("(k p) n -> p k n", p=P)[:, :, GATE_COL:GATE_COL + 16])
            pool.wait_ge(S_.xn_ready, 9)
            pool.dma_start(norm_gb[:, 0, :], over(A["final_g_2"], D)).then_inc(S_.norm2_loaded, 16)

        @block.tensor
        def _(pe):
            def unit_parts(u, k, n):
                pe.wait_ge(S_.lo_ready, u.value(plus=RAW + 1))
                slot = u.const % SPL
                return [w[:, slot, 0:k * n].rearrange("p (k n) -> p k n", k=k) for w in (w_hi, w_lo)]

            def product(out, lhs, rhs, first, last):
                pe.matmul(out, lhs[0], rhs[0], start=first, stop=False)
                pe.matmul(out, lhs[0], rhs[1], start=False, stop=False)
                return pe.matmul(out, lhs[1], rhs[0], start=False, stop=last)

            def project_T(u, b, lhsT=None):
                w = unit_parts(u, KC, 256)
                o = bank(b, 2, S)
                for c in range(2):
                    for k in range(KC):
                        m = product(o[:, c, :], [v[:, k, c * P:(c + 1) * P] for v in w],
                                    [v[:, k, :] for v in (xT_hi, xT_lo)], k == 0, k == KC - 1)
                m.then_inc(S_.unit_used, 1)

            def project_tok(u, outs, chunks, n):
                w = unit_parts(u, len(chunks), n)
                for t in range(TT):
                    for k, c in enumerate(chunks):
                        m = product(outs[t], [v[:, t * P:(t + 1) * P] for v in c], [v[:, k, :] for v in w],
                                    k == 0, k == len(chunks) - 1)
                m.then_inc(S_.unit_used, 1)

            x_chunks = [(xT_hi[:, k, :], xT_lo[:, k, :]) for k in range(KC)]
            yA_chunks = [(yA_hi[:, k, :], yA_lo[:, k, :]) for k in range(4)]
            yM_chunks = [(yM_hi[:, k, :], yM_lo[:, k, :]) for k in range(4)]

            def transpose_x(src, count):
                for b in range(4):
                    o = bank(4 + b, 2, TT, P)
                    for c in range(2):
                        for t in range(TT):
                            m = pe.transpose(o[:, c, t, :], src[:, t, (2 * b + c) * P:(2 * b + c + 1) * P], ident)
                    m.then_inc(S_.xT_psum, 1)
                pe.wait_ge(S_.xT_lo_ready, count)

            def open_sums():
                for b in range(4):
                    pe.matmul(ps[:, b, :], zeros[:, 0:P], zeros[:], start=True, stop=False)

            def close_sums():
                for b in range(4):
                    m = pe.matmul(ps[:, b, :], zeros[:, 0:P], zeros[:], start=False, stop=True)
                m.then_inc(S_.sums_closed, 1)

            def feed_forward(u, steps, count, hh, hl, sig):
                def up(at, b):
                    project_T(at, b)

                def step_up(j, at, odd, dyn):
                    pe.wait_ge(sig["h_ready"], dyn.value(plus=1))
                    up(at, 4 + 2 * odd)
                    up(at + 1, 5 + 2 * odd)

                def down(at, odd, dyn):
                    pe.wait_ge(sig["h_lo_ready"], dyn.value(plus=1))
                    w = unit_parts(at, 2, D)
                    for c in range(2):
                        for t in range(TT):
                            for h in range(2):
                                m = pe_sum(ps[:, 2 * t + h, :], [v[:, odd, c, t * P:(t + 1) * P] for v in (hh, hl)],
                                           [v[:, c, h * HALF:(h + 1) * HALF] for v in w])
                    m.then_inc(S_.unit_used, 1)

                def pe_sum(o, lhs, rhs):
                    return product(o, lhs, rhs, False, False)

                step_up(0, u, 0, count)
                pairs = (steps - 1) // 2
                with pe.Fori(0, pairs) as i:
                    for q in range(2):
                        at = (u + (2 + STEP * q)).loop(i, 2 * STEP)
                        j = (count + (1 + q)).loop(i, 2)
                        step_up(None, at, (1 + q) % 2, j)
                        down(at + 2, q, j + -1)
                for j in range(2 * pairs + 1, steps):
                    at = u + (2 + STEP * (j - 1))
                    step_up(j, at, j % 2, count + j)
                    down(at + 2, (j - 1) % 2, count + (j - 1))
                down(u + (STEP * steps - 1), (steps - 1) % 2, count + (steps - 1))

            def attention_out(L, heads, sc, pT, v, names):
                s_prob, s_psum, s_ready, s_pv = names
                w = 64

                def blocks(h):
                    o = bank(6 + h % 2, 3, P)
                    if h >= 2:
                        pe.wait_ge(s_ready, L * heads + (h - 1))
                    pe.transpose(o[:, 0, :], sc[0][:, h, :], ident)
                    pe.transpose(o[:, 1, :], sc[1][:, h, 0:P], ident)
                    pe.transpose(o[:, 2, :], sc[1][:, h, P:S], ident).then_inc(s_psum, 1)

                def values(h):
                    pe.wait_ge(s_ready, L * heads + (h + 1))
                    b, cols = pT[:, h % 2], slice(h * w, (h + 1) * w)
                    pe.matmul(ps[:, 4, cols], b[:, 0, :], v[:, 0, cols], start=True, stop=True)
                    pe.matmul(ps[:, 5, cols], b[:, 1, :], v[:, 0, cols], start=True, stop=False)
                    pe.matmul(ps[:, 5, cols], b[:, 2, :], v[:, 1, cols], start=False, stop=True).then_inc(s_pv, 1)

                pe.wait_ge(s_prob, L * 2 + 2)
                for h in range(heads):
                    blocks(h)
                    if h:
                        values(h - 1)
                values(heads - 1)

            def to_T(src, done):
                for b in range(2):
                    o = bank(6 + b, 2, TT, P)
                    for c in range(2):
                        for t in range(TT):
                            m = pe.transpose(o[:, c, t, :], src(t, 2 * b + c), ident)
                    m.then_inc(done, 1)

            def mixer1(L, u):
                pe.wait_ge(S_.xn_ready, L * 2 + 1)
                transpose_x(x, L * 12 + 4)
                pe.wait_ge(S_.p1_loaded, L * 112 + 112)
                pe.sem_inc(S_.pe_passed, 1)
                pe.transpose(ps[:, 7, 0:20], rows1[:], ident[0:20, 0:20]).then_inc(S_.p1_cols_psum, 1)

                def bank_free(n):
                    if n >= 4:
                        pe.wait_ge(S_.proj1_out, L * 10 + (n - 3))

                def scores(tile, h, b, col):
                    rows = slice(64 * (h % 2), 64 * (h % 2) + 64)
                    n = P * (tile + 1)
                    return pe.matmul(ps[:, b, col:col + n], qT[rows, h // 2, tile * P:(tile + 1) * P],
                                     kT[rows, h // 2, 0:n], start=True, stop=True)

                for n in range(4):
                    bank_free(n)
                    project_T(u + n, n % 4)
                for n in (4, 5):
                    bank_free(n)
                    project_tok(u + n, [bank(n % 4, TT, 256)[:, t, :] for t in range(TT)], x_chunks, 256)
                pe.wait_ge(S_.proj1_out, L * 10 + 4)
                pe.wait_ge(S_.p1_cols_ready, L + 1)
                for h in range(HA):
                    m = scores(0, h, 4 + h % 2, (h // 2) * P)
                m.then_inc(S_.scores1, 1)
                for h in range(4):
                    m = scores(1, h, 6 + h % 2, (h // 2) * S)
                m.then_inc(S_.scores1, 1)
                for n in (6, 7):
                    bank_free(n)
                    project_T(u + n, n % 4)
                pe.wait_ge(S_.scores1_in, L * 3 + 1)
                for h in range(4, 8):
                    m = scores(1, h, 4 + h % 2, (h // 2 - 2) * S)
                m.then_inc(S_.scores1, 1)
                for n in (8, 9):
                    bank_free(n)
                    project_tok(u + n, [bank(n % 4, TT, 256)[:, t, :] for t in range(TT)], x_chunks, 256)
                pe.wait_ge(S_.xc_ready, L + 1)
                pe.wait_ge(S_.proj1_out, L * 10 + 10)
                for i in range(2):
                    for h in range(HM):
                        m = pe.matmul(bank(2 * i + h // 2, 2, S)[:, h % 2, :], wqk[:, 4 * i + h, :], xcT[:, h, :],
                                      start=True, stop=True)
                m.then_inc(S_.qk_m_psum, 1)
                attention_out(L, HA, (sc0, sc1), pT1, vA, (S_.prob1, S_.pT1_psum, S_.pT1_ready, S_.pv1))
                pe.wait_ge(S_.ya1_ready, L + 1)
                pe.wait_ge(S_.pT1_ready, L * HA + HA)
                ya = ht[:].rearrange("p t h e -> p (t h e)")[:, 0:TT * DM].rearrange("p (t n) -> p t n", t=TT)
                to_T(lambda t, c: ya[:, t, c * P:(c + 1) * P], S_.yT_psum)
                pe.wait_ge(S_.qk_m_ready, L + 1)
                for h in range(HM):
                    pe.matmul(bank(h // 2, 2, S)[:, h % 2, :], wqk[:, 8 + h, :], xmT[:, h, CONV_K - 1:], start=True, stop=True)
                for t in range(TT):
                    for h in range(HM):
                        at = CONV_K - 1 + t * P
                        pe.matmul(ps[:, 2 + t, h * P:(h + 1) * P], xmT[:, h, at:at + P], wqk[:, 8 + h, :],
                                  start=True, stop=True)
                for h in range(HM):
                    m = pe.matmul(ps[:, 4, h * P:(h + 1) * P], xcT[:, h, 0:P], wqk[:, 4 + h, :], start=True, stop=True)
                m.then_inc(S_.v_m_psum, 1)
                pe.wait_ge(S_.v_m_ready, L + 1)
                for t in range(TT):
                    for c in range(12):
                        src = (qT, kT, vT)[c // 4]
                        m = pe.matmul(ps[:, 5, 8 * t:8 * t + 8], src[:, c % 4, t * P:(t + 1) * P], w_if[:, c, :],
                                      start=c == 0, stop=c == 11)
                m.then_inc(S_.gates_psum, 1)
                for t in range(TT):
                    for h in range(HM):
                        pe.matmul(ps[:, t, h * P:(h + 1) * P], qT[:, h, t * P:(t + 1) * P], kT[:, h, t * P:(t + 1) * P],
                                  start=True, stop=True)
                pe.wait_ge(S_.logf_ready, L + 1)
                for t in range(TT):
                    lf = stat[:, 16 + 4 * t:20 + 4 * t]
                    pe.matmul(ps[:, 5, 32 + 4 * t:36 + 4 * t], K["upto"], lf, start=True, stop=True)
                    m = pe.matmul(ps[:, 5, 40 + 4 * t:44 + 4 * t], ones, lf, start=True, stop=True)
                m.then_inc(S_.cum_psum, 1)
                pe.wait_ge(S_.diag_ready, L + 1)
                dg = ht[:].rearrange("p t h e -> p (t h e)")[:, 0:TT * DM].rearrange("p (t n) -> p t n", t=TT)
                pe.wait_ge(S_.yT_lo_ready, L * 4 + 2)
                for t in range(TT):
                    m = pe.matmul(ps[:, 6 + t, :], ones, dg[:, t, :], start=True, stop=True)
                m.then_inc(S_.rowr_psum, 1)
                pe.wait_ge(S_.s_ready, L + 1)
                for t in range(TT):
                    for h in range(HM):
                        m = pe.transpose(ps[:, 6 + t, h * P:(h + 1) * P], dm[:, t, h, :], ident)
                m.then_inc(S_.sT_psum, 1)
                pe.wait_ge(S_.kw_ready, L + 1)
                E1 = HDM + 1
                for h in range(HM):
                    m = pe.matmul(ps[:, 2 + h // 2, (h % 2) * E1:(h % 2 + 1) * E1], kw[:, h, :], vme[:, 0, h, :],
                                  start=True, stop=True)
                m.then_inc(S_.cn_psum, 1)
                pe.wait_ge(S_.sT_ready, L + 1)
                for t in range(TT):
                    for h in range(HM):
                        pe.matmul(ps[:, 4 * t + h // 2, (h % 2) * E1:(h % 2 + 1) * E1], sTm[:, t, h, :], vme[:, t, h, :],
                                  start=True, stop=True)
                pe.wait_ge(S_.cn_ready, L + 1)
                for h in range(HM):
                    m = pe.matmul(ps[:, 2 + h // 2, (h % 2) * E1:(h % 2 + 1) * E1], qT[:, h, P:S], cn[:, h, :],
                                  start=True, stop=True)
                m.then_inc(S_.num_psum, 1)
                pe.wait_ge(S_.ym_ready, L + 1)
                to_T(lambda t, c: ht[:, t, c, 0:P], S_.yT_psum)
                pe.wait_ge(S_.yT_lo_ready, L * 4 + 4)
                gates = 0
                for m_, (kind, c) in enumerate(MERGE_UNITS):
                    at = u + (10 + m_)
                    if kind in "am":
                        if c:
                            pe.wait_ge(S_.merged_ready, L * 4 + 2)
                        b = 0 if kind == "a" else 2
                        project_tok(at, [ps[:, b, :], ps[:, b + 1, :]], yA_chunks if kind == "a" else yM_chunks, HALF)
                    else:
                        if gates >= 4:
                            pe.wait_ge(S_.gate_lin, L * 8 + (gates - 3))
                        b = 4 + gates % 4
                        project_tok(at, [bank(b, TT, FFC)[:, t, :] for t in range(TT)], x_chunks, FFC)
                        gates += 1
                pe.wait_ge(S_.merged_ready, L * 4 + 4)
                transpose_x(merged, L * 12 + 8)
                for n, (c0, w) in enumerate(WO_UNITS):
                    o = [ps[:, 2 * t + c0 // HALF, c0 % HALF:c0 % HALF + w] for t in range(TT)]
                    project_tok(u + (22 + n), o, x_chunks, w)
                pe.wait_ge(S_.xn_ready, L * 2 + 2)
                transpose_x(x, L * 12 + 12)
                open_sums()

            def router():
                pe.wait_ge(S_.rw_split, 1)
                for t in range(TT):
                    for k in range(KC):
                        m = product(ps[:, 4, 8 * t:8 * t + 8], [v[:, k, t * P:(t + 1) * P] for v in (xT_hi, xT_lo)],
                                    [v[:, k, :] for v in (rw_hi, rw_lo)], k == 0, k == KC - 1)
                m.then_inc(S_.logits_psum, 1)
                for q in range(4):
                    pe.wait_ge(S_.gcols_ready, q + 1)
                    for e in range(2):
                        for t in range(TT):
                            m = pe.matmul(ps[:, 4 + q, e * S + t * P:e * S + (t + 1) * P], gcols[:, q % 2, e, t, :], ident,
                                          start=True, stop=True)
                    m.then_inc(S_.gateb_psum, 1)
                pe.wait_ge(S_.gateb_ready, 4)

            def mixer2(L, u):
                pe.wait_ge(S_.xn_ready, L * 2 + 6)
                transpose_x(xn, L * 8 + 28)
                def bank_free(n):
                    if n >= 4:
                        pe.wait_ge(S_.proj2_out, L * 11 + (n - 3))

                def tok(n):
                    bank_free(n)
                    project_tok(u + n, [bank(n % 4, TT, 256)[:, t, :] for t in range(TT)], x_chunks, 256)

                def T(n):
                    bank_free(n)
                    project_T(u + n, n % 4)

                T(0)
                T(1)
                pe.wait_ge(S_.p2_loaded, L * 192 + 192)
                pe.sem_inc(S_.pe_passed, 1)
                pe.transpose(ps[:, 7, 0:74], rows2[0:74, 0, :], ident[0:74, 0:74])
                pe.transpose(ps[:, 7, 74:162], rows2[0:88, 1, :], ident[0:88, 0:88])
                pe.transpose(ps[:, 7, 162:250], rows2[0:88, 2, :], ident[0:88, 0:88]).then_inc(S_.p2_cols_psum, 1)
                for i, part in enumerate((xT_hi, xT_lo)):
                    for k in range(KC):
                        m = pe.matmul(ps[0:16, 6, 0:S], w16[:, k, :], part[:, k, :].bitcast(F32),
                                      start=i == 0 and k == 0, stop=i == 1 and k == KC - 1)
                m.then_inc(S_.g16_psum, 1)
                T(2)
                T(3)
                tok(4)
                pe.wait_ge(S_.proj2_out, L * 11 + 4)

                def scores(tile, h, b, col):
                    rows = slice(64 * (h % 2), 64 * (h % 2) + 64)
                    n = P * (tile + 1)
                    return pe.matmul(ps[:, b, col:col + n], qbT[rows, h // 2, tile * P:(tile + 1) * P],
                                     kbT[rows, h // 2, 0:n], start=True, stop=True)

                for h in range(HB):
                    m = scores(0, h, 4 + h % 2, (h // 2) * P)
                m.then_inc(S_.scores2, 1)
                pe.wait_ge(S_.g16_ready, L + 1)
                pe.wait_ge(S_.p2_cols_ready, L + 1)
                for h in range(HB):
                    m = scores(1, h, 6 + h % 2, (h // 2) * S)
                m.then_inc(S_.scores2, 1)
                T(5)
                pe.wait_ge(S_.scores2_in, L + 1)
                for c in range(2):
                    m = pe.matmul(ps[:, 7, c * S:(c + 1) * S], wg[:, c * P:(c + 1) * P], gT[:], start=True, stop=True)
                m.then_inc(S_.glog_psum, 1)
                T(6)
                tok(7)
                tok(8)
                T(9)
                T(10)
                pe.wait_ge(S_.glog_in, L + 1)
                attention_out(L, HB, (sb0, sb1), pT2, vb, (S_.prob2, S_.pT2_psum, S_.pT2_ready, S_.pv2))
                pe.wait_ge(S_.yb_ready, L + 1)
                pe.wait_ge(S_.pT2_ready, L * HB + HB)
                o = bank(6, 2, TT, P)
                for c in range(2):
                    for t in range(TT):
                        m = pe.transpose(o[:, c, t, :], yb[:, t, c * P:(c + 1) * P], ident)
                m.then_inc(S_.yb_psum, 1)
                pe.wait_ge(S_.qkg_ready, L + 1)
                pe.wait_ge(S_.proj2_out, L * 11 + 11)
                for t in range(TT):
                    for c in range(2):
                        m = pe.transpose(ps[:, 0, (2 * t + c) * P:(2 * t + c + 1) * P], kdT[:, c, t * P:(t + 1) * P], ident)
                m.then_inc(S_.kd_psum, 1)
                for h in range(GH):
                    rows = slice(64 * (h % 2), 64 * (h % 2) + 64)
                    for t in range(TT):
                        m = pe.matmul(bank(1 + h % 2, 2, TT, P)[:, h // 2, t, :], kgT[rows, h // 2, t * P:(t + 1) * P],
                                      qgT[rows, h // 2, t * P:(t + 1) * P], start=True, stop=True)
                m.then_inc(S_.at_psum, 1)
                pe.wait_ge(S_.kd_ready, L + 1)
                pe.wait_ge(S_.yb_ready, L + 1)
                for n in range(NCH - 1):
                    if n >= 2:
                        pe.wait_ge(S_.state_ready, L * (NCH - 1) + (n - 1))
                    rows = slice(GCH * (n % 4), GCH * (n % 4) + GCH)
                    for c in range(2):
                        m = pe.matmul(bank(3 + n % 2, 2, S)[:, c, :], kd[rows, n // 4, c, :],
                                      vc[rows, n // 4, c * 2 * GDV:(c + 1) * 2 * GDV], start=True, stop=True)
                    m.then_inc(S_.ds_psum, 1)
                pe.wait_ge(S_.conv_ready, L + 1)
                for c in range(2):
                    m = pe.matmul(ps[:, 0, 0:S], ones, cvT[:, c, :], start=c == 0, stop=c == 1)
                m.then_inc(S_.csum_psum, 1)
                pe.wait_ge(S_.at_ready, L + 1)
                pe.wait_ge(S_.state_ready, L * (NCH - 1) + NCH - 1)
                pe.wait_ge(S_.yT2_lo_ready, L * 4 + 1)
                for h in range(GH):
                    o = bank(5 + h % 2, 2, S)[:, h // 2, :]
                    rows = slice(64 * (h % 2), 64 * (h % 2) + 64)
                    for t in range(TT):
                        pe.matmul(o[:, t * P:(t + 1) * P], vc[:, t, h * P:(h + 1) * P], atT[:, h, t, :],
                                  start=True, stop=False)
                        for n in range(max(1, 4 * t), 4 * t + 4):
                            m = pe.matmul(o[:, n * GCH:(n + 1) * GCH], st8[rows, n, h // 2, :],
                                          qgT[rows, h // 2, n * GCH:(n + 1) * GCH], start=False, stop=n == 4 * t + 3)
                m.then_inc(S_.o_psum, 1)
                pe.wait_ge(S_.csq_ready, L + 1)
                for c in range(2):
                    m = pe.matmul(ps[:, 0, S:2 * S], ones, agT[:, c, :], start=c == 0, stop=c == 1)
                m.then_inc(S_.cvar_psum, 1)
                pe.wait_ge(S_.osq_ready, L + 1)
                for h in range(GH):
                    m = pe.matmul(bank(1 + h // 2, 2, S)[:, h % 2, :], ones, rv[:, h, :], start=True, stop=True)
                m.then_inc(S_.osum_psum, 1)
                pe.wait_ge(S_.yT2_lo_ready, L * 4 + 4)
                for n in range(4):
                    o = [ps[:, 2 * t + n // 2, (n % 2) * 256:(n % 2) * 256 + 256] for t in range(TT)]
                    project_tok(u + (11 + n), o, yA_chunks + yM_chunks, 256)
                pe.wait_ge(S_.xn_ready, L * 2 + 7)
                transpose_x(xn, L * 8 + 32)
                open_sums()

            pe.wait_ge(S_.start_loaded, 96)
            pe.transpose(ps[:, 0, 0:P], ident, ident).then_inc(S_.unit_used, SPL)
            pe.wait_ge(S_.relb_ready, 1)
            for h in range(HA):
                m = pe.matmul(ps[:, h, 0:BUCKET_W], relb[:, h, :], onehot_sb[:], start=True, stop=True)
            m.then_inc(S_.bvec_psum, 1)
            pe.wait_ge(S_.bvec_ready, 1)
            with pe.Fori(0, 2) as L:
                mixer1(L, Count(0).loop(L, LAYER1_UNITS))
                with pe.If(L == 0):
                    feed_forward(Count(MIX1_UNITS), DENSE_STEPS, Count(0), hT_hi, hT_lo, F1)
                with pe.Else():
                    router()
                    with pe.Fori(0, E_N) as e:
                        feed_forward(Count(MOE_UNIT0).loop(e, EXPERT_UNITS), MOE_STEPS,
                                     Count(DENSE_STEPS).loop(e, MOE_STEPS), hT_hi, hT_lo, F1)
                close_sums()
            with pe.Fori(0, 2) as L:
                u = Count(BLOCK2_UNIT0).loop(L, LAYER2_UNITS)
                mixer2(L, u)
                feed_forward(u + MIX2_UNITS, DENSE_STEPS, Count(0).loop(L, DENSE_STEPS), h2_hi, h2_lo, F2)
                close_sums()

        @block.scalar
        def _(act):
            def split(u, width=UW):
                act.wait_ge(raw_landed[u.const % RAW], u.turns(RAW).value(16, 16))
                act.wait_ge(S_.unit_used, u.value(plus=1))
                act.activation(w_hi[:, u.const % SPL, 0:width], raw[:, u.const % RAW, 0:width], ACT.Copy)\
                   .then_inc(S_.hi_ready, 1)

            def split_next(u):
                for n in range(AHEAD):
                    split(u + n)

            def used(u):
                act.wait_ge(S_.unit_used, u.value(plus=SPL + 1))

            def x_parts(count):
                for b in range(4):
                    act.wait_ge(S_.xT_psum, count + b + 1)
                    act.activation(xT_hi[:, 2 * b:2 * b + 2, :], bank(4 + b, 2, S), ACT.Copy).then_inc(S_.xT_hi_ready, 1)

            def y_parts(src, dst, psum, count, done):
                for b in range(2):
                    act.wait_ge(psum, count + b + 1)
                    act.activation(dst[:, 2 * b:2 * b + 2, :], bank(6 + b, 2, S), ACT.Copy).then_inc(done, 1)

            def square_root(ready, done, count, v):
                act.wait_ge(ready, count)
                act.activation(v, v, ACT.Sqrt).then_inc(done, 1)

            def feed_forward(u, steps, count, hh, sig, gated):
                def step(j, at, odd, dyn, first):
                    if not first:
                        split(at + 1)
                        split(at + 2)
                    gated(at, odd, dyn)
                    split(at + (2 if first else 3))
                    act.wait_ge(sig["h_ready"], dyn.value(plus=3))
                    act.activation(hh[:, odd], sig["h"][:, odd].rearrange("p (c n) -> p c n", c=2), ACT.Copy)\
                       .then_inc(sig["h_hi_ready"], 1)

                step(0, u, 0, count, True)
                pairs = (steps - 1) // 2
                with act.Fori(0, pairs) as i:
                    for q in range(2):
                        step(None, (u + (2 + STEP * q)).loop(i, 2 * STEP), (1 + q) % 2, (count + (1 + q)).loop(i, 2), False)
                for j in range(2 * pairs + 1, steps):
                    step(j, u + (2 + STEP * (j - 1)), j % 2, count + j, False)

            def silu1(at, odd, dyn):
                act.wait_ge(S_.h1_ready, dyn.value(plus=1))
                used(at)
                act.activation(sa[:, odd], ps[:, 4 + 2 * odd, :], ACT.Silu).then_inc(S_.silu1_ready, 1)

            def conv2(at, odd, dyn):
                act.wait_ge(S_.h2_ready, dyn.value(plus=1))
                used(at)
                act.activation(u_a[:, odd, :, 2:], bank(4 + 2 * odd, 2, S), ACT.Copy).then_inc(S_.ua_ready, 1)
                used(at + 1)
                act.activation(u_g[:, odd, :, 2:], bank(5 + 2 * odd, 2, S), ACT.Copy).then_inc(S_.ug_ready, 1)
                act.wait_ge(S_.ca_ready, dyn.value(plus=1))
                act.activation(c_a[:, odd], c_a[:, odd], ACT.Silu).then_inc(S_.silu2_ready, 1)

            def mixer1(L, u):
                x_parts(L * 12)
                act.wait_ge(S_.p1_cols_psum, L + 1)
                act.activation(cols1[:], ps[:, 7, 0:20], ACT.Copy).then_inc(S_.p1_cols_ready, 1)
                for n in range(10):
                    split(u + (n + AHEAD))
                    used(u + n)
                    c = n % 2
                    if n < 4:
                        act.activation((qT if n < 2 else kT)[:, 2 * c:2 * c + 2, :], bank(n % 4, 2, S), ACT.Copy)\
                           .then_inc(S_.proj1_out, 1)
                    elif n < 6:
                        act.activation(vA[:, :, c * 256:(c + 1) * 256], bank(n % 4, TT, 256), ACT.Copy).then_inc(S_.proj1_out, 1)
                    elif n < 8:
                        act.activation(xmT[:, 2 * c:2 * c + 2, CONV_K - 1:], bank(n % 4, 2, S), ACT.Copy)\
                           .then_inc(S_.proj1_out, 1)
                    else:
                        act.activation(zg[:, :, c * 256:(c + 1) * 256], bank(n % 4, TT, 256), ACT.Sigmoid)\
                           .then_inc(S_.proj1_out, 1)
                    if n == 7:
                        act.wait_ge(S_.smax1, L * 2 + 1)
                        act.activation(sc0[:], sc0[:], ACT.Exp).then_inc(S_.expd1, 1)
                act.wait_ge(S_.smax1, L * 2 + 2)
                act.activation(sc1[:], sc1[:], ACT.Exp).then_inc(S_.expd1, 1)
                act.wait_ge(S_.conv1_done, L + 1)
                for c in range(4):
                    m = act.activation(xcT[:, c, :], xcT[:, c, :], ACT.Silu, bias=cols1[:, 16 + c:17 + c])
                m.then_inc(S_.xc_ready, 1)
                act.wait_ge(S_.qk_m_psum, L + 1)
                act.activation(qT[:], bank(0, 4, S), ACT.Copy)
                act.activation(kT[:], bank(2, 4, S), ACT.Copy).then_inc(S_.qk_m_ready, 1)
                for h in range(HA):
                    act.wait_ge(S_.pT1_psum, L * HA + (h + 1))
                    if h >= 2:
                        act.wait_ge(S_.pv1, L * HA + (h - 1))
                    act.activation(pT1[:, h % 2], bank(6 + h % 2, 3, P), ACT.Copy).then_inc(S_.pT1_ready, 1)
                y_parts(None, yA_hi, S_.yT_psum, L * 4, S_.yT_hi_ready)
                act.wait_ge(S_.v_m_psum, L + 1)
                act.activation(vT[:], bank(0, 4, S), ACT.Copy)
                for t in range(TT):
                    m = act.activation(vme[:, t, :, 0:HDM], bank(2 + t, HM, HDM), ACT.Copy)
                m.then_inc(S_.v_m_ready, 1)
                act.wait_ge(S_.f_ready, L + 1)
                act.activation(stat[:, 16:24], stat[:, 8:16], ACT.Abs)
                act.drain()
                act.activation(stat[:, 16:24], stat[:, 16:24], ACT.Exp, scale=-1.0)
                act.drain()
                act.activation(stat[:, 16:24], stat[:, 16:24], ACT.Ln, bias=1.0).then_inc(S_.f_ln, 1)
                act.wait_ge(S_.dloc_ready, L + 1)
                for t in range(TT):
                    for h in range(HM):
                        act.activation(dm[:, t, h, :], dm[:, t, h, :], ACT.Exp, bias=stat[:, 72 + 4 * t + h:73 + 4 * t + h])
                act.activation(stat[:, 80:96], stat[:, 80:96], ACT.Exp).then_inc(S_.dexp_ready, 1)
                act.wait_ge(S_.sT_psum, L + 1)
                act.activation(dm[:].rearrange("p t h n -> p (t h n)"), ps[:, 6:8, :].rearrange("p b n -> p (b n)"), ACT.Copy)\
                   .then_inc(S_.sT_ready, 1)
                act.wait_ge(S_.cn_psum, L + 1)
                act.activation(cn[:].rearrange("p (b h) e -> p b (h e)", b=2), ps[:, 2:4, 0:2 * (HDM + 1)], ACT.Copy)\
                   .then_inc(S_.cn_ready, 1)
                square_root(S_.sqrt_in, S_.sqrt_out, L * 3 + 1, stat[:, 112:120])
                y_parts(None, yM_hi, S_.yT_psum, L * 4 + 2, S_.yT_hi_ready)
                gates = 0
                for m_, (kind, c) in enumerate(MERGE_UNITS):
                    split(u + (10 + m_ + AHEAD))
                    if kind in ("ga", "gm"):
                        act.wait_ge(S_.gate_lin, L * 8 + (gates + 1))
                        v = ga if kind == "ga" else gm
                        act.activation(v[:], v[:], ACT.Sigmoid).then_inc(S_.gate_sig, 1)
                        gates += 1
                x_parts(L * 12 + 4)
                for n, (c0, w) in enumerate(WO_UNITS):
                    k = n + AHEAD
                    split(u + (22 + k), KC * WO_UNITS[k][1] if k < len(WO_UNITS) else UW)
                layer_norm_root(L * 3 + 2)
                x_parts(L * 12 + 8)

            def layer_norm_root(count):
                square_root(S_.sqrt_in, S_.sqrt_out, count, stat[:, 120:122])

            def router():
                act.wait_ge(S_.rexp_in, 1)
                act.activation(rt[:, 0], rt[:, 0], ACT.Exp).then_inc(S_.rexp_out, 1)
                for q in range(4):
                    act.wait_ge(S_.gateb_psum, q + 1)
                    act.activation(gateb[:, 2 * q:2 * q + 2, :], bank(4 + q, 2, S), ACT.Copy).then_inc(S_.gateb_ready, 1)

            def mixer2(L, u):
                square_root(S_.sqrt2_in, S_.sqrt2_out, L * 5 + 1, stat[:, 120:122])
                x_parts(L * 8 + 24)

                def out(n):
                    split(u + (n + AHEAD))
                    used(u + n)

                out(0)
                act.activation(avT[:, :, CW - 1:], bank(0, 2, S), ACT.Copy).then_inc(S_.proj2_out, 1)
                out(1)
                act.activation(agT[:], bank(1, 2, S), ACT.Sigmoid).then_inc(S_.proj2_out, 1)
                act.wait_ge(S_.p2_cols_psum, L + 1)
                act.activation(cols2[:], ps[:, 7, 0:250], ACT.Copy).then_inc(S_.p2_cols_ready, 1)
                act.wait_ge(S_.g16_psum, L + 1)
                act.activation(gT[:], ps[0:16, 6, 0:S], ACT.Copy).then_inc(S_.g16_ready, 1)
                out(2)
                act.activation(qbT[:], bank(2, 2, S), ACT.Copy).then_inc(S_.proj2_out, 1)
                out(3)
                act.activation(kbT[:], bank(3, 2, S), ACT.Copy).then_inc(S_.proj2_out, 1)
                out(4)
                act.activation(vb[:], bank(0, TT, 256), ACT.Copy).then_inc(S_.proj2_out, 1)
                out(5)
                act.activation(qcT[:], bank(1, 2, S), ACT.Copy, scale=float(GDK) ** -0.5).then_inc(S_.proj2_out, 1)
                out(6)
                act.activation(kcT[:], bank(2, 2, S), ACT.Copy).then_inc(S_.proj2_out, 1)
                out(7)
                act.activation(vc[:, :, 0:256], bank(3, TT, 256), ACT.Copy).then_inc(S_.proj2_out, 1)
                act.wait_ge(S_.smax2, L + 1)
                act.activation(sb0[:], sb0[:], ACT.Exp)
                act.activation(sb1[:], sb1[:], ACT.Exp).then_inc(S_.expd2, 1)
                act.wait_ge(S_.glog_in, L + 1)
                act.activation(egT[:], laT[:], ACT.Abs)
                act.drain()
                act.activation(egT[:], egT[:], ACT.Exp, scale=-1.0)
                act.drain()
                act.activation(egT[:], egT[:], ACT.Ln, bias=1.0).then_inc(S_.gln_ready, 1)
                out(8)
                act.activation(vc[:, :, 256:512], bank(0, TT, 256), ACT.Copy).then_inc(S_.proj2_out, 1)
                out(9)
                act.activation(rT[:, 0:2, :], bank(1, 2, S), ACT.Silu).then_inc(S_.proj2_out, 1)
                out(10)
                act.activation(rT[:, 2:4, :], bank(2, 2, S), ACT.Silu).then_inc(S_.proj2_out, 1)
                act.wait_ge(S_.cum_ready, L + 1)
                act.activation(egT[:], cumT[:], ACT.Exp, scale=1.0 / TAU)
                act.activation(laT[:], cumT[:], ACT.Exp, scale=-1.0 / TAU)
                act.activation(dec[:], stat[:, 128:144].rearrange("p (c n) -> p c n", c=2), ACT.Exp, scale=1.0 / TAU)\
                   .then_inc(S_.gexp_ready, 1)
                act.wait_ge(S_.rest_ready, L + 1)
                act.activation(cumT[:], cumT[:], ACT.Exp, scale=1.0 / TAU).then_inc(S_.gexp_ready, 1)
                for h in range(HB):
                    act.wait_ge(S_.pT2_psum, L * HB + (h + 1))
                    if h >= 2:
                        act.wait_ge(S_.pv2, L * HB + (h - 1))
                    act.activation(pT2[:, h % 2], bank(6 + h % 2, 3, P), ACT.Copy).then_inc(S_.pT2_ready, 1)
                square_root(S_.sqrt2_in, S_.sqrt2_out, L * 5 + 2, stat[:, 112:120])
                act.wait_ge(S_.yb_psum, L + 1)
                act.activation(yA_hi[:, 2:4, :], bank(6, 2, S), ACT.Copy).then_inc(S_.yT2_hi_ready, 1)
                act.wait_ge(S_.kd_psum, L + 1)
                act.activation(kd[:].rearrange("p t c n -> p (t c n)"), ps[:, 0, :], ACT.Copy).then_inc(S_.kd_ready, 1)
                act.wait_ge(S_.cent_ready, L + 1)
                act.activation(agT[:], cvT[:], ACT.Square).then_inc(S_.csq_ready, 1)
                act.wait_ge(S_.o_psum, L + 1)
                act.activation(rv[:], bank(5, 4, S), ACT.Square).then_inc(S_.osq_ready, 1)
                square_root(S_.sqrt2_in, S_.sqrt2_out, L * 5 + 3, agT[:, 0, :])
                act.wait_ge(S_.cnorm_ready, L + 1)
                for c in range(2):
                    act.activation(cvT[:, c, :], cvT[:, c, :], ACT.Silu, scale=cols2[:, 64 + c:65 + c], bias=cols2[:, 66 + c:67 + c])
                act.drain()
                act.activation(yA_hi[:, 0:2, :], cvT[:], ACT.Copy).then_inc(S_.yT2_hi_ready, 1)
                square_root(S_.sqrt2_in, S_.sqrt2_out, L * 5 + 4, rv[:])
                for q in range(2):
                    act.wait_ge(S_.oc_ready, L * 2 + (q + 1))
                    act.activation(yM_hi[:, 2 * q:2 * q + 2, :], oc[:, 2 * q:2 * q + 2, :], ACT.Copy).then_inc(S_.yT2_hi_ready, 1)
                for n in range(4):
                    split(u + (11 + n + AHEAD))
                square_root(S_.sqrt2_in, S_.sqrt2_out, L * 5 + 5, stat[:, 120:122])
                x_parts(L * 8 + 28)

            act.wait_ge(S_.start_loaded, 96)
            act.activation(stat[:, 0:1], ones[:, 0:1], ACT.Copy).then_inc(S_.hi_ready, RAW)
            act.wait_ge(S_.bvec_psum, 1)
            act.activation(bvec[:], ps[:, :, 0:BUCKET_W], ACT.Copy).then_inc(S_.bvec_ready, 1)
            for n in range(AHEAD):
                split(Count(n))
            with act.Fori(0, 2) as L:
                mixer1(L, Count(0).loop(L, LAYER1_UNITS))
                with act.If(L == 0):
                    feed_forward(Count(MIX1_UNITS), DENSE_STEPS, Count(0), hT_hi, F1, silu1)
                    split_next(Count(LAYER1_UNITS))
                with act.Else():
                    router()
                    with act.Fori(0, E_N) as e:
                        at = Count(MOE_UNIT0).loop(e, EXPERT_UNITS)
                        feed_forward(at, MOE_STEPS, Count(DENSE_STEPS).loop(e, MOE_STEPS), hT_hi, F1, silu1)
                        split_next(at + EXPERT_UNITS)
                square_root(S_.sqrt_in, S_.sqrt_out, L * 3 + 3, stat[:, 120:122])
            with act.Fori(0, 2) as L:
                u = Count(BLOCK2_UNIT0).loop(L, LAYER2_UNITS)
                mixer2(L, u)
                at = u + MIX2_UNITS
                feed_forward(at, DENSE_STEPS, Count(0).loop(L, DENSE_STEPS), h2_hi, F2, conv2)
                with act.If(L == 0):
                    split_next(at + STEP * DENSE_STEPS)
                with act.Else():
                    act.nop()
            square_root(S_.sqrt2_in, S_.sqrt2_out, 11, stat[:, 120:122])

        @block.vector
        def _(dve):
            def split(u, width=UW):
                dve.wait_ge(S_.hi_ready, u.value(plus=RAW + 1))
                dve.tensor_tensor(w_lo[:, u.const % SPL, 0:width], raw[:, u.const % RAW, 0:width],
                                  w_hi[:, u.const % SPL, 0:width].bitcast(F32), ALU.subtract).then_inc(S_.lo_ready, 1)

            def split_next(u):
                for n in range(AHEAD):
                    split(u + n)

            def used(u):
                dve.wait_ge(S_.unit_used, u.value(plus=SPL + 1))

            def x_parts(count):
                for b in range(4):
                    dve.wait_ge(S_.xT_hi_ready, count + b + 1)
                    hi = xT_hi[:, 2 * b:2 * b + 2, :]
                    dve.tensor_tensor(xT_lo[:, 2 * b:2 * b + 2, :], bank(4 + b, 2, S), hi.bitcast(F32), ALU.subtract)\
                       .then_inc(S_.xT_lo_ready, 1)

            def y_parts(dst, hi, ready, count, done):
                for b in range(2):
                    dve.wait_ge(ready, count + b + 1)
                    dve.tensor_tensor(dst[:, 2 * b:2 * b + 2, :], bank(6 + b, 2, S), hi[:, 2 * b:2 * b + 2, :].bitcast(F32),
                                      ALU.subtract).then_inc(done, 1)

            def col(a, n=1):
                return stat[:, a:a + n]

            def layer_norm(count, norms):
                for t in range(TT):
                    dve.scalar_tensor_tensor(x[:, t, :], x[:, t, :], ALPHA, bank(2 * t, D), ALU.mult, ALU.add)
                dve.drain()
                for t in range(TT):
                    for h in range(2):
                        dve.bn_stats(col(122 + 12 * t + 6 * h, 6), x[:, t, h * HALF:(h + 1) * HALF])
                dve.drain()
                for t in range(TT):
                    dve.bn_aggr(col(146 + 2 * t, 2), col(122 + 12 * t, 12))
                dve.drain()
                for t in range(TT):
                    m = dve.tensor_scalar(col(120 + t), col(147 + 2 * t), LN_EPS, None, ALU.add)
                m.then_inc(S_.sqrt_in, 1)
                dve.wait_ge(S_.sqrt_out, count)
                dve.reciprocal(col(120, 2), col(120, 2))
                dve.drain()
                for t in range(TT):
                    dve.tensor_scalar(x[:, t, :], x[:, t, :], col(146 + 2 * t), col(120 + t), ALU.subtract, ALU.mult)
                dve.drain()
                dve.wait_ge(S_.norm_loaded, norms)
                for t in range(TT):
                    dve.tensor_tensor(x[:, t, :], x[:, t, :], norm_gb[:, 0, :], ALU.mult)
                dve.drain()
                for t in range(TT):
                    m = dve.tensor_tensor(x[:, t, :], x[:, t, :], norm_gb[:, 1, :], ALU.add)
                m.then_inc(S_.xn_ready, 1)

            def rms_norm(count, norms, done):
                for t in range(TT):
                    dve.tensor_tensor_reduce(out=xn[:, t, :], in0=x[:, t, :], in1=x[:, t, :], scale=1.0, scalar=0.0,
                                             op0=ALU.mult, op1=ALU.add, accum_out=col(120 + t))
                dve.drain()
                dve.tensor_scalar(col(120, 2), col(120, 2), 1.0 / D, RMS_EPS, ALU.mult, ALU.add).then_inc(S_.sqrt2_in, 1)
                dve.wait_ge(S_.sqrt2_out, count)
                dve.reciprocal(col(120, 2), col(120, 2))
                dve.drain()
                dve.wait_ge(S_.norm2_loaded, norms)
                for t in range(TT):
                    m = dve.scalar_tensor_tensor(xn[:, t, :], x[:, t, :], col(120 + t), norm_gb[:, 0, :], ALU.mult, ALU.mult)
                m.then_inc(done, 1)

            def feed_forward(u, steps, count, hh, hl, sig, hidden):
                def step(at, odd, dyn, first):
                    if not first:
                        split(at + 1)
                        split(at + 2)
                    hidden(at, odd, dyn)
                    split(at + (2 if first else 3))
                    dve.wait_ge(sig["h_hi_ready"], dyn.value(plus=1))
                    dve.tensor_tensor(hl[:, odd], sig["h"][:, odd].rearrange("p (c n) -> p c n", c=2),
                                      hh[:, odd].bitcast(F32), ALU.subtract).then_inc(sig["h_lo_ready"], 1)

                step(u, 0, count, True)
                pairs = (steps - 1) // 2
                with dve.Fori(0, pairs) as i:
                    for q in range(2):
                        step((u + (2 + STEP * q)).loop(i, 2 * STEP), (1 + q) % 2, (count + (1 + q)).loop(i, 2), False)
                for j in range(2 * pairs + 1, steps):
                    step(u + (2 + STEP * (j - 1)), j % 2, count + j, False)

            def dense_hidden(at, odd, dyn):
                dve.wait_ge(S_.silu1_ready, dyn.value(plus=1))
                used(at + 1)
                dve.tensor_tensor(hf[:, odd], sa[:, odd], ps[:, 5 + 2 * odd, :], ALU.mult).then_inc(S_.h1_ready, 1)

            def expert_hidden(e):
                def hidden(at, odd, dyn):
                    dve.wait_ge(S_.silu1_ready, dyn.value(plus=1))
                    used(at + 1)
                    dve.tensor_tensor(hf[:, odd], sa[:, odd], ps[:, 5 + 2 * odd, :], ALU.mult)
                    dve.drain()
                    h = hf[:, odd].rearrange("p (c n) -> p c n", c=2)
                    g = gateb[:, bass.ds(e, 1), :].rearrange("p o n -> p (o n)")
                    dve.tensor_tensor(h, h, spread(g, 1, 2), ALU.mult).then_inc(S_.h1_ready, 1)
                return hidden

            def less_max(sc, mx):
                dve.reduce_max(mx, sc, AX_X)
                dve.drain()
                return dve.tensor_tensor(sc, sc, spread(mx, 2, sc.shape[2]), ALU.subtract)

            def mixer1(L, u):
                dve.memset(xmT[:, :, 0:CONV_K - 1], 0.0)
                x_parts(L * 12)
                for n in range(6):
                    split(u + (n + AHEAD))
                for tile, heads, b, per, step in ((0, range(0, 8), 4, 4, 1), (1, range(0, 4), 6, 2, 2), (1, range(4, 8), 4, 2, 3)):
                    dve.wait_ge(S_.scores1, L * 3 + step)
                    n = P * (tile + 1)
                    for q in range(2):
                        hs = slice(heads[0] + q, heads[-1] + 1, 2)
                        m = dve.scalar_tensor_tensor((sc0, sc1)[tile][:, hs, :], bank(b + q, per, n), HDA ** -0.5,
                                                     bias[:, hs, S - n:S], ALU.mult, ALU.add)
                    m.then_inc(S_.scores1_in, 1)
                    dve.drain()
                    if step == 1:
                        less_max(sc0[:], col(160, 8)).then_inc(S_.smax1, 1)
                    if step == 2:
                        split(u + (6 + AHEAD))
                        split(u + (7 + AHEAD))
                less_max(sc1[:], col(168, 8)).then_inc(S_.smax1, 1)
                dve.wait_ge(S_.proj1_out, L * 10 + 8)
                dve.wait_ge(S_.p1_cols_ready, L + 1)
                for k in range(CONV_K):
                    for c in range(4):
                        w = cols1[:, 4 * k + c:4 * k + c + 1]
                        if k == 0:
                            m = dve.tensor_scalar(xcT[:, c, :], xmT[:, c, 0:S], w, None, ALU.mult)
                        else:
                            m = dve.scalar_tensor_tensor(xcT[:, c, :], xmT[:, c, k:k + S], w, xcT[:, c, :], ALU.mult, ALU.add)
                    if k < CONV_K - 1:
                        dve.drain()
                m.then_inc(S_.conv1_done, 1)
                split(u + (8 + AHEAD))
                for t, sc in enumerate((sc0, sc1)):
                    dve.wait_ge(S_.expd1, L * 2 + t + 1)
                    n = P * (t + 1)
                    dve.tensor_tensor(sc[:], sc[:], spread(K["wincount"][:, S - n:S], 1, HA), ALU.mult).then_inc(S_.prob1, 1)
                    dve.drain()
                    dve.reduce_sum(col(176 + 8 * t, 8), sc[:], AX_X)
                dve.drain()
                dve.reciprocal(col(176, 16), col(176, 16))
                dve.drain()
                dve.wait_ge(S_.proj1_out, L * 10 + 10)
                dve.tensor_tensor(zg[:], zg[:], spread(gain_m[:], 1, TT), ALU.mult)
                split(u + (9 + AHEAD))
                ya = ht[:].rearrange("p t h e -> p (t h e)")[:, 0:TT * DM].rearrange("p (t n) -> p t n", t=TT)
                dve.wait_ge(S_.pv1, L * HA + HA)
                for t in range(TT):
                    m = dve.tensor_tensor(ya[:, t, :].rearrange("p (h e) -> p h e", h=HA), bank(4 + t, HA, HDA),
                                          spread(col(176 + 8 * t, 8), 2, HDA), ALU.mult)
                m.then_inc(S_.ya1_ready, 1)
                y_parts(yA_lo, yA_hi, S_.yT_hi_ready, L * 4, S_.yT_lo_ready)
                dve.wait_ge(S_.v_m_psum, L + 1)
                dve.memset(vme[:, :, :, HDM:], 1.0)
                dve.wait_ge(S_.gates_psum, L + 1)
                g = bank(5, 2, 8)
                dve.tensor_tensor(col(0, 8).rearrange("p (t h) -> p t h", t=TT), g[:, :, 0:4], spread(b_if[:, 0:4], 1, TT), ALU.add)
                dve.tensor_tensor(col(8, 8).rearrange("p (t h) -> p t h", t=TT), g[:, :, 4:8], spread(b_if[:, 4:8], 1, TT), ALU.add)\
                   .then_inc(S_.f_ready, 1)
                dve.wait_ge(S_.f_ln, L + 1)
                dve.scalar_tensor_tensor(col(16, 8), col(8, 8), 0.0, col(16, 8), ALU.min, ALU.subtract).then_inc(S_.logf_ready, 1)
                dve.wait_ge(S_.cum_psum, L + 1)
                c4 = lambda a: col(a, 8).rearrange("p (t h) -> p t h", t=TT)
                dve.tensor_copy(col(24, 8), ps[:, 5, 32:40])
                dve.tensor_copy(col(32, 8), ps[:, 5, 40:48])
                dve.tensor_tensor(col(40, 8), col(0, 8), ps[:, 5, 32:40], ALU.subtract)
                dve.drain()
                dg = ya
                for t in range(TT):
                    m = dve.tensor_tensor(dg[:, t, :].rearrange("p (h s) -> p h s", h=HM), spread(ident, 1, HM),
                                          spread(col(40 + 4 * t, 4), 2, P), ALU.mult)
                m.then_inc(S_.diag_ready, 1)
                dve.wait_ge(S_.rowr_psum, L + 1)
                dve.reduce_max(col(48, 4), bank(6, HM, P), AX_X)
                for t in range(TT):
                    dve.tensor_tensor(dm[:, t], bank(6 + t, HM, P), spread(K["tri"], 1, HM), ALU.add)
                dve.drain()
                for t in range(TT):
                    dve.reduce_max(col(52 + 4 * t, 4), dm[:, t], AX_X)
                dve.scalar_tensor_tensor(col(60, 4), col(48, 4), 0.0, col(32, 4), ALU.max, ALU.add)
                dve.drain()
                dve.tensor_copy(col(152, 4), col(24, 4))
                dve.tensor_tensor(col(156, 4), col(28, 4), col(60, 4), ALU.add)
                dve.tensor_tensor(col(64, 8), col(52, 8), col(24, 8), ALU.add)
                dve.drain()
                dve.tensor_tensor(col(64, 8), col(64, 8), col(152, 8), ALU.max)
                dve.tensor_tensor(col(92, 4), col(40, 4), col(32, 4), ALU.add)
                dve.drain()
                dve.tensor_tensor(col(72, 8), col(24, 8), col(64, 8), ALU.subtract)
                dve.tensor_tensor(col(80, 4), col(156, 4), col(68, 4), ALU.subtract)
                dve.tensor_scalar(col(84, 8), col(64, 8), -1.0, None, ALU.mult)
                dve.tensor_tensor(col(92, 4), col(92, 4), col(60, 4), ALU.subtract).then_inc(S_.dloc_ready, 1)
                dve.wait_ge(S_.dexp_ready, L + 1)
                for t in range(TT):
                    m = dve.scalar_tensor_tensor(dm[:, t].rearrange("p h n -> p (h n)"), ps[:, t, :], HDM ** -0.5,
                                                 dm[:, t].rearrange("p h n -> p (h n)"), ALU.mult, ALU.mult)
                m.then_inc(S_.s_ready, 1)
                dve.scalar_tensor_tensor(kw[:], bank(4, HM, HDM), HDM ** -0.5, spread(col(92, 4), 2, HDM), ALU.mult, ALU.mult)\
                   .then_inc(S_.kw_ready, 1)
                dve.wait_ge(S_.num_psum, L + 1)
                E1 = HDM + 1
                flat = ht[:].rearrange("p t (b h) e -> p t b (h e)", b=2)
                dve.tensor_copy(flat[:, 0], ps[:, 0:2, 0:2 * E1])
                for b in range(2):
                    dve.tensor_tensor(ht[:, 1, 2 * b:2 * b + 2, :], bank(2 + b, 2, E1), spread(col(80 + 2 * b, 2), 2, E1), ALU.mult)
                dve.drain()
                dve.tensor_tensor(flat[:, 1], flat[:, 1], ps[:, 4:6, 0:2 * E1], ALU.add)
                dve.drain()
                hv = ht[:].rearrange("p t h e -> p (t h) e")
                nq = hv[:, :, HDM:HDM + 1].rearrange("p a o -> p (a o)")
                h_ = hv[:, :, 0:HDM]
                dve.tensor_scalar(col(96, 8), nq, -1.0, None, ALU.mult)
                dve.drain()
                dve.tensor_tensor(col(96, 8), col(96, 8), nq, ALU.max)
                dve.drain()
                dve.tensor_tensor(col(96, 8), col(96, 8), col(84, 8), ALU.max)
                dve.drain()
                dve.reciprocal(col(96, 8), col(96, 8))
                dve.drain()
                dve.tensor_tensor(h_, h_, spread(col(96, 8), 2, HDM), ALU.mult)
                dve.drain()
                dve.reduce_sum(col(104, 8), h_, AX_X)
                dve.drain()
                dve.tensor_scalar(col(104, 8), col(104, 8), 1.0 / HDM, None, ALU.mult)
                dve.drain()
                dve.tensor_tensor(h_, h_, spread(col(104, 8), 2, HDM), ALU.subtract)
                dve.drain()
                sq = dm[:].rearrange("p t h n -> p (t h) n")
                dve.tensor_tensor(sq, h_, h_, ALU.mult)
                dve.drain()
                dve.reduce_sum(col(112, 8), sq, AX_X)
                dve.drain()
                dve.tensor_scalar(col(112, 8), col(112, 8), 1.0 / HDM, LN_EPS, ALU.mult, ALU.add).then_inc(S_.sqrt_in, 1)
                dve.wait_ge(S_.sqrt_out, L * 3 + 1)
                dve.reciprocal(col(112, 8), col(112, 8))
                dve.drain()
                dve.tensor_tensor(h_, h_, spread(col(112, 8), 2, HDM), ALU.mult)
                dve.drain()
                dve.tensor_tensor(h_, h_, zg[:].rearrange("p t (h e) -> p (t h) e", h=HM), ALU.mult).then_inc(S_.ym_ready, 1)
                y_parts(yM_lo, yM_hi, S_.yT_hi_ready, L * 4 + 2, S_.yT_lo_ready)
                dve.wait_ge(S_.bg_loaded, L * 16 + 16)
                gates = 0

                def merge(c):
                    dve.wait_ge(S_.gate_sig, L * 8 + 2 * c + 2)
                    q = slice((c % 2) * FFC, (c % 2 + 1) * FFC)
                    dve.tensor_tensor(ga[:], ga[:], ps[:, 0:2, q], ALU.mult)
                    dve.tensor_tensor(gm[:], gm[:], ps[:, 2:4, q], ALU.mult)
                    dve.drain()
                    dve.tensor_tensor(merged[:, :, c * FFC:(c + 1) * FFC], ga[:], gm[:], ALU.add).then_inc(S_.merged_ready, 1)
                    dve.drain()

                for m_, (kind, c) in enumerate(MERGE_UNITS):
                    split(u + (10 + m_ + AHEAD))
                    if kind in ("ga", "gm"):
                        used(u + (10 + m_))
                        i = kind == "gm"
                        dve.tensor_tensor((ga, gm)[i][:], bank(4 + gates % 4, TT, FFC),
                                          spread(bg[:, int(i), c * FFC:(c + 1) * FFC], 1, TT), ALU.add).then_inc(S_.gate_lin, 1)
                        gates += 1
                        if i and c != 2:
                            merge(c)
                            if c == 3:
                                pass
                    elif c and kind == "m":
                        used(u + (10 + m_))
                        merge(2)
                x_parts(L * 12 + 4)
                for n, (c0, w) in enumerate(WO_UNITS):
                    k = n + AHEAD
                    split(u + (22 + k), KC * WO_UNITS[k][1] if k < len(WO_UNITS) else UW)
                used(u + (MIX1_UNITS - 1))
                layer_norm(L * 3 + 2, L * 64 + 32)
                x_parts(L * 12 + 8)

            def router():
                dve.wait_ge(S_.router_loaded, 32)
                dve.tensor_copy(rw_hi[:], rw_raw[:])
                dve.drain()
                dve.tensor_tensor(rw_lo[:], rw_raw[:], rw_hi[:].bitcast(F32), ALU.subtract).then_inc(S_.rw_split, 1)
                dve.wait_ge(S_.logits_psum, 1)
                dve.tensor_tensor(lg[:], bank(4, TT, E_N), spread(rb[:], 1, TT), ALU.add)
                dve.drain()
                for t in range(TT):
                    other, own = spread(lg[:, t, :], 1, E_N), spread(lg[:, t, :], 2, E_N)
                    dve.tensor_tensor(cmp2[:, 0], other, own, ALU.is_gt)
                    dve.tensor_tensor(cmp2[:, 1], other, own, ALU.is_equal)
                    dve.drain()
                    dve.tensor_tensor(cmp2[:, 1], cmp2[:, 1], K["lower"].rearrange("p (e j) -> p e j", e=E_N), ALU.mult)
                    dve.drain()
                    dve.tensor_tensor(cmp2[:, 0], cmp2[:, 0], cmp2[:, 1], ALU.add)
                    dve.drain()
                    dve.reduce_sum(rt[:, 1, t, :], cmp2[:, 0], AX_X)
                    dve.reduce_max(rt[:, 2, t, 0:1], lg[:, t, :], AX_X)
                    dve.drain()
                    dve.tensor_scalar(rt[:, 1, t, :], rt[:, 1, t, :], 2.0, None, ALU.is_lt)
                    m = dve.tensor_scalar(rt[:, 0, t, :], lg[:, t, :], rt[:, 2, t, 0:1], None, ALU.subtract)
                m.then_inc(S_.rexp_in, 1)
                dve.wait_ge(S_.rexp_out, 1)
                dve.tensor_tensor(rt[:, 0], rt[:, 0], rt[:, 1], ALU.mult)
                dve.drain()
                dve.reduce_sum(col(100, 2), rt[:, 0], AX_X)
                dve.drain()
                dve.reciprocal(col(100, 2), col(100, 2))
                dve.drain()
                dve.tensor_tensor(rt[:, 0], rt[:, 0], spread(col(100, 2), 2, E_N), ALU.mult)
                dve.drain()
                for q in range(4):
                    if q >= 2:
                        dve.wait_ge(S_.gateb_psum, q - 1)
                    for e in range(2):
                        m = dve.tensor_copy(gcols[:, q % 2, e], spread(rt[:, 0, :, 2 * q + e], 2, P))
                    m.then_inc(S_.gcols_ready, 1)

            def mixer2(L, u):
                rms_norm(L * 5 + 1, L * 32 + 16, S_.xn_ready)
                dve.memset(avT[:, :, 0:CW - 1], 0.0)
                x_parts(L * 8 + 24)
                for n in (0, 1):
                    split(u + (n + AHEAD))
                dve.wait_ge(S_.proj2_out, L * 11 + 2)
                dve.tensor_tensor(avT[:, :, CW - 1:], avT[:, :, CW - 1:], agT[:], ALU.mult)
                dve.drain()
                dve.wait_ge(S_.p2_cols_ready, L + 1)
                taps = [0]

                def convolve(n):
                    for k in range(taps[0], taps[0] + n):
                        for c in range(2):
                            w = cols2[:, 2 * k + c:2 * k + c + 1]
                            if k == 0:
                                m = dve.tensor_scalar(cvT[:, c, :], avT[:, c, 0:S], w, cols2[:, 62 + c:63 + c], ALU.mult, ALU.add)
                            else:
                                m = dve.scalar_tensor_tensor(cvT[:, c, :], avT[:, c, k:k + S], w, cvT[:, c, :], ALU.mult, ALU.add)
                        if k < CW - 1:
                            dve.drain()
                    taps[0] += n
                    if taps[0] == CW:
                        m.then_inc(S_.conv_ready, 1)

                split(u + (2 + AHEAD))
                convolve(3)
                split(u + (3 + AHEAD))
                convolve(3)
                split(u + (4 + AHEAD))
                dve.wait_ge(S_.scores2, L * 2 + 1)
                for q in range(2):
                    dve.scalar_tensor_tensor(sb0[:, q::2, :], bank(4 + q, 2, P), HDB ** -0.5,
                                             spread(K["causal"][:, P:S], 1, 2), ALU.mult, ALU.add)
                dve.wait_ge(S_.scores2, L * 2 + 2)
                for q in range(2):
                    m = dve.scalar_tensor_tensor(sb1[:, q::2, :], bank(6 + q, 2, S), HDB ** -0.5,
                                                 spread(K["causal"], 1, 2), ALU.mult, ALU.add)
                m.then_inc(S_.scores2_in, 1)
                dve.drain()
                less_max(sb0[:], col(160, 4))
                split(u + (5 + AHEAD))
                less_max(sb1[:], col(164, 4)).then_inc(S_.smax2, 1)
                dve.wait_ge(S_.glog_psum, L + 1)
                for c in range(2):
                    m = dve.tensor_scalar(laT[:, c, :], ps[:, 7, c * S:(c + 1) * S], cols2[:, 68 + c:69 + c], None, ALU.add)
                m.then_inc(S_.glog_in, 1)
                for n in range(6, 11):
                    if n == 8:
                        dve.wait_ge(S_.expd2, L + 1)
                        for t, sc in enumerate((sb0, sb1)):
                            dve.reduce_sum(col(176 + 4 * t, 4), sc[:], AX_X)
                        dve.drain()
                        dve.reciprocal(col(176, 8), col(176, 8))
                        dve.drain()
                        dve.memset(stat[:, 0:1], 0.0).then_inc(S_.prob2, 2)
                    split(u + (n + AHEAD))
                    convolve(4)
                dve.wait_ge(S_.gln_ready, L + 1)
                dve.scalar_tensor_tensor(laT[:], laT[:], 0.0, egT[:], ALU.min, ALU.subtract)
                dve.drain()
                for c in range(2):
                    dve.tensor_tensor_scan(cumT[:, c, :], K["reset"], laT[:, c, :], 0.0, ALU.mult, ALU.add)
                dve.drain()
                ends = cumT[:].rearrange("p c (n i) -> p c n i", i=GCH)
                gam = col(128, 16).rearrange("p (c n) -> p c n", c=2)
                dve.tensor_copy(gam, ends[:, :, :, GCH - 1:GCH].rearrange("p c n o -> p c (n o)")).then_inc(S_.cum_ready, 1)
                dve.wait_ge(S_.gexp_ready, L * 2 + 1)
                for c in range(2):
                    m = dve.tensor_tensor(ends[:, c], spread(gam[:, c, :], 2, GCH), ends[:, c], ALU.subtract)
                m.then_inc(S_.rest_ready, 1)
                dve.tensor_tensor(qcT[:], qcT[:], egT[:], ALU.mult)
                dve.tensor_tensor(laT[:], kcT[:], laT[:], ALU.mult)
                convolve(2)
                dve.wait_ge(S_.gexp_ready, L * 2 + 2)
                dve.tensor_tensor(cumT[:], kcT[:], cumT[:], ALU.mult).then_inc(S_.qkg_ready, 1)
                dve.wait_ge(S_.pv2, L * HB + HB)
                yh = yb[:].rearrange("p t (h e) -> p t h e", h=HB)
                for t in range(TT):
                    dve.tensor_tensor(yh[:, t], bank(4 + t, HB, HDB), spread(col(176 + 4 * t, 4), 2, HDB), ALU.mult)
                dve.drain()
                yq = yb[:].rearrange("p t (h e) -> p (t h) e", h=HB)
                sq = sb0[:].rearrange("p h n -> p (h n)").rearrange("p (a e) -> p a e", e=HDB)
                dve.tensor_tensor(sq, yq, yq, ALU.mult)
                dve.drain()
                dve.reduce_sum(col(112, 8), sq, AX_X)
                dve.drain()
                dve.tensor_scalar(col(112, 8), col(112, 8), 1.0 / HDB, RMS_EPS, ALU.mult, ALU.add).then_inc(S_.sqrt2_in, 1)
                convolve(2)
                dve.wait_ge(S_.sqrt2_out, L * 5 + 2)
                dve.reciprocal(col(112, 8), col(112, 8))
                dve.drain()
                dve.tensor_tensor(yq, yq, spread(col(112, 8), 2, HDB), ALU.mult)
                dve.drain()
                dve.tensor_tensor(yb[:], yb[:], spread(gain_b[:], 1, TT), ALU.mult).then_inc(S_.yb_ready, 1)
                convolve(1)
                dve.wait_ge(S_.yT2_hi_ready, L * 4 + 1)
                dve.tensor_tensor(yA_lo[:, 2:4, :], bank(6, 2, S), yA_hi[:, 2:4, :].bitcast(F32), ALU.subtract)\
                   .then_inc(S_.yT2_lo_ready, 1)
                dve.wait_ge(S_.at_psum, L + 1)
                for q in range(2):
                    m = dve.tensor_tensor(atT[:, q::2], bank(1 + q, 2, TT, P), spread(spread(K["glamask"], 1, TT), 1, 2), ALU.mult)
                m.then_inc(S_.at_ready, 1)
                for n in range(NCH - 1):
                    dve.wait_ge(S_.ds_psum, L * (NCH - 1) + (n + 1))
                    for c in range(2):
                        for half in range(2):
                            rows = slice(64 * half, 64 * half + 64)
                            add = bank(3 + n % 2, 2, S)[rows, c, half * GDV:(half + 1) * GDV]
                            if n == 0:
                                m = dve.tensor_copy(st8[rows, 1, c, :], add)
                            else:
                                m = dve.scalar_tensor_tensor(st8[rows, n + 1, c, :], st8[rows, n, c, :], dec[rows, c, n:n + 1],
                                                             add, ALU.mult, ALU.add)
                    m.then_inc(S_.state_ready, 1)
                    dve.drain()
                dve.wait_ge(S_.csum_psum, L + 1)
                for c in range(2):
                    m = dve.scalar_tensor_tensor(cvT[:, c, :], ps[:, 0, 0:S], -1.0 / S, cvT[:, c, :], ALU.mult, ALU.add)
                m.then_inc(S_.cent_ready, 1)
                dve.wait_ge(S_.cvar_psum, L + 1)
                dve.tensor_scalar(agT[:, 0, :], ps[:, 0, S:2 * S], 1.0 / S, LN_EPS, ALU.mult, ALU.add).then_inc(S_.sqrt2_in, 1)
                dve.wait_ge(S_.sqrt2_out, L * 5 + 3)
                dve.reciprocal(agT[:, 0, :], agT[:, 0, :])
                dve.drain()
                dve.tensor_tensor(cvT[:], cvT[:], spread(agT[:, 0, :], 1, 2), ALU.mult).then_inc(S_.cnorm_ready, 1)
                dve.wait_ge(S_.yT2_hi_ready, L * 4 + 2)
                dve.tensor_tensor(yA_lo[:, 0:2, :], cvT[:], yA_hi[:, 0:2, :].bitcast(F32), ALU.subtract).then_inc(S_.yT2_lo_ready, 1)
                dve.wait_ge(S_.osum_psum, L + 1)
                dve.tensor_scalar(rv[:], bank(1, 4, S), 1.0 / GDV, RMS_EPS, ALU.mult, ALU.add).then_inc(S_.sqrt2_in, 1)
                dve.wait_ge(S_.sqrt2_out, L * 5 + 4)
                dve.reciprocal(rv[:], rv[:])
                dve.drain()
                dve.tensor_tensor(rv[:], rv[:], bank(5, 4, S), ALU.mult)
                dve.drain()
                for h in range(GH):
                    at_h = 2 * (h % 2) + h // 2
                    m = dve.scalar_tensor_tensor(oc[:, h, :], rv[:, at_h, :], cols2[:, 70 + h:71 + h], rT[:, h, :], ALU.mult, ALU.mult)
                    if h % 2:
                        m.then_inc(S_.oc_ready, 1)
                for q in range(2):
                    dve.wait_ge(S_.yT2_hi_ready, L * 4 + 3 + q)
                    dve.tensor_tensor(yM_lo[:, 2 * q:2 * q + 2, :], oc[:, 2 * q:2 * q + 2, :],
                                      yM_hi[:, 2 * q:2 * q + 2, :].bitcast(F32), ALU.subtract).then_inc(S_.yT2_lo_ready, 1)
                for n in range(4):
                    split(u + (11 + n + AHEAD))
                used(u + 14)
                for t in range(TT):
                    dve.tensor_tensor(x[:, t, :], x[:, t, :], bank(2 * t, D), ALU.add)
                dve.drain()
                rms_norm(L * 5 + 5, L * 32 + 32, S_.xn_ready)
                dve.memset(u_a[:, :, :, 0:2], 0.0)
                dve.memset(u_g[:, :, :, 0:2], 0.0)
                dve.drain()
                x_parts(L * 8 + 28)

            def conv_ffn(L):
                def hidden(at, odd, dyn):
                    j = Count(dyn.const, dyn.terms[1:]).value() * 2

                    def columns(src, dst, first):
                        for k in range(3):
                            for c in range(2):
                                w = cols2[:, bass.ds(j + (74 + 44 * k + first + c), 1)]
                                if k == 0:
                                    b = cols2[:, bass.ds(j + (74 + 132 + first + c), 1)]
                                    m = dve.tensor_scalar(dst[:, c, :], src[:, odd, c, 0:S], w, b, ALU.mult, ALU.add)
                                else:
                                    m = dve.scalar_tensor_tensor(dst[:, c, :], src[:, odd, c, k:k + S], w, dst[:, c, :],
                                                                 ALU.mult, ALU.add)
                            if k < 2:
                                dve.drain()
                        return m

                    dve.wait_ge(S_.ua_ready, dyn.value(plus=1))
                    columns(u_a, c_a[:, odd], 0).then_inc(S_.ca_ready, 1)
                    dve.wait_ge(S_.ug_ready, dyn.value(plus=1))
                    columns(u_g, c_g, 22)
                    dve.drain()
                    dve.wait_ge(S_.silu2_ready, dyn.value(plus=1))
                    dve.tensor_tensor(h2f[:, odd].rearrange("p (c n) -> p c n", c=2), c_a[:, odd], c_g[:], ALU.mult)\
                       .then_inc(S_.h2_ready, 1)
                return hidden

            dve.memset(zeros[:], 0.0)
            dve.memset(stat[:, 1:2], 0.0).then_inc(S_.h1_ready, 2)
            dve.memset(stat[:, 2:3], 0.0).then_inc(S_.h2_ready, 2)
            dve.memset(stat[:, 3:4], 0.0).then_inc(S_.lo_ready, RAW)
            dve.wait_ge(S_.start_loaded, 96)
            dve.tensor_copy(relb, spread(relrow, 2, P)).then_inc(S_.relb_ready, 1)
            dve.wait_ge(S_.bias_loaded, 16 * HA)
            dve.tensor_tensor(bias[:], bias[:], spread(K["winmask"], 1, HA), ALU.add).then_inc(S_.bias_done, 1)
            dve.memset(stat[:, 4:5], 0.0).then_inc(S_.xn_ready, 1)
            for n in range(AHEAD):
                split(Count(n))
            with dve.Fori(0, 2) as L:
                mixer1(L, Count(0).loop(L, LAYER1_UNITS))
                with dve.If(L == 0):
                    feed_forward(Count(MIX1_UNITS), DENSE_STEPS, Count(0), hT_hi, hT_lo, F1, dense_hidden)
                    split_next(Count(LAYER1_UNITS))
                with dve.Else():
                    router()
                    with dve.Fori(0, E_N) as e:
                        at = Count(MOE_UNIT0).loop(e, EXPERT_UNITS)
                        feed_forward(at, MOE_STEPS, Count(DENSE_STEPS).loop(e, MOE_STEPS), hT_hi, hT_lo, F1, expert_hidden(e))
                        split_next(at + EXPERT_UNITS)
                dve.wait_ge(S_.sums_closed, L + 1)
                layer_norm(L * 3 + 3, L * 64 + 64)
            dve.wait_ge(S_.const2_loaded, 16)
            with dve.Fori(0, 2) as L:
                u = Count(BLOCK2_UNIT0).loop(L, LAYER2_UNITS)
                mixer2(L, u)
                at = u + MIX2_UNITS
                feed_forward(at, DENSE_STEPS, Count(0).loop(L, DENSE_STEPS), h2_hi, h2_lo, F2, conv_ffn(L))
                with dve.If(L == 0):
                    split_next(at + STEP * DENSE_STEPS)
                with dve.Else():
                    dve.nop()
                dve.wait_ge(S_.sums_closed, L + 3)
                for t in range(TT):
                    dve.tensor_tensor(x[:, t, :], x[:, t, :], bank(2 * t, D), ALU.add)
                dve.drain()
            rms_norm(11, 80, S_.result_ready)


_OUTS = [((1, S, D), "float32")]


def kernel(**inputs):
    import concourse.bacc as _bacc
    from concourse.bass_utils import run_bass_kernel_spmd as _run

    nc = _bacc.Bacc("TRN2", target_bir_lowering=False, num_devices=1)
    arrays = {name: np.ascontiguousarray(a) for name, a in inputs.items()}
    packed, onehot = constants()
    arrays.update({f"const{i}": a for i, a in enumerate(packed)})
    arrays["onehot"] = onehot
    A = {name: nc.dram_tensor(f"in_{name}", a.shape, mybir.dt.from_np(a.dtype), kind="ExternalInput").ap()
         for name, a in arrays.items()}
    out = nc.dram_tensor("out_0", *_OUTS[0][:1], F32, kind="ExternalOutput").ap()
    build(nc, A, out)
    r = _run(nc, [{f"in_{name}": a for name, a in arrays.items()}], core_ids=[0])
    return r.results[0]["out_0"]
```

```python
from contextlib import ExitStack

import numpy as np

import concourse.bass as bass
from concourse import mybir

ALU = mybir.AluOpType
ACT = mybir.ActivationFunctionType
F32 = mybir.dt.float32
F32R = mybir.dt.float32r
BF16 = mybir.dt.bfloat16
I32 = mybir.dt.int32
AX_X = mybir.AxisListType.X

P = 128
TT = 2
S = TT * P
D = 1024
KC = D // P
HALF = 512
NEG = -1e30
ALPHA = 4.0 ** 0.25
LN_EPS = 1e-5
RMS_EPS = 1e-6

HA, HDA = 8, 64
DA = HA * HDA
HM, HDM = 4, 128
DM = HM * HDM
CONV_K = 4
BUCKETS = 32
D_FF = 2816
E_N, D_FF_E = 8, 3584
CW = 31
POOL_TAPS = range(0, 18)
HB, HDB = 4, 64
GH, GDK, GDV = 4, 64, 128
GCH = 32
NCH = S // GCH
TAU = 16.0

RAW = 6
SPL = 3
AHEAD = 2
UW = KC * 256
STEP = 3
FFC = 256

MIX1_UNITS = 27
DENSE_STEPS = D_FF // FFC
MOE_STEPS = D_FF_E // FFC
LAYER1_UNITS = MIX1_UNITS + STEP * DENSE_STEPS
EXPERT_UNITS = STEP * MOE_STEPS
MIX2_UNITS = 15
LAYER2_UNITS = MIX2_UNITS + STEP * DENSE_STEPS
MOE_UNIT0 = LAYER1_UNITS + MIX1_UNITS
BLOCK2_UNIT0 = 2 * MIX1_UNITS + STEP * DENSE_STEPS + E_N * EXPERT_UNITS
assert LAYER1_UNITS % RAW == 0 and LAYER2_UNITS % RAW == 0 and EXPERT_UNITS % RAW == 0

MERGE_UNITS = (("ga", 0), ("gm", 0), ("a", 0), ("m", 0), ("ga", 1), ("gm", 1), ("ga", 2), ("gm", 2), ("a", 1), ("m", 1),
               ("ga", 3), ("gm", 3))
GATE_BANKS = (6, 7, 4, 5)
WO_UNITS = ((0, 256), (256, 256), (512, 256), (768, 128), (896, 128))
assert 10 + len(MERGE_UNITS) + len(WO_UNITS) == MIX1_UNITS
IN1_COLS = (0, 1, 2, 3, 6, 7, 4, 5, 8, 9)
IN2_COLS = (0, 256, 512, 768, 1024, 1280, 1536, 1792, 2048, 2320, 2576)
GATE_COL = 2304

CONST = {"ident": P, "ones": P}
CONST1 = {"upto": P, "before": P, "tri": P, "iota": P, "wincount": S, "lower": E_N * E_N}
CONST2 = {"glamask": P, "reset": S, "causal": S}
CONST_INIT = {"winmask": S, "flip": P}
GROUPS = (CONST, CONST1, CONST2, CONST_INIT)
BUCKET_W = 384


def constants():
    parts = {}

    def put(name, value):
        parts[name] = np.ascontiguousarray(np.broadcast_to(value, (P, np.shape(value)[-1] if np.ndim(value) else P)),
                                           dtype=np.float32)

    p = np.arange(P)[:, None]
    j = np.arange(P)[None, :]
    dist = p + P - np.arange(S)[None, :]
    count = (((dist >= 0) & (dist <= 128)).astype(np.float32) + ((dist >= 0) & (dist % 4 == 0))
             + ((dist >= 0) & (dist % 16 == 0)))
    put("ident", p == j)
    put("flip", p + j == P - 1)
    put("ones", 1.0)
    put("upto", p <= j)
    put("before", p < j)
    put("tri", np.where(j <= p, 0.0, NEG))
    put("winmask", np.where(count > 0, 0.0, NEG))
    put("wincount", count)
    put("causal", np.where(dist >= 0, 0.0, NEG))
    put("glamask", (p // GCH == j // GCH) & (p <= j))
    put("reset", np.broadcast_to((np.arange(S) % GCH != 0), (P, S)))
    put("iota", np.broadcast_to(j, (P, P)))
    e = np.arange(E_N)
    put("lower", np.broadcast_to((e[None, :] < e[:, None]).reshape(1, -1), (P, E_N * E_N)))
    u = np.maximum(S - 1 - np.arange(BUCKET_W), 0)
    exact = BUCKETS // 2
    log_b = exact + (np.log(np.maximum(u, exact).astype(np.float32) / exact) / np.log(2048 / exact)
                     * (BUCKETS - exact)).astype(np.int32)
    bucket = np.where(u < exact, u, np.minimum(log_b, BUCKETS - 1))
    onehot = (np.arange(BUCKETS)[:, None] == bucket[None, :]).astype(np.float32)
    packed = [np.concatenate([parts[n] for n in g], axis=1) for g in GROUPS]
    assert all(a.shape[1] == sum(g.values()) for a, g in zip(packed, GROUPS))
    return packed, onehot


class Count:

    def __init__(self, const, terms=()):
        self.const, self.terms = const, tuple(terms)

    def __add__(self, n):
        if isinstance(n, Count):
            return Count(self.const + n.const, self.terms + n.terms)
        return Count(self.const + n, self.terms)

    def loop(self, register, step):
        return Count(self.const, self.terms + ((register, step),))

    def value(self, scale=1, plus=0):
        out = self.const * scale + plus
        for register, k in self.terms:
            out = register * (k * scale) + out
        return out

    def turns(self, ring):
        assert all(k % ring == 0 for _, k in self.terms)
        return Count(self.const // ring, [(r, k // ring) for r, k in self.terms])


class Signals(dict):

    def __init__(self, nc, ctx):
        super().__init__()
        self.nc, self.ctx = nc, ctx

    def __getattr__(self, name):
        if name not in self:
            self[name] = self.ctx.enter_context(self.nc.semaphore(name))
        return self[name]


def spread(ap, axis, n):
    ap = ap.unsqueeze(axis)
    shape = list(ap.shape)
    shape[axis] = n
    return ap.to_broadcast(shape)


def build(nc, A, out):
    ctx = ExitStack()
    with ctx:
        def sb(name, shape, dt=F32, scope=None):
            return (scope or ctx).enter_context(nc.sbuf_tensor(name, shape, dt))

        S_ = Signals(nc, ctx)
        bias_rows = nc.dram_tensor("bias_rows", (HA * BUCKET_W,), F32, kind="Internal").ap()

        raw = sb("raw", [P, RAW, UW])
        w_hi = sb("w_hi", [P, SPL, UW], F32R)
        w_lo = sb("w_lo", [P, SPL, UW], F32R)
        x = sb("x", [P, TT, D])
        xT_hi = sb("xT_hi", [P, KC, S], F32R)
        xT_lo = sb("xT_lo", [P, KC, S], F32R)
        yA_hi = sb("yA_hi", [P, 4, S], F32R)
        yA_lo = sb("yA_lo", [P, 4, S], F32R)
        with ExitStack() as shared:
            wqk = sb("wqk", [P, 12, HDM], scope=shared)
        yM_hi = sb("yM_hi", [P, 4, S], F32R)
        yM_lo = sb("yM_lo", [P, 4, S], F32R)
        zeros = sb("zeros", [32, HALF], BF16)
        stat = sb("stat", [P, 192])
        norm_gb = sb("norm_gb", [P, 2, D])

        K = {}

        def const_tile(name, group, scope=None):
            t = sb(name, [P, sum(group.values())], scope=scope)
            at = 0
            for n, w in group.items():
                K[n] = t[:, at:at + w]
                at += w
            return t

        cst = const_tile("cst", CONST)
        ident, ones = K["ident"], K["ones"]

        with ExitStack() as b1:
            cst1 = const_tile("cst1", CONST1, b1)
            bias = sb("bias", [P, HA, S], scope=b1)
            with ExitStack() as m1:
                with ExitStack() as s:
                    xmT = sb("xmT", [P, HM, CONV_K - 1 + S], scope=s)
                    xcT = sb("xcT", [P, HM, S], scope=s)
                bg = sb("bg", [P, 2, D], scope=m1)
                sb("bg_pad", [P, HM * (CONV_K - 1)], scope=m1)
                with ExitStack() as s:
                    qT = sb("qT", [P, HM, S], scope=s)
                    kT = sb("kT", [P, HM, S], scope=s)
                    vA = sb("vA", [P, TT, DM], scope=s)
                merged = sb("merged", [P, TT, D], scope=m1)
                vT = sb("vT_place", [P, HM, S], scope=m1)
                zg = sb("zg", [P, TT, DM], scope=m1)
                gain_m = sb("gain_m", [P, DM], scope=m1)
                cols1 = sb("cols1", [P, 20], scope=m1)
                rows1 = sb("rows1", [20, P], scope=m1)
                w_if = sb("w_if", [P, 12, 8], scope=m1)
                b_if = sb("b_if", [P, 8], scope=m1)
                ht = sb("ht", [P, TT, HM, HDM + 1], scope=m1)
                with ExitStack() as s:
                    sc0 = sb("sc0", [P, HA, P], scope=s)
                    sc1 = sb("sc1", [P, HA, S], scope=s)
                    pT1 = sb("pT1", [P, 2, 3, P], scope=s)
                with ExitStack() as s:
                    bvec = sb("bvec", [HA, BUCKET_W], scope=s)
                    shifted = sb("shifted", [P, HA, S], scope=s)
                    cst_init = const_tile("cst_init", CONST_INIT, s)
                    onehot_sb = sb("onehot_sb", [BUCKETS, BUCKET_W], scope=s)
                with ExitStack() as s:
                    vme = sb("vme", [P, TT, HM, HDM + 1], scope=s)
                    kw = sb("kw", [P, HM, HDM], scope=s)
                    cn = sb("cn", [P, HM, HDM + 1], scope=s)
                    dm = sb("dm", [P, TT, HM, P], scope=s)
                with ExitStack() as s:
                    ga = sb("ga", [P, TT, FFC], scope=s)
                    gm = sb("gm", [P, TT, FFC], scope=s)
            relrow = merged[0:BUCKETS, 1, 0:HA]
            with ExitStack() as s:
                sa = sb("sa", [P, 2, HALF], scope=s)
                hf = sb("hf", [P, 2, HALF], scope=s)
                hT_hi = sb("hT_hi", [P, 2, 2, S], F32R, scope=s)
                hT_lo = sb("hT_lo", [P, 2, 2, S], F32R, scope=s)
                slot_of = sb("slot_of", [P, TT, 2 * E_N + 1], scope=s)
                gate_of = sb("gate_of", [P, TT, 2 * E_N + 1], scope=s)
                pick = sb("pick", [P, TT, P], scope=s)
                pick_gate = sb("pick_gate", [P, TT, P], scope=s)
                put = sb("put", [P, TT, P], scope=s)
                xg_hi = sb("xg_hi", [P, KC, P], F32R, scope=s)
                xg_lo = sb("xg_lo", [P, KC, P], F32R, scope=s)
                eo = sb("eo", [P, D], scope=s)
                y_sum = sb("y_sum", [P, TT, D], scope=s)
                passes_sb = sb("passes_sb", [1, 1], I32, scope=s)
                rw_raw = sb("rw_raw", [P, KC, E_N], scope=s)
                rw_hi = sb("rw_hi", [P, KC, E_N], F32R, scope=s)
                rw_lo = sb("rw_lo", [P, KC, E_N], F32R, scope=s)
                rb = sb("rb", [P, E_N], scope=s)
                lg = sb("lg", [P, TT, E_N], scope=s)
                cmp2 = sb("cmp2", [P, 2, E_N, E_N], scope=s)
                rt = sb("rt", [P, 6, TT, E_N], scope=s)
        with ExitStack() as b2:
            cst2 = const_tile("cst2", CONST2, b2)
            cols2 = sb("cols2", [P, 250], scope=b2)
            with ExitStack() as s:
                rows2 = sb("rows2", [P, 3, P], scope=s)
            egT = sb("egT", [P, 2, S], scope=b2)
            with ExitStack() as s:
                xn = sb("xn", [P, TT, D], scope=s)
            st8 = sb("st8", [P, NCH, 2, GDV], scope=b2)
            with ExitStack() as m2:
                avT = sb("avT", [P, 2, CW - 1 + S], scope=m2)
                agT = sb("agT", [P, 2, S], scope=m2)
                cvT = sb("cvT", [P, 2, S], scope=m2)
                qcT = sb("qcT", [P, 2, S], scope=m2)
                kcT = sb("kcT", [P, 2, S], scope=m2)
                vc = sb("vc", [P, TT, GH * GDV], scope=m2)
                rT = sb("rT", [P, GH, S], scope=m2)
                gT = sb("gT", [16, S], scope=m2)
                wg = sb("wg", [16, 2 * P], scope=m2)
                w16 = sb("w16", [P, KC, 16], scope=m2)
                gain_b = sb("gain_b", [P, HB * HDB], scope=m2)
                laT = sb("laT", [P, 2, S], scope=m2)
                cumT = sb("cumT", [P, 2, S], scope=m2)
                dec = sb("dec", [P, 2, NCH], scope=m2)
                with ExitStack() as s:
                    qbT = sb("qbT", [P, 2, S], scope=s)
                    kbT = sb("kbT", [P, 2, S], scope=s)
                    vb = sb("vb", [P, TT, HB * HDB], scope=s)
                    sb0 = sb("sb0", [P, HB, P], scope=s)
                    sb1 = sb("sb1", [P, HB, S], scope=s)
                    pT2 = sb("pT2", [P, 2, 3, P], scope=s)
                with ExitStack() as s:
                    kd = sb("kd", [P, TT, 2, P], scope=s)
                    atT = sb("atT", [P, GH, TT, P], scope=s)
                    oc = sb("oc", [P, GH, S], scope=s)
                    rv = sb("rv", [P, GH, S], scope=s)
            with ExitStack() as s:
                u_a = sb("u_a", [P, 2, 2, 2 + S], scope=s)
                u_g = sb("u_g", [P, 2, 2, 2 + S], scope=s)
                c_a = sb("c_a", [P, 2, 2, S], scope=s)
                c_g = sb("c_g", [P, 2, S], scope=s)
                h2f = sb("h2f", [P, 2, HALF], scope=s)
                h2_hi = sb("h2_hi", [P, 2, 2, S], F32R, scope=s)
                h2_lo = sb("h2_lo", [P, 2, 2, S], F32R, scope=s)

        tap1 = ht[:].rearrange("p t h e -> p (t h e)")[:, 0:HM * S].rearrange("p (c n) -> p c n", c=HM)
        conv_work = st8[:].rearrange("p n c v -> p (n c v)")
        conv_part = conv_work[:, 0:2 * S].rearrange("p (c n) -> p c n", c=2)
        tap2 = conv_work[:, 2 * S:6 * S].rearrange("p (b c n) -> p b c n", b=2, c=2)
        ps = ctx.enter_context(nc.psum_tensor("ps", [P, 8, HALF], F32))
        raw_landed = [ctx.enter_context(nc.semaphore(f"raw_landed{i}")) for i in range(RAW)]
        block = ctx.enter_context(nc.Block())
        yb, qgT, kgT, kdT, sTm = vb, qcT, laT, cumT, dm
        F1 = {"h": hf, "h_ready": S_.h1_ready, "h_hi_ready": S_.h1_hi_ready, "h_lo_ready": S_.h1_lo_ready}
        F2 = {"h": h2f, "h_ready": S_.h2_ready, "h_hi_ready": S_.h2_hi_ready, "h_lo_ready": S_.h2_lo_ready}

        def bank(b, *shape):
            n = int(np.prod(shape))
            v = ps[:, b:b + -(-n // HALF), :].rearrange("p b n -> p (b n)")[:, 0:n]
            if len(shape) == 2:
                v = v.rearrange("p (a b) -> p a b", a=shape[0])
            if len(shape) == 3:
                v = v.rearrange("p (a b c) -> p a b c", a=shape[0], b=shape[1])
            return v

        def block2_units(passes):
            return Count(MOE_UNIT0, [(passes, E_N * EXPERT_UNITS)])

        @block.sync
        def _(sp):
            def load(u, src, width):
                slot = u.const % RAW
                sp.wait_ge(S_.lo_ready, u.value(plus=1))
                dst = raw[:, slot, 0:width].rearrange("p (k n) -> p k n", k=src.shape[1])
                sp.dma_start(dst, src).then_inc(raw_landed[slot], 16)

            def columns(w, c0, n):
                return w.rearrange("(k p) n -> p k n", p=P)[:, :, c0:c0 + n]

            def feed_forward(u, w13, w2, steps):
                hidden = steps * FFC

                def val(j):
                    return w13[:, 0:hidden].rearrange("(k p) (j n) -> p k j n", p=P, n=FFC)[:, :, j, :]

                def gat(j):
                    return w13[:, hidden:2 * hidden].rearrange("(k p) (j n) -> p k j n", p=P, n=FFC)[:, :, j, :]

                def down(j):
                    return w2.rearrange("(j c p) n -> p j c n", p=P, c=2)[:, j, :, :]

                load(u, val(0), UW)
                load(u + 1, gat(0), UW)
                pairs = (steps - 1) // 2
                with sp.Fori(0, pairs) as i:
                    for q in range(2):
                        at = (u + (2 + STEP * q)).loop(i, 2 * STEP)
                        load(at, val(i * 2 + (1 + q)), UW)
                        load(at + 1, gat(i * 2 + (1 + q)), UW)
                        load(at + 2, down(i * 2 + q), UW)
                for j in range(2 * pairs + 1, steps):
                    at = u + (2 + STEP * (j - 1))
                    load(at, val(j), UW)
                    load(at + 1, gat(j), UW)
                    load(at + 2, down(j - 1), UW)
                load(u + (STEP * steps - 1), down(steps - 1), UW)

            sp.dma_start(cst[:], A["const0"]).then_inc(S_.ident_loaded, 16)
            sp.dma_start(onehot_sb[:], A["onehot"]).then_inc(S_.table_loaded, 16)
            sp.dma_start(relrow, A["rel_bias"]).then_inc(S_.table_loaded, 16)
            sp.dma_start(x[:], A["x"][0].rearrange("(t p) d -> p t d", p=P)).then_inc(S_.x_loaded, 16)
            sp.dma_start(cst_init[:], A["const3"]).then_inc(S_.start_loaded, 16)
            sp.dma_start(cst1[:], A["const1"]).then_inc(S_.start_loaded, 16)

            with sp.Fori(0, 2) as L:
                u = Count(0).loop(L, LAYER1_UNITS)
                w_in, w_gate = A["w_in"][L], A["w_gate"][L]
                for n, c in enumerate(IN1_COLS):
                    load(u + n, columns(w_in, 256 * c, 256), UW)
                br = {"a": A["w_br_a"][L], "m": A["w_br_m"][L]}
                for m, (kind, c) in enumerate(MERGE_UNITS):
                    if kind in br:
                        load(u + (10 + m), columns(br[kind], HALF * c, HALF), UW)
                    else:
                        load(u + (10 + m), columns(w_gate, D * (kind == "gm") + 256 * c, 256), UW)
                for n, (c0, w) in enumerate(WO_UNITS):
                    load(u + (22 + n), columns(A["w_o"][L], c0, w), KC * w)
                with sp.If(L == 0):
                    feed_forward(Count(MIX1_UNITS), A["ffn_w13"][0], A["ffn_w2"][0], DENSE_STEPS)
                with sp.Else():
                    with sp.Fori(0, E_N) as e:
                        feed_forward(Count(MOE_UNIT0).loop(e, EXPERT_UNITS), A["exp_w13"][0][e], A["exp_w2"][0][e],
                                     MOE_STEPS)
            sp.wait_ge(S_.passes_ready, 1)
            passes = sp.value_load(passes_sb[0:1, 0:1], min_val=1, max_val=2)
            with sp.If(passes == 2):
                with sp.Fori(0, E_N) as e:
                    feed_forward(Count(MOE_UNIT0 + E_N * EXPERT_UNITS).loop(e, EXPERT_UNITS), A["exp_w13"][0][e],
                                 A["exp_w2"][0][e], MOE_STEPS)
            with sp.Else():
                sp.nop()
            with sp.Fori(0, 2) as L:
                u = block2_units(passes).loop(L, LAYER2_UNITS)
                w_in = A["w_in_2"][L]
                for n, c0 in enumerate(IN2_COLS):
                    load(u + n, columns(w_in, c0, 256), UW)
                for n in range(4):
                    load(u + (11 + n), columns(A["w_out_2"][L], 256 * n, 256), UW)
                feed_forward(u + MIX2_UNITS, A["ffn_w_up_2"][L], A["ffn_w_down_2"][L], DENSE_STEPS)
            sp.wait_ge(S_.result_ready, 1)
            sp.dma_start(out[0].rearrange("(t p) d -> p t d", p=P), xn[:]).then_inc(S_.result_stored, 16)
            sp.wait_ge(S_.result_stored, 16)

        @block.gpsimd
        def _(pool):
            def over(v, n):
                return v.partition_broadcast(P)

            pool.wait_ge(S_.bvec_ready, 1)
            pool.dma_start(bias_rows.rearrange("(h n) -> h n", h=HA), bvec[:]).then_inc(S_.bias_stored, 16)
            pool.wait_ge(S_.bias_stored, 16)
            pool.dma_start(shifted[:], bass.AP(tensor=bias_rows.tensor, offset=0, ap=[[1, P], [BUCKET_W, HA], [1, S]]))\
                .then_inc(S_.bias_loaded, 16)

            with pool.Fori(0, 2) as L:
                pool.wait_ge(S_.xn_ready, L * 2 + 1)
                pool.sem_inc(S_.pool_passed, 1)
                pool.dma_start(rows1[0:16, :], A["conv_w"][L].rearrange("k (c p) -> (k c) p", p=P)).then_inc(S_.p1_loaded, 16)
                pool.dma_start(rows1[16:20, :], A["conv_b"][L].rearrange("(c p) -> c p", p=P)).then_inc(S_.p1_loaded, 16)
                pool.dma_start(wqk[:, 0:8, :], A["w_qk_m"][L].rearrange("a h d e -> d (a h) e")).then_inc(S_.p1_loaded, 16)
                pool.dma_start(wqk[:, 8:12, :], A["w_v_m"][L].rearrange("h d e -> d h e")).then_inc(S_.p1_loaded, 16)
                pool.dma_start(w_if[:], A["w_if"][L].rearrange("(c p) g -> p c g", p=P)).then_inc(S_.p1_loaded, 16)
                pool.dma_start(b_if[:], over(A["b_if"][L], 8)).then_inc(S_.p1_loaded, 16)
                pool.dma_start(gain_m[:], over(A["m_norm_g"][L], DM)).then_inc(S_.p1_loaded, 16)
                pool.dma_start(norm_gb[:, 0, :], over(A["ln_g"][L, 0], D)).then_inc(S_.norm_loaded, 16)
                pool.dma_start(norm_gb[:, 1, :], over(A["ln_b"][L, 0], D)).then_inc(S_.norm_loaded, 16)
                pool.memset(xmT[:, :, 0:CONV_K - 1], 0.0)
                pool.drain()
                pool.wait_ge(S_.proj1_out, L * 10 + 6)
                pool.sem_inc(S_.pool_passed, 1)
                pool.wait_ge(S_.p1_cols_ready, L + 1)
                pool.sem_inc(S_.pool_passed, 1)
                for c in range(4):
                    pool.tensor_scalar(xcT[:, c, :], xmT[:, c, 0:S], cols1[:, c:c + 1], None, ALU.mult)
                for k in range(1, CONV_K):
                    for c in range(4):
                        pool.tensor_scalar(tap1[:, c, :], xmT[:, c, k:k + S], cols1[:, 4 * k + c:4 * k + c + 1], None, ALU.mult)
                    pool.drain()
                    m = pool.tensor_tensor(xcT[:], xcT[:], tap1, ALU.add)
                    if k < CONV_K - 1:
                        pool.drain()
                m.then_inc(S_.conv1_done, 1)
                pool.wait_ge(S_.v_m_psum, L + 1)
                pool.sem_inc(S_.pool_passed, 1)
                pool.dma_start(bg[:], over(A["b_gate"][L], 2 * D).rearrange("p (a d) -> p a d", a=2)).then_inc(S_.bg_loaded, 16)
                pool.wait_ge(S_.xn_ready, L * 2 + 2)
                pool.sem_inc(S_.pool_passed, 1)
                pool.dma_start(norm_gb[:, 0, :], over(A["ln_g"][L, 1], D)).then_inc(S_.norm_loaded, 16)
                pool.dma_start(norm_gb[:, 1, :], over(A["ln_b"][L, 1], D)).then_inc(S_.norm_loaded, 16)
                with pool.If(L == 0):
                    pool.nop()
                with pool.Else():
                    pool.dma_start(rw_raw[:], A["router_w"][0].rearrange("(k p) e -> p k e", p=P)).then_inc(S_.router_loaded, 16)
                    pool.dma_start(rb[:], over(A["router_b"][0], E_N)).then_inc(S_.router_loaded, 16)
            pool.wait_ge(S_.xn_ready, 5)
            pool.dma_start(cst2[:], A["const2"]).then_inc(S_.const2_loaded, 16)
            with pool.Fori(0, 2) as L:
                pool.wait_ge(S_.xn_ready, L * 2 + 5)
                pool.sem_inc(S_.pool_passed, 1)
                pool.dma_start(norm_gb[:, 0, :], over(A["norm_mix_g_2"][L], D)).then_inc(S_.norm2_loaded, 16)
                pool.wait_ge(S_.xn_ready, L * 2 + 6)
                pool.sem_inc(S_.pool_passed, 1)
                pool.dma_start(norm_gb[:, 0, :], over(A["norm_ffn_g_2"][L], D)).then_inc(S_.norm2_loaded, 16)
                p2 = lambda dst, src: pool.dma_start(dst, src).then_inc(S_.p2_loaded, 16)
                p2(rows2[0:62, 0, :], A["conv_w_2"][L].rearrange("k (c p) -> (k c) p", p=P))
                p2(rows2[62:64, 0, :], A["conv_b_2"][L].rearrange("(c p) -> c p", p=P))
                p2(rows2[64:66, 0, :], A["conv_ln_g_2"][L].rearrange("(c p) -> c p", p=P))
                p2(rows2[66:68, 0, :], A["conv_ln_b_2"][L].rearrange("(c p) -> c p", p=P))
                p2(rows2[68:70, 0, :], A["gla_gate_b_2"][L].rearrange("(c p) -> c p", p=P))
                p2(rows2[70:74, 0, :], A["gla_out_g_2"][L].rearrange("(c p) -> c p", p=P))
                p2(rows2[0:88, 1, :], A["ffn_conv_w_2"][L, 0:2].rearrange("k (c p) -> (k c) p", p=P))
                p2(rows2[0:44, 2, :], A["ffn_conv_w_2"][L, 2].rearrange("(c p) -> c p", p=P))
                p2(rows2[44:88, 2, :], A["ffn_conv_b_2"][L].rearrange("(c p) -> c p", p=P))
                p2(wg[:], A["gla_gate_w_2"][L])
                p2(gain_b[:], over(A["moba_out_g_2"][L], HB * HDB))
                p2(w16[:], A["w_in_2"][L].rearrange("(k p) n -> p k n", p=P)[:, :, GATE_COL:GATE_COL + 16])
                pool.wait_ge(S_.glu_ready, L + 1)
                pool.sem_inc(S_.pool_passed, 1)
                pool.wait_ge(S_.p2_cols_ready, L + 1)
                pool.sem_inc(S_.pool_passed, 1)
                def tap(k, dst):
                    for c in range(2):
                        pool.tensor_scalar(dst[:, c, :], avT[:, c, k:k + S], cols2[:, 2 * k + c:2 * k + c + 1], None, ALU.mult)

                tap(POOL_TAPS[0], conv_part)
                tap(POOL_TAPS[1], tap2[:, 1])
                for k in POOL_TAPS[1:]:
                    pool.drain()
                    m = pool.tensor_tensor(conv_part, conv_part, tap2[:, k % 2], ALU.add)
                    if k + 1 in POOL_TAPS:
                        tap(k + 1, tap2[:, (k + 1) % 2])
                m.then_inc(S_.conv_part_ready, 1)
            pool.wait_ge(S_.xn_ready, 9)
            pool.dma_start(norm_gb[:, 0, :], over(A["final_g_2"], D)).then_inc(S_.norm2_loaded, 16)

        @block.tensor
        def _(pe):
            def unit_parts(u, k, n):
                pe.wait_ge(S_.lo_ready, u.value(plus=RAW + 1))
                slot = u.const % SPL
                return [w[:, slot, 0:k * n].rearrange("p (k n) -> p k n", k=k) for w in (w_hi, w_lo)]

            def product(out, lhs, rhs, first, last):
                pe.matmul(out, lhs[0], rhs[0], start=first, stop=False)
                pe.matmul(out, lhs[0], rhs[1], start=False, stop=False)
                return pe.matmul(out, lhs[1], rhs[0], start=False, stop=last)

            def project_T(u, b, lhsT=None):
                w = unit_parts(u, KC, 256)
                o = bank(b, 2, S)
                for c in range(2):
                    for k in range(KC):
                        m = product(o[:, c, :], [v[:, k, c * P:(c + 1) * P] for v in w],
                                    [v[:, k, :] for v in (xT_hi, xT_lo)], k == 0, k == KC - 1)
                m.then_inc(S_.unit_used, 1)

            def project_tok(u, outs, chunks, n):
                w = unit_parts(u, len(chunks), n)
                for t in range(TT):
                    for k, c in enumerate(chunks):
                        m = product(outs[t], [v[:, t * P:(t + 1) * P] for v in c], [v[:, k, :] for v in w],
                                    k == 0, k == len(chunks) - 1)
                m.then_inc(S_.unit_used, 1)

            x_chunks = [(xT_hi[:, k, :], xT_lo[:, k, :]) for k in range(KC)]
            yA_chunks = [(yA_hi[:, k, :], yA_lo[:, k, :]) for k in range(4)]
            yM_chunks = [(yM_hi[:, k, :], yM_lo[:, k, :]) for k in range(4)]

            def transpose_x(src, count):
                for b in range(4):
                    o = bank(4 + b, 2, TT, P)
                    for c in range(2):
                        for t in range(TT):
                            m = pe.transpose(o[:, c, t, :], src[:, t, (2 * b + c) * P:(2 * b + c + 1) * P], ident)
                    m.then_inc(S_.xT_psum, 1)
                pe.wait_ge(S_.xT_lo_ready, count)

            def open_sums():
                for b in range(4):
                    pe.matmul(ps[:, b, :], zeros[:, 0:P], zeros[:], start=True, stop=False)

            def close_sums():
                for b in range(4):
                    m = pe.matmul(ps[:, b, :], zeros[:, 0:P], zeros[:], start=False, stop=True)
                m.then_inc(S_.sums_closed, 1)

            def feed_forward(u, steps, count, hh, hl, sig):
                def up(at, b):
                    project_T(at, b)

                def step_up(j, at, odd, dyn):
                    pe.wait_ge(sig["h_ready"], dyn.value(plus=1))
                    up(at, 4 + 2 * odd)
                    up(at + 1, 5 + 2 * odd)

                def down(at, odd, dyn):
                    pe.wait_ge(sig["h_lo_ready"], dyn.value(plus=1))
                    w = unit_parts(at, 2, D)
                    for c in range(2):
                        for t in range(TT):
                            for h in range(2):
                                m = pe_sum(ps[:, 2 * t + h, :], [v[:, odd, c, t * P:(t + 1) * P] for v in (hh, hl)],
                                           [v[:, c, h * HALF:(h + 1) * HALF] for v in w])
                    m.then_inc(S_.unit_used, 1)

                def pe_sum(o, lhs, rhs):
                    return product(o, lhs, rhs, False, False)

                step_up(0, u, 0, count)
                pairs = (steps - 1) // 2
                with pe.Fori(0, pairs) as i:
                    for q in range(2):
                        at = (u + (2 + STEP * q)).loop(i, 2 * STEP)
                        j = (count + (1 + q)).loop(i, 2)
                        step_up(None, at, (1 + q) % 2, j)
                        down(at + 2, q, j + -1)
                for j in range(2 * pairs + 1, steps):
                    at = u + (2 + STEP * (j - 1))
                    step_up(j, at, j % 2, count + j)
                    down(at + 2, (j - 1) % 2, count + (j - 1))
                down(u + (STEP * steps - 1), (steps - 1) % 2, count + (steps - 1))

            def attention_out(L, heads, sc, pT, v, names):
                s_prob, s_psum, s_ready, s_pv = names
                w = 64

                def blocks(h):
                    o = bank(6 + h % 2, 3, P)
                    if h >= 2:
                        pe.wait_ge(s_ready, L * heads + (h - 1))
                    pe.transpose(o[:, 0, :], sc[0][:, h, :], ident)
                    pe.transpose(o[:, 1, :], sc[1][:, h, 0:P], ident)
                    pe.transpose(o[:, 2, :], sc[1][:, h, P:S], ident).then_inc(s_psum, 1)

                def values(h):
                    pe.wait_ge(s_ready, L * heads + (h + 1))
                    b, cols = pT[:, h % 2], slice(h * w, (h + 1) * w)
                    pe.matmul(ps[:, 4, cols], b[:, 0, :], v[:, 0, cols], start=True, stop=True)
                    pe.matmul(ps[:, 5, cols], b[:, 1, :], v[:, 0, cols], start=True, stop=False)
                    pe.matmul(ps[:, 5, cols], b[:, 2, :], v[:, 1, cols], start=False, stop=True).then_inc(s_pv, 1)

                pe.wait_ge(s_prob, L * 2 + 2)
                for h in range(heads):
                    blocks(h)
                    if h:
                        values(h - 1)
                values(heads - 1)

            def to_T(src, done, first):
                for b in range(2):
                    o = bank(first + b, 2, TT, P)
                    for c in range(2):
                        for t in range(TT):
                            m = pe.transpose(o[:, c, t, :], src(t, 2 * b + c), ident)
                    m.then_inc(done, 1)

            def mixer1(L, u):
                pe.wait_ge(S_.xn_ready, L * 2 + 1)
                transpose_x(x, L * 12 + 4)
                def bank_free(n):
                    if n >= 4:
                        pe.wait_ge(S_.proj1_out, L * 10 + (n - 3))

                def scores(tile, h, b, col):
                    rows = slice(64 * (h % 2), 64 * (h % 2) + 64)
                    n = P * (tile + 1)
                    return pe.matmul(ps[:, b, col:col + n], qT[rows, h // 2, tile * P:(tile + 1) * P],
                                     kT[rows, h // 2, 0:n], start=True, stop=True)

                for n in range(4):
                    bank_free(n)
                    project_T(u + n, n % 4)
                with pe.If(L == 0):
                    pe.wait_ge(S_.start_loaded, 32)
                    pe.wait_ge(S_.bias_loaded, 16)
                    for h in range(HA):
                        m = pe.matmul(bank(4, HA, S)[:, h, :], K["flip"], shifted[:, h, :], start=True, stop=True)
                    m.then_inc(S_.bias_psum, 1)
                with pe.Else():
                    pe.nop()
                for n in (4, 5):
                    bank_free(n)
                    project_T(u + n, n % 4)
                pe.wait_ge(S_.bias_done, 1)
                pe.wait_ge(S_.p1_loaded, L * 112 + 112)
                pe.sem_inc(S_.pe_passed, 1)
                pe.transpose(ps[:, 7, 0:20], rows1[:], ident[0:20, 0:20]).then_inc(S_.p1_cols_psum, 1)
                pe.wait_ge(S_.proj1_out, L * 10 + 4)
                for h in range(HA):
                    m = scores(0, h, 4 + h % 2, (h // 2) * P)
                m.then_inc(S_.scores1, 1)
                pe.wait_ge(S_.p1_cols_ready, L + 1)
                for h in range(4):
                    m = scores(1, h, 6 + h % 2, (h // 2) * S)
                m.then_inc(S_.scores1, 1)
                for n in (6, 7):
                    bank_free(n)
                    project_tok(u + n, [bank(n % 4, TT, 256)[:, t, :] for t in range(TT)], x_chunks, 256)
                pe.wait_ge(S_.scores1_in, L * 3 + 1)
                for h in range(4, 8):
                    m = scores(1, h, 4 + h % 2, (h // 2 - 2) * S)
                m.then_inc(S_.scores1, 1)
                for n in (8, 9):
                    bank_free(n)
                    project_tok(u + n, [bank(n % 4, TT, 256)[:, t, :] for t in range(TT)], x_chunks, 256)
                pe.wait_ge(S_.xc_ready, L + 1)
                pe.wait_ge(S_.proj1_out, L * 10 + 10)
                for i in range(2):
                    for h in range(HM):
                        m = pe.matmul(bank(2 * i + h // 2, 2, S)[:, h % 2, :], wqk[:, 4 * i + h, :], xcT[:, h, :],
                                      start=True, stop=True)
                m.then_inc(S_.qk_m_psum, 1)
                attention_out(L, HA, (sc0, sc1), pT1, vA, (S_.prob1, S_.pT1_psum, S_.pT1_ready, S_.pv1))
                pe.wait_ge(S_.ya1_ready, L + 1)
                pe.wait_ge(S_.pT1_ready, L * HA + HA)
                ya = ht[:].rearrange("p t h e -> p (t h e)")[:, 0:TT * DM].rearrange("p (t n) -> p t n", t=TT)
                to_T(lambda t, c: ya[:, t, c * P:(c + 1) * P], S_.yT_psum, 6)
                pe.wait_ge(S_.qk_m_ready, L + 1)
                for h in range(HM):
                    pe.matmul(bank(h // 2, 2, S)[:, h % 2, :], wqk[:, 8 + h, :], xmT[:, h, CONV_K - 1:], start=True, stop=True)
                for t in range(TT):
                    for h in range(HM):
                        at = CONV_K - 1 + t * P
                        pe.matmul(ps[:, 2 + t, h * P:(h + 1) * P], xmT[:, h, at:at + P], wqk[:, 8 + h, :],
                                  start=True, stop=True)
                for h in range(HM):
                    m = pe.matmul(ps[:, 4, h * P:(h + 1) * P], xcT[:, h, 0:P], wqk[:, 4 + h, :], start=True, stop=True)
                m.then_inc(S_.v_m_psum, 1)
                pe.wait_ge(S_.v_m_ready, L + 1)
                for t in range(TT):
                    for c in range(12):
                        src = (qT, kT, vT)[c // 4]
                        m = pe.matmul(ps[:, 5, 8 * t:8 * t + 8], src[:, c % 4, t * P:(t + 1) * P], w_if[:, c, :],
                                      start=c == 0, stop=c == 11)
                m.then_inc(S_.gates_psum, 1)
                for t in range(TT):
                    for h in range(HM):
                        pe.matmul(ps[:, t, h * P:(h + 1) * P], qT[:, h, t * P:(t + 1) * P], kT[:, h, t * P:(t + 1) * P],
                                  start=True, stop=True)
                pe.wait_ge(S_.logf_ready, L + 1)
                for t in range(TT):
                    lf = stat[:, 16 + 4 * t:20 + 4 * t]
                    pe.matmul(ps[:, 5, 32 + 4 * t:36 + 4 * t], K["upto"], lf, start=True, stop=True)
                    m = pe.matmul(ps[:, 5, 40 + 4 * t:44 + 4 * t], ones, lf, start=True, stop=True)
                m.then_inc(S_.cum_psum, 1)
                pe.wait_ge(S_.diag_ready, L + 1)
                dg = ht[:].rearrange("p t h e -> p (t h e)")[:, 0:TT * DM].rearrange("p (t n) -> p t n", t=TT)
                pe.wait_ge(S_.yT_lo_ready, L * 4 + 2)
                for t in range(TT):
                    m = pe.matmul(ps[:, 6 + t, :], ones, dg[:, t, :], start=True, stop=True)
                m.then_inc(S_.rowr_psum, 1)
                pe.wait_ge(S_.s_ready, L + 1)
                for t in range(TT):
                    for h in range(HM):
                        m = pe.transpose(ps[:, 6 + t, h * P:(h + 1) * P], dm[:, t, h, :], ident)
                m.then_inc(S_.sT_psum, 1)
                pe.wait_ge(S_.kw_ready, L + 1)
                E1 = HDM + 1
                for h in range(HM):
                    m = pe.matmul(ps[:, 2 + h // 2, (h % 2) * E1:(h % 2 + 1) * E1], kw[:, h, :], vme[:, 0, h, :],
                                  start=True, stop=True)
                m.then_inc(S_.cn_psum, 1)
                pe.wait_ge(S_.sT_ready, L + 1)
                for t in range(TT):
                    for h in range(HM):
                        pe.matmul(ps[:, 4 * t + h // 2, (h % 2) * E1:(h % 2 + 1) * E1], sTm[:, t, h, :], vme[:, t, h, :],
                                  start=True, stop=True)
                pe.wait_ge(S_.cn_ready, L + 1)
                for h in range(HM):
                    m = pe.matmul(ps[:, 2 + h // 2, (h % 2) * E1:(h % 2 + 1) * E1], qT[:, h, P:S], cn[:, h, :],
                                  start=True, stop=True)
                m.then_inc(S_.num_psum, 1)
                gates = 0
                for m_, (kind, c) in enumerate(MERGE_UNITS):
                    at = u + (10 + m_)
                    if m_ == 2:
                        pe.wait_ge(S_.ym_ready, L + 1)
                        to_T(lambda t, c: ht[:, t, c, 0:P], S_.yT_psum, 4)
                        pe.wait_ge(S_.yT_lo_ready, L * 4 + 4)
                    if kind in "am":
                        if c:
                            pe.wait_ge(S_.merged_ready, L * 4 + 2)
                        b = 0 if kind == "a" else 2
                        project_tok(at, [ps[:, b, :], ps[:, b + 1, :]], yA_chunks if kind == "a" else yM_chunks, HALF)
                    else:
                        if gates >= 4:
                            pe.wait_ge(S_.gate_lin, L * 8 + (gates - 3))
                        b = GATE_BANKS[gates % 4]
                        project_tok(at, [bank(b, TT, FFC)[:, t, :] for t in range(TT)], x_chunks, FFC)
                        gates += 1
                pe.wait_ge(S_.merged_ready, L * 4 + 4)
                transpose_x(merged, L * 12 + 8)
                for n, (c0, w) in enumerate(WO_UNITS):
                    o = [ps[:, 2 * t + c0 // HALF, c0 % HALF:c0 % HALF + w] for t in range(TT)]
                    project_tok(u + (22 + n), o, x_chunks, w)
                pe.wait_ge(S_.xn_ready, L * 2 + 2)
                transpose_x(x, L * 12 + 12)

            def router():
                pe.wait_ge(S_.rw_split, 1)
                for t in range(TT):
                    for k in range(KC):
                        m = product(ps[:, 4, 8 * t:8 * t + 8], [v[:, k, t * P:(t + 1) * P] for v in (xT_hi, xT_lo)],
                                    [v[:, k, :] for v in (rw_hi, rw_lo)], k == 0, k == KC - 1)
                m.then_inc(S_.logits_psum, 1)
                pe.wait_ge(S_.chosen_ready, 1)
                chosen = rt[:, 1]
                pe.matmul(ps[:, 5, 0:8], K["before"], chosen[:, 0], start=True, stop=True)
                pe.matmul(ps[:, 5, 8:16], K["before"], chosen[:, 1], start=True, stop=False)
                pe.matmul(ps[:, 5, 8:16], ones, chosen[:, 0], start=False, stop=True)
                pe.matmul(ps[:, 5, 16:24], ones, chosen[:, 0], start=True, stop=False)
                pe.matmul(ps[:, 5, 16:24], ones, chosen[:, 1], start=False, stop=True).then_inc(S_.slots_psum, 1)

            def experts(passes):
                def dispatch(n):
                    pe.wait_ge(S_.pick_ready, n.value(plus=1))
                    for k in range(KC):
                        for t in range(TT):
                            m = pe.matmul(bank(0, KC, P)[:, k, :], x[:, t, k * P:(k + 1) * P], pick[:, t, :],
                                          start=t == 0, stop=t == TT - 1)
                    m.then_inc(S_.xg_psum, 1)

                def up(at, half):
                    w = unit_parts(at, KC, FFC)
                    for k in range(KC):
                        m = product(ps[:, (6, 2)[half], 0:FFC], [v[:, k, :] for v in (xg_hi, xg_lo)],
                                    [v[:, k, :] for v in w], k == 0, k == KC - 1)
                    m.then_inc(S_.unit_used, 1)

                def hidden_T(n):
                    pe.wait_ge(S_.he_ready, n.value(plus=1))
                    for c in range(2):
                        m = pe.transpose(ps[:, 7, c * P:(c + 1) * P], hf[:, 0, c * P:(c + 1) * P], ident)
                    m.then_inc(S_.heT_psum, 1)

                def down(at, n):
                    pe.wait_ge(S_.heT_lo_ready, n.value(plus=1))
                    w = unit_parts(at, 2, D)
                    for c in range(2):
                        for h in range(2):
                            m = product(ps[:, 4 + h, :], [v[:, 0, 0, c * P:(c + 1) * P] for v in (hT_hi, hT_lo)],
                                        [v[:, c, h * HALF:(h + 1) * HALF] for v in w], False, False)
                    m.then_inc(S_.unit_used, 1)

                def step(at, n):
                    pe.wait_ge(S_.silue_ready, n.value(plus=1))
                    up(at, 0)
                    hidden_T(n + -1)
                    up(at + 1, 1)

                dispatch(Count(0))
                pe.wait_ge(S_.xg_lo_ready, 1)
                with pe.Fori(0, passes * E_N) as e:
                    item = Count(0).loop(e, 1)
                    u, n = Count(MOE_UNIT0).loop(e, EXPERT_UNITS), Count(0).loop(e, MOE_STEPS)
                    for t in range(TT):
                        m = pe.transpose(ps[:, 7, S + t * P:S + (t + 1) * P], pick_gate[:, t, :], ident)
                    m.then_inc(S_.put_psum, 1)
                    pe.wait_ge(S_.xg_lo_ready, e + 1)
                    for h in range(2):
                        pe.matmul(ps[:, 4 + h, :], zeros[:, 0:P], zeros[:], start=True, stop=False)
                    pe.wait_ge(S_.silue_ready, n.value(plus=1))
                    up(u, 0)
                    pe.wait_ge(S_.y_added, e + 1)
                    up(u + 1, 1)
                    pairs = (MOE_STEPS - 1) // 2
                    with pe.Fori(0, pairs) as i:
                        for q in range(2):
                            at = (u + (2 + STEP * q)).loop(i, 2 * STEP)
                            j = (n + (1 + q)).loop(i, 2)
                            step(at, j)
                            down(at + 2, j + -1)
                    assert 2 * pairs + 2 == MOE_STEPS
                    at, j = u + (2 + STEP * 2 * pairs), n + (MOE_STEPS - 1)
                    step(at, j)
                    dispatch(item + 1)
                    down(at + 2, j + -1)
                    hidden_T(j)
                    down(at + 3, j)
                    for h in range(2):
                        m = pe.matmul(ps[:, 4 + h, :], zeros[:, 0:P], zeros[:], start=False, stop=True)
                    m.then_inc(S_.eo_psum, 1)
                    pe.wait_ge(S_.eo_ready, e * 2 + 2)
                    pe.wait_ge(S_.put_ready, e + 1)
                    for t in range(TT):
                        for h in range(2):
                            m = pe.matmul(ps[:, 2 * t + h, :], put[:, t, :], eo[:, h * HALF:(h + 1) * HALF],
                                          start=True, stop=True)
                    m.then_inc(S_.y_psum, 1)

            def mixer2(L, u):
                pe.wait_ge(S_.xn_ready, L * 2 + 6)
                transpose_x(xn, L * 8 + 28)
                def bank_free(n):
                    if n >= 4:
                        pe.wait_ge(S_.proj2_out, L * 11 + (n - 3))

                def tok(n):
                    bank_free(n)
                    project_tok(u + n, [bank(n % 4, TT, 256)[:, t, :] for t in range(TT)], x_chunks, 256)

                def T(n):
                    bank_free(n)
                    project_T(u + n, n % 4)

                T(0)
                T(1)
                pe.wait_ge(S_.p2_loaded, L * 192 + 192)
                pe.sem_inc(S_.pe_passed, 1)
                pe.transpose(ps[:, 7, 0:74], rows2[0:74, 0, :], ident[0:74, 0:74])
                pe.transpose(ps[:, 7, 74:162], rows2[0:88, 1, :], ident[0:88, 0:88])
                pe.transpose(ps[:, 7, 162:250], rows2[0:88, 2, :], ident[0:88, 0:88]).then_inc(S_.p2_cols_psum, 1)
                for i, part in enumerate((xT_hi, xT_lo)):
                    for k in range(KC):
                        m = pe.matmul(ps[0:16, 6, 0:S], w16[:, k, :], part[:, k, :].bitcast(F32),
                                      start=i == 0 and k == 0, stop=i == 1 and k == KC - 1)
                m.then_inc(S_.g16_psum, 1)
                T(2)
                T(3)
                tok(4)
                pe.wait_ge(S_.proj2_out, L * 11 + 4)

                def scores(tile, h, b, col):
                    rows = slice(64 * (h % 2), 64 * (h % 2) + 64)
                    n = P * (tile + 1)
                    return pe.matmul(ps[:, b, col:col + n], qbT[rows, h // 2, tile * P:(tile + 1) * P],
                                     kbT[rows, h // 2, 0:n], start=True, stop=True)

                for h in range(HB):
                    m = scores(0, h, 4 + h % 2, (h // 2) * P)
                m.then_inc(S_.scores2, 1)
                pe.wait_ge(S_.g16_ready, L + 1)
                pe.wait_ge(S_.p2_cols_ready, L + 1)
                for h in range(HB):
                    m = scores(1, h, 6 + h % 2, (h // 2) * S)
                m.then_inc(S_.scores2, 1)
                T(5)
                pe.wait_ge(S_.scores2_in, L + 1)
                for c in range(2):
                    m = pe.matmul(ps[:, 7, c * S:(c + 1) * S], wg[:, c * P:(c + 1) * P], gT[:], start=True, stop=True)
                m.then_inc(S_.glog_psum, 1)
                T(6)
                tok(7)
                tok(8)
                T(9)
                T(10)
                pe.wait_ge(S_.glog_in, L + 1)
                attention_out(L, HB, (sb0, sb1), pT2, vb, (S_.prob2, S_.pT2_psum, S_.pT2_ready, S_.pv2))
                pe.wait_ge(S_.qkg_ready, L + 1)
                pe.wait_ge(S_.proj2_out, L * 11 + 11)
                for t in range(TT):
                    for c in range(2):
                        m = pe.transpose(ps[:, 0, (2 * t + c) * P:(2 * t + c + 1) * P], kdT[:, c, t * P:(t + 1) * P], ident)
                m.then_inc(S_.kd_psum, 1)
                for h in range(GH):
                    rows = slice(64 * (h % 2), 64 * (h % 2) + 64)
                    for t in range(TT):
                        m = pe.matmul(bank(1 + h % 2, 2, TT, P)[:, h // 2, t, :], kgT[rows, h // 2, t * P:(t + 1) * P],
                                      qgT[rows, h // 2, t * P:(t + 1) * P], start=True, stop=True)
                m.then_inc(S_.at_psum, 1)
                pe.wait_ge(S_.yb_ready, L + 1)
                pe.wait_ge(S_.pT2_ready, L * HB + HB)
                o = bank(6, 2, TT, P)
                for c in range(2):
                    for t in range(TT):
                        m = pe.transpose(o[:, c, t, :], yb[:, t, c * P:(c + 1) * P], ident)
                m.then_inc(S_.yb_psum, 1)
                pe.wait_ge(S_.conv_ready, L + 1)
                for c in range(2):
                    m = pe.matmul(ps[:, 7, 0:S], ones, cvT[:, c, :], start=c == 0, stop=c == 1)
                m.then_inc(S_.csum_psum, 1)
                pe.wait_ge(S_.kd_ready, L + 1)
                for n in range(NCH - 1):
                    if n >= 2:
                        pe.wait_ge(S_.state_ready, L * (NCH - 1) + (n - 1))
                    rows = slice(GCH * (n % 4), GCH * (n % 4) + GCH)
                    for c in range(2):
                        m = pe.matmul(bank(3 + n % 2, 2, S)[:, c, :], kd[rows, n // 4, c, :],
                                      vc[rows, n // 4, c * 2 * GDV:(c + 1) * 2 * GDV], start=True, stop=True)
                    m.then_inc(S_.ds_psum, 1)
                pe.wait_ge(S_.csq_ready, L + 1)
                for c in range(2):
                    m = pe.matmul(ps[:, 7, S:2 * S], ones, agT[:, c, :], start=c == 0, stop=c == 1)
                m.then_inc(S_.cvar_psum, 1)
                pe.wait_ge(S_.at_ready, L + 1)
                pe.wait_ge(S_.state_ready, L * (NCH - 1) + NCH - 1)
                pe.wait_ge(S_.yT2_lo_ready, L * 4 + 1)
                for h in range(GH):
                    o = bank(5 + h % 2, 2, S)[:, h // 2, :]
                    rows = slice(64 * (h % 2), 64 * (h % 2) + 64)
                    for t in range(TT):
                        pe.matmul(o[:, t * P:(t + 1) * P], vc[:, t, h * P:(h + 1) * P], atT[:, h, t, :],
                                  start=True, stop=False)
                        for n in range(max(1, 4 * t), 4 * t + 4):
                            m = pe.matmul(o[:, n * GCH:(n + 1) * GCH], st8[rows, n, h // 2, :],
                                          qgT[rows, h // 2, n * GCH:(n + 1) * GCH], start=False, stop=n == 4 * t + 3)
                m.then_inc(S_.o_psum, 1)
                pe.wait_ge(S_.osq_ready, L + 1)
                for h in range(GH):
                    for t in range(TT):
                        m = pe.matmul(ps[:, 0, 2 * h + t:2 * h + t + 1], rv[:, h, t * P:(t + 1) * P], ones[:, 0:1],
                                      start=True, stop=True)
                m.then_inc(S_.osum_psum, 1)
                pe.wait_ge(S_.odiag_ready, L + 1)
                for b in range(2):
                    m = pe.matmul(ps[:, 1 + b, :], ones, rv[:, 2 * b:2 * b + 2, :].rearrange("p h n -> p (h n)"),
                                  start=True, stop=True)
                m.then_inc(S_.oscale_psum, 1)
                pe.wait_ge(S_.yT2_lo_ready, L * 4 + 4)
                for n in range(4):
                    o = [ps[:, 2 * t + n // 2, (n % 2) * 256:(n % 2) * 256 + 256] for t in range(TT)]
                    project_tok(u + (11 + n), o, yA_chunks + yM_chunks, 256)
                pe.wait_ge(S_.xn_ready, L * 2 + 7)
                transpose_x(xn, L * 8 + 32)
                open_sums()

            pe.wait_ge(S_.ident_loaded, 16)
            pe.transpose(ps[:, 4, 0:P], ident, ident).then_inc(S_.unit_used, SPL)
            pe.wait_ge(S_.table_loaded, 32)
            pe.matmul(ps[0:HA, 0, 0:BUCKET_W], relrow, onehot_sb[:], start=True, stop=True).then_inc(S_.bvec_psum, 1)
            pe.wait_ge(S_.bvec_ready, 1)
            pe.wait_ge(S_.x_loaded, 16)
            with pe.Fori(0, 2) as L:
                mixer1(L, Count(0).loop(L, LAYER1_UNITS))
                with pe.If(L == 0):
                    open_sums()
                    feed_forward(Count(MIX1_UNITS), DENSE_STEPS, Count(0), hT_hi, hT_lo, F1)
                    close_sums()
                with pe.Else():
                    router()
                    pe.wait_ge(S_.passes_ready, 1)
                    experts(pe.value_load(passes_sb[0:1, 0:1], min_val=1, max_val=2))
            passes = pe.value_load(passes_sb[0:1, 0:1], min_val=1, max_val=2)
            with pe.Fori(0, 2) as L:
                u = block2_units(passes).loop(L, LAYER2_UNITS)
                mixer2(L, u)
                feed_forward(u + MIX2_UNITS, DENSE_STEPS, Count(0).loop(L, DENSE_STEPS), h2_hi, h2_lo, F2)
                close_sums()

        @block.scalar
        def _(act):
            def split(u, width=UW):
                act.wait_ge(raw_landed[u.const % RAW], u.turns(RAW).value(16, 16))
                act.wait_ge(S_.unit_used, u.value(plus=1))
                act.activation(w_hi[:, u.const % SPL, 0:width], raw[:, u.const % RAW, 0:width], ACT.Copy)\
                   .then_inc(S_.hi_ready, 1)

            def split_next(u):
                for n in range(AHEAD):
                    split(u + n)

            def used(u):
                act.wait_ge(S_.unit_used, u.value(plus=SPL + 1))

            def x_parts(count):
                for b in range(4):
                    act.wait_ge(S_.xT_psum, count + b + 1)
                    act.activation(xT_hi[:, 2 * b:2 * b + 2, :], bank(4 + b, 2, S), ACT.Copy).then_inc(S_.xT_hi_ready, 1)

            def y_parts(first, dst, psum, count, done):
                for b in range(2):
                    act.wait_ge(psum, count + b + 1)
                    act.activation(dst[:, 2 * b:2 * b + 2, :], bank(first + b, 2, S), ACT.Copy).then_inc(done, 1)

            def square_root(ready, done, count, v):
                act.wait_ge(ready, count)
                act.activation(v, v, ACT.Sqrt).then_inc(done, 1)

            def feed_forward(u, steps, count, hh, sig, gated):
                def step(j, at, odd, dyn, first):
                    if not first:
                        split(at + 1)
                        split(at + 2)
                    gated(at, odd, dyn, at + (2 if first else 3))
                    act.wait_ge(sig["h_ready"], dyn.value(plus=3))
                    act.activation(hh[:, odd], sig["h"][:, odd].rearrange("p (c n) -> p c n", c=2), ACT.Copy)\
                       .then_inc(sig["h_hi_ready"], 1)

                step(0, u, 0, count, True)
                pairs = (steps - 1) // 2
                with act.Fori(0, pairs) as i:
                    for q in range(2):
                        step(None, (u + (2 + STEP * q)).loop(i, 2 * STEP), (1 + q) % 2, (count + (1 + q)).loop(i, 2), False)
                for j in range(2 * pairs + 1, steps):
                    step(j, u + (2 + STEP * (j - 1)), j % 2, count + j, False)

            def silu1(at, odd, dyn, after):
                act.wait_ge(S_.h1_ready, dyn.value(plus=1))
                used(at)
                act.activation(sa[:, odd], ps[:, 4 + 2 * odd, :], ACT.Silu).then_inc(S_.silu1_ready, 1)
                split(after)

            def conv2(at, odd, dyn, after):
                act.wait_ge(S_.h2_ready, dyn.value(plus=1))
                used(at)
                act.activation(u_a[:, odd, :, 2:], bank(4 + 2 * odd, 2, S), ACT.Copy).then_inc(S_.ua_ready, 1)
                split(after)
                used(at + 1)
                act.activation(u_g[:, odd, :, 2:], bank(5 + 2 * odd, 2, S), ACT.Copy).then_inc(S_.ug_ready, 1)
                act.wait_ge(S_.ca_ready, dyn.value(plus=1))
                act.activation(c_a[:, odd], c_a[:, odd], ACT.Silu).then_inc(S_.silu2_ready, 1)

            def mixer1(L, u):
                x_parts(L * 12)
                for n in range(10):
                    split(u + (n + AHEAD))
                    used(u + n)
                    c = n % 2
                    if n < 4:
                        act.activation((qT if n < 2 else kT)[:, 2 * c:2 * c + 2, :], bank(n % 4, 2, S), ACT.Copy)\
                           .then_inc(S_.proj1_out, 1)
                    elif n < 6:
                        act.activation(xmT[:, 2 * c:2 * c + 2, CONV_K - 1:], bank(n % 4, 2, S), ACT.Copy)\
                           .then_inc(S_.proj1_out, 1)
                    elif n < 8:
                        act.activation(vA[:, :, c * 256:(c + 1) * 256], bank(n % 4, TT, 256), ACT.Copy).then_inc(S_.proj1_out, 1)
                    else:
                        act.activation(zg[:, :, c * 256:(c + 1) * 256], bank(n % 4, TT, 256), ACT.Sigmoid)\
                           .then_inc(S_.proj1_out, 1)
                    if n == 5:
                        act.wait_ge(S_.p1_cols_psum, L + 1)
                        act.activation(cols1[:], ps[:, 7, 0:20], ACT.Copy).then_inc(S_.p1_cols_ready, 1)
                    if n == 7:
                        act.wait_ge(S_.smax1, L * 2 + 1)
                        act.activation(sc0[:], sc0[:], ACT.Exp).then_inc(S_.expd1, 1)
                act.wait_ge(S_.smax1, L * 2 + 2)
                act.activation(sc1[:], sc1[:], ACT.Exp).then_inc(S_.expd1, 1)
                act.wait_ge(S_.conv1_done, L + 1)
                for c in range(4):
                    m = act.activation(xcT[:, c, :], xcT[:, c, :], ACT.Silu, bias=cols1[:, 16 + c:17 + c])
                m.then_inc(S_.xc_ready, 1)
                act.wait_ge(S_.qk_m_psum, L + 1)
                act.activation(qT[:], bank(0, 4, S), ACT.Copy)
                act.activation(kT[:], bank(2, 4, S), ACT.Copy).then_inc(S_.qk_m_ready, 1)
                for h in range(HA):
                    act.wait_ge(S_.pT1_psum, L * HA + (h + 1))
                    if h >= 2:
                        act.wait_ge(S_.pv1, L * HA + (h - 1))
                    act.activation(pT1[:, h % 2], bank(6 + h % 2, 3, P), ACT.Copy).then_inc(S_.pT1_ready, 1)
                y_parts(6, yA_hi, S_.yT_psum, L * 4, S_.yT_hi_ready)
                act.wait_ge(S_.v_m_psum, L + 1)
                act.activation(vT[:], bank(0, 4, S), ACT.Copy)
                for t in range(TT):
                    m = act.activation(vme[:, t, :, 0:HDM], bank(2 + t, HM, HDM), ACT.Copy)
                m.then_inc(S_.v_m_ready, 1)
                act.wait_ge(S_.f_ready, L + 1)
                act.activation(stat[:, 16:24], stat[:, 8:16], ACT.Abs)
                act.drain()
                act.activation(stat[:, 16:24], stat[:, 16:24], ACT.Exp, scale=-1.0)
                act.drain()
                act.activation(stat[:, 16:24], stat[:, 16:24], ACT.Ln, bias=1.0).then_inc(S_.f_ln, 1)
                act.wait_ge(S_.dloc_ready, L + 1)
                for t in range(TT):
                    for h in range(HM):
                        act.activation(dm[:, t, h, :], dm[:, t, h, :], ACT.Exp, bias=stat[:, 72 + 4 * t + h:73 + 4 * t + h])
                act.activation(stat[:, 80:96], stat[:, 80:96], ACT.Exp).then_inc(S_.dexp_ready, 1)
                act.wait_ge(S_.sT_psum, L + 1)
                act.activation(dm[:].rearrange("p t h n -> p (t h n)"), ps[:, 6:8, :].rearrange("p b n -> p (b n)"), ACT.Copy)\
                   .then_inc(S_.sT_ready, 1)
                act.wait_ge(S_.cn_psum, L + 1)
                act.activation(cn[:].rearrange("p (b h) e -> p b (h e)", b=2), ps[:, 2:4, 0:2 * (HDM + 1)], ACT.Copy)\
                   .then_inc(S_.cn_ready, 1)
                split(u + (10 + AHEAD))
                square_root(S_.sqrt_in, S_.sqrt_out, L * 3 + 1, stat[:, 112:120])
                y_parts(4, yM_hi, S_.yT_psum, L * 4 + 2, S_.yT_hi_ready)
                gates = 0
                for m_, (kind, c) in enumerate(MERGE_UNITS):
                    if m_:
                        split(u + (10 + m_ + AHEAD))
                    if kind in ("ga", "gm"):
                        act.wait_ge(S_.gate_lin, L * 8 + (gates + 1))
                        v = ga if kind == "ga" else gm
                        act.activation(v[:], v[:], ACT.Sigmoid).then_inc(S_.gate_sig, 1)
                        gates += 1
                x_parts(L * 12 + 4)
                for n, (c0, w) in enumerate(WO_UNITS):
                    k = n + AHEAD
                    split(u + (22 + k), KC * WO_UNITS[k][1] if k < len(WO_UNITS) else UW)
                layer_norm_root(L * 3 + 2)
                x_parts(L * 12 + 8)

            def layer_norm_root(count):
                square_root(S_.sqrt_in, S_.sqrt_out, count, stat[:, 120:122])

            def router():
                act.wait_ge(S_.rexp_in, 1)
                act.activation(rt[:, 0], rt[:, 0], ACT.Exp).then_inc(S_.rexp_out, 1)

            def experts(passes):
                def tokens(n):
                    act.wait_ge(S_.xg_psum, n.value(plus=1))
                    act.activation(xg_hi[:], bank(0, KC, P), ACT.Copy).then_inc(S_.xg_hi_ready, 1)

                def silu(at, odd):
                    used(at)
                    act.activation(sa[:, odd, 0:FFC], ps[:, 6, 0:FFC], ACT.Silu).then_inc(S_.silue_ready, 1)

                def hidden_part(n):
                    act.wait_ge(S_.heT_psum, n.value(plus=1))
                    act.activation(hT_hi[:, 0, 0, :], ps[:, 7, 0:S], ACT.Copy).then_inc(S_.heT_hi_ready, 1)

                def step(at, odd, n):
                    split(at + 1)
                    split(at + 2)
                    silu(at, odd)
                    hidden_part(n + -1)
                    split(at + 3)

                act.activation(stat[:, 5:6], ones[:, 0:1], ACT.Copy).then_inc(S_.silue_ready, 1)
                tokens(Count(0))
                with act.Fori(0, passes * E_N) as e:
                    item = Count(0).loop(e, 1)
                    u, n = Count(MOE_UNIT0).loop(e, EXPERT_UNITS), Count(0).loop(e, MOE_STEPS)
                    act.wait_ge(S_.put_psum, e + 1)
                    act.activation(put[:], bank(7, 4, P)[:, 2:4, :], ACT.Copy).then_inc(S_.put_ready, 1)
                    silu(u, 0)
                    split(u + 2)
                    pairs = (MOE_STEPS - 1) // 2
                    with act.Fori(0, pairs) as i:
                        for q in range(2):
                            step((u + (2 + STEP * q)).loop(i, 2 * STEP), (1 + q) % 2, (n + (1 + q)).loop(i, 2))
                    at, j = u + (2 + STEP * 2 * pairs), n + (MOE_STEPS - 1)
                    step(at, 1, j)
                    tokens(item + 1)
                    hidden_part(j)
                    split_next(u + EXPERT_UNITS)
                    act.wait_ge(S_.eo_psum, e + 1)
                    act.activation(eo[:, 0:HALF], ps[:, 4, :], ACT.Copy).then_inc(S_.eo_ready, 1)

            def mixer2(L, u):
                square_root(S_.sqrt2_in, S_.sqrt2_out, L * 5 + 1, stat[:, 120:122])
                x_parts(L * 8 + 24)

                def out(n):
                    split(u + (n + AHEAD))
                    used(u + n)

                out(0)
                act.activation(avT[:, :, CW - 1:], bank(0, 2, S), ACT.Copy).then_inc(S_.proj2_out, 1)
                out(1)
                act.activation(agT[:], bank(1, 2, S), ACT.Sigmoid).then_inc(S_.proj2_out, 1)
                act.wait_ge(S_.p2_cols_psum, L + 1)
                act.activation(cols2[:], ps[:, 7, 0:250], ACT.Copy).then_inc(S_.p2_cols_ready, 1)
                act.wait_ge(S_.g16_psum, L + 1)
                act.activation(gT[:], ps[0:16, 6, 0:S], ACT.Copy).then_inc(S_.g16_ready, 1)
                out(2)
                act.activation(qbT[:], bank(2, 2, S), ACT.Copy).then_inc(S_.proj2_out, 1)
                out(3)
                act.activation(kbT[:], bank(3, 2, S), ACT.Copy).then_inc(S_.proj2_out, 1)
                out(4)
                act.activation(vb[:], bank(0, TT, 256), ACT.Copy).then_inc(S_.proj2_out, 1)
                out(5)
                act.activation(qcT[:], bank(1, 2, S), ACT.Copy, scale=float(GDK) ** -0.5).then_inc(S_.proj2_out, 1)
                out(6)
                act.activation(kcT[:], bank(2, 2, S), ACT.Copy).then_inc(S_.proj2_out, 1)
                out(7)
                act.activation(vc[:, :, 0:256], bank(3, TT, 256), ACT.Copy).then_inc(S_.proj2_out, 1)
                act.wait_ge(S_.smax2, L + 1)
                act.activation(sb0[:], sb0[:], ACT.Exp)
                act.activation(sb1[:], sb1[:], ACT.Exp).then_inc(S_.expd2, 1)
                act.wait_ge(S_.glog_in, L + 1)
                act.activation(egT[:], laT[:], ACT.Abs)
                act.drain()
                act.activation(egT[:], egT[:], ACT.Exp, scale=-1.0)
                act.drain()
                act.activation(egT[:], egT[:], ACT.Ln, bias=1.0).then_inc(S_.gln_ready, 1)
                out(8)
                act.activation(vc[:, :, 256:512], bank(0, TT, 256), ACT.Copy).then_inc(S_.proj2_out, 1)
                act.wait_ge(S_.cum_ready, L + 1)
                act.activation(egT[:], cumT[:], ACT.Exp, scale=1.0 / TAU)
                act.activation(laT[:], cumT[:], ACT.Exp, scale=-1.0 / TAU)
                act.activation(dec[:], stat[:, 128:144].rearrange("p (c n) -> p c n", c=2), ACT.Exp, scale=1.0 / TAU)\
                   .then_inc(S_.gexp_ready, 1)
                act.wait_ge(S_.rest_ready, L + 1)
                act.activation(cumT[:], cumT[:], ACT.Exp, scale=1.0 / TAU).then_inc(S_.gexp_ready, 1)
                out(9)
                act.activation(rT[:, 0:2, :], bank(1, 2, S), ACT.Silu).then_inc(S_.proj2_out, 1)
                out(10)
                act.activation(rT[:, 2:4, :], bank(2, 2, S), ACT.Silu).then_inc(S_.proj2_out, 1)
                for h in range(HB):
                    act.wait_ge(S_.pT2_psum, L * HB + (h + 1))
                    if h >= 2:
                        act.wait_ge(S_.pv2, L * HB + (h - 1))
                    act.activation(pT2[:, h % 2], bank(6 + h % 2, 3, P), ACT.Copy).then_inc(S_.pT2_ready, 1)
                square_root(S_.sqrt2_in, S_.sqrt2_out, L * 5 + 2, stat[:, 112:120])
                act.wait_ge(S_.yb_psum, L + 1)
                act.activation(yA_hi[:, 2:4, :], bank(6, 2, S), ACT.Copy).then_inc(S_.yT2_hi_ready, 1)
                act.wait_ge(S_.kd_psum, L + 1)
                act.activation(kd[:].rearrange("p t c n -> p (t c n)"), ps[:, 0, :], ACT.Copy).then_inc(S_.kd_ready, 1)
                act.wait_ge(S_.cent_ready, L + 1)
                act.activation(agT[:], cvT[:], ACT.Square).then_inc(S_.csq_ready, 1)
                square_root(S_.sqrt2_in, S_.sqrt2_out, L * 5 + 3, agT[:, 0, :])
                act.wait_ge(S_.cnorm_ready, L + 1)
                for c in range(2):
                    act.activation(cvT[:, c, :], cvT[:, c, :], ACT.Silu, scale=cols2[:, 64 + c:65 + c], bias=cols2[:, 66 + c:67 + c])
                act.drain()
                act.activation(yA_hi[:, 0:2, :], cvT[:], ACT.Copy).then_inc(S_.yT2_hi_ready, 1)
                act.wait_ge(S_.o_psum, L + 1)
                act.activation(rv[:], bank(5, 4, S), ACT.Square).then_inc(S_.osq_ready, 1)
                square_root(S_.sqrt2_in, S_.sqrt2_out, L * 5 + 4, stat[:, 96:104])
                for q in range(2):
                    act.wait_ge(S_.oc_ready, L * 2 + (q + 1))
                    act.activation(yM_hi[:, 2 * q:2 * q + 2, :], oc[:, 2 * q:2 * q + 2, :], ACT.Copy).then_inc(S_.yT2_hi_ready, 1)
                for n in range(4):
                    split(u + (11 + n + AHEAD))
                square_root(S_.sqrt2_in, S_.sqrt2_out, L * 5 + 5, stat[:, 120:122])
                x_parts(L * 8 + 28)

            act.wait_ge(S_.ident_loaded, 16)
            act.activation(stat[:, 0:1], ones[:, 0:1], ACT.Copy).then_inc(S_.hi_ready, RAW)
            act.wait_ge(S_.bvec_psum, 1)
            act.activation(bvec[:], ps[0:HA, 0, 0:BUCKET_W], ACT.Copy).then_inc(S_.bvec_ready, 1)
            for n in range(AHEAD):
                split(Count(n))
            with act.Fori(0, 2) as L:
                mixer1(L, Count(0).loop(L, LAYER1_UNITS))
                with act.If(L == 0):
                    feed_forward(Count(MIX1_UNITS), DENSE_STEPS, Count(0), hT_hi, F1, silu1)
                    split_next(Count(LAYER1_UNITS))
                with act.Else():
                    router()
                    act.wait_ge(S_.passes_ready, 1)
                    experts(act.value_load(passes_sb[0:1, 0:1], min_val=1, max_val=2))
                square_root(S_.sqrt_in, S_.sqrt_out, L * 3 + 3, stat[:, 120:122])
            passes = act.value_load(passes_sb[0:1, 0:1], min_val=1, max_val=2)
            with act.Fori(0, 2) as L:
                u = block2_units(passes).loop(L, LAYER2_UNITS)
                mixer2(L, u)
                at = u + MIX2_UNITS
                feed_forward(at, DENSE_STEPS, Count(0).loop(L, DENSE_STEPS), h2_hi, F2, conv2)
                with act.If(L == 0):
                    split_next(at + STEP * DENSE_STEPS)
                with act.Else():
                    act.nop()
            square_root(S_.sqrt2_in, S_.sqrt2_out, 11, stat[:, 120:122])

        @block.vector
        def _(dve):
            def split(u, width=UW):
                dve.wait_ge(S_.hi_ready, u.value(plus=RAW + 1))
                dve.tensor_tensor(w_lo[:, u.const % SPL, 0:width], raw[:, u.const % RAW, 0:width],
                                  w_hi[:, u.const % SPL, 0:width].bitcast(F32), ALU.subtract).then_inc(S_.lo_ready, 1)

            def split_next(u):
                for n in range(AHEAD):
                    split(u + n)

            def used(u):
                dve.wait_ge(S_.unit_used, u.value(plus=SPL + 1))

            def x_parts(count):
                for b in range(4):
                    dve.wait_ge(S_.xT_hi_ready, count + b + 1)
                    hi = xT_hi[:, 2 * b:2 * b + 2, :]
                    dve.tensor_tensor(xT_lo[:, 2 * b:2 * b + 2, :], bank(4 + b, 2, S), hi.bitcast(F32), ALU.subtract)\
                       .then_inc(S_.xT_lo_ready, 1)

            def y_parts(first, dst, hi, ready, count, done):
                for b in range(2):
                    dve.wait_ge(ready, count + b + 1)
                    dve.tensor_tensor(dst[:, 2 * b:2 * b + 2, :], bank(first + b, 2, S), hi[:, 2 * b:2 * b + 2, :].bitcast(F32),
                                      ALU.subtract).then_inc(done, 1)

            def col(a, n=1):
                return stat[:, a:a + n]

            def add_to_x():
                for t in range(TT):
                    dve.scalar_tensor_tensor(x[:, t, :], x[:, t, :], ALPHA, bank(2 * t, D), ALU.mult, ALU.add)
                dve.drain()

            def layer_norm(count, norms):
                for t in range(TT):
                    for h in range(2):
                        dve.bn_stats(col(122 + 12 * t + 6 * h, 6), x[:, t, h * HALF:(h + 1) * HALF])
                dve.drain()
                for t in range(TT):
                    dve.bn_aggr(col(146 + 2 * t, 2), col(122 + 12 * t, 12))
                dve.drain()
                for t in range(TT):
                    m = dve.tensor_scalar(col(120 + t), col(147 + 2 * t), LN_EPS, None, ALU.add)
                m.then_inc(S_.sqrt_in, 1)
                dve.wait_ge(S_.sqrt_out, count)
                dve.reciprocal(col(120, 2), col(120, 2))
                dve.drain()
                for t in range(TT):
                    dve.tensor_scalar(x[:, t, :], x[:, t, :], col(146 + 2 * t), col(120 + t), ALU.subtract, ALU.mult)
                dve.drain()
                dve.wait_ge(S_.norm_loaded, norms)
                for t in range(TT):
                    dve.tensor_tensor(x[:, t, :], x[:, t, :], norm_gb[:, 0, :], ALU.mult)
                dve.drain()
                for t in range(TT):
                    m = dve.tensor_tensor(x[:, t, :], x[:, t, :], norm_gb[:, 1, :], ALU.add)
                m.then_inc(S_.xn_ready, 1)

            def rms_norm(count, norms, done):
                for t in range(TT):
                    dve.tensor_tensor_reduce(out=xn[:, t, :], in0=x[:, t, :], in1=x[:, t, :], scale=1.0, scalar=0.0,
                                             op0=ALU.mult, op1=ALU.add, accum_out=col(120 + t))
                dve.drain()
                dve.tensor_scalar(col(120, 2), col(120, 2), 1.0 / D, RMS_EPS, ALU.mult, ALU.add).then_inc(S_.sqrt2_in, 1)
                dve.wait_ge(S_.sqrt2_out, count)
                dve.reciprocal(col(120, 2), col(120, 2))
                dve.drain()
                dve.wait_ge(S_.norm2_loaded, norms)
                for t in range(TT):
                    m = dve.scalar_tensor_tensor(xn[:, t, :], x[:, t, :], col(120 + t), norm_gb[:, 0, :], ALU.mult, ALU.mult)
                m.then_inc(done, 1)

            def feed_forward(u, steps, count, hh, hl, sig, hidden):
                def step(at, odd, dyn, first):
                    if not first:
                        split(at + 1)
                        split(at + 2)
                    hidden(at, odd, dyn, at + (2 if first else 3))
                    dve.wait_ge(sig["h_hi_ready"], dyn.value(plus=1))
                    dve.tensor_tensor(hl[:, odd], sig["h"][:, odd].rearrange("p (c n) -> p c n", c=2),
                                      hh[:, odd].bitcast(F32), ALU.subtract).then_inc(sig["h_lo_ready"], 1)

                step(u, 0, count, True)
                pairs = (steps - 1) // 2
                with dve.Fori(0, pairs) as i:
                    for q in range(2):
                        step((u + (2 + STEP * q)).loop(i, 2 * STEP), (1 + q) % 2, (count + (1 + q)).loop(i, 2), False)
                for j in range(2 * pairs + 1, steps):
                    step(u + (2 + STEP * (j - 1)), j % 2, count + j, False)

            def dense_hidden(at, odd, dyn, after):
                dve.wait_ge(S_.silu1_ready, dyn.value(plus=1))
                split(after)
                used(at + 1)
                dve.tensor_tensor(hf[:, odd], sa[:, odd], ps[:, 5 + 2 * odd, :], ALU.mult).then_inc(S_.h1_ready, 1)

            def less_max(sc, mx):
                dve.reduce_max(mx, sc, AX_X)
                dve.drain()
                return dve.tensor_tensor(sc, sc, spread(mx, 2, sc.shape[2]), ALU.subtract)

            def mixer1(L, u):
                x_parts(L * 12)
                for n in range(4):
                    split(u + (n + AHEAD))
                with dve.If(L == 0):
                    dve.wait_ge(S_.start_loaded, 32)
                    dve.wait_ge(S_.x_loaded, 16)
                    dve.wait_ge(S_.bias_psum, 1)
                    dve.tensor_tensor(bias[:], bank(4, HA, S), spread(K["winmask"], 1, HA), ALU.add).then_inc(S_.bias_done, 1)
                with dve.Else():
                    dve.nop()
                for n in (4, 5):
                    split(u + (n + AHEAD))
                for tile, heads, b, per, step in ((0, range(0, 8), 4, 4, 1), (1, range(0, 4), 6, 2, 2), (1, range(4, 8), 4, 2, 3)):
                    dve.wait_ge(S_.scores1, L * 3 + step)
                    n = P * (tile + 1)
                    for q in range(2):
                        hs = slice(heads[0] + q, heads[-1] + 1, 2)
                        m = dve.scalar_tensor_tensor((sc0, sc1)[tile][:, hs, :], bank(b + q, per, n), HDA ** -0.5,
                                                     bias[:, hs, S - n:S], ALU.mult, ALU.add)
                    m.then_inc(S_.scores1_in, 1)
                    dve.drain()
                    if step == 1:
                        less_max(sc0[:], col(160, 8)).then_inc(S_.smax1, 1)
                    if step == 2:
                        split(u + (6 + AHEAD))
                        split(u + (7 + AHEAD))
                less_max(sc1[:], col(168, 8)).then_inc(S_.smax1, 1)
                split(u + (8 + AHEAD))
                for t, sc in enumerate((sc0, sc1)):
                    dve.wait_ge(S_.expd1, L * 2 + t + 1)
                    n = P * (t + 1)
                    dve.tensor_tensor(sc[:], sc[:], spread(K["wincount"][:, S - n:S], 1, HA), ALU.mult).then_inc(S_.prob1, 1)
                    dve.drain()
                    dve.reduce_sum(col(176 + 8 * t, 8), sc[:], AX_X)
                dve.drain()
                dve.reciprocal(col(176, 16), col(176, 16))
                dve.drain()
                dve.wait_ge(S_.proj1_out, L * 10 + 10)
                dve.tensor_tensor(zg[:], zg[:], spread(gain_m[:], 1, TT), ALU.mult)
                split(u + (9 + AHEAD))
                ya = ht[:].rearrange("p t h e -> p (t h e)")[:, 0:TT * DM].rearrange("p (t n) -> p t n", t=TT)
                dve.wait_ge(S_.pv1, L * HA + HA)
                for t in range(TT):
                    m = dve.tensor_tensor(ya[:, t, :].rearrange("p (h e) -> p h e", h=HA), bank(4 + t, HA, HDA),
                                          spread(col(176 + 8 * t, 8), 2, HDA), ALU.mult)
                m.then_inc(S_.ya1_ready, 1)
                y_parts(6, yA_lo, yA_hi, S_.yT_hi_ready, L * 4, S_.yT_lo_ready)
                dve.wait_ge(S_.v_m_psum, L + 1)
                dve.memset(vme[:, :, :, HDM:], 1.0)
                dve.wait_ge(S_.gates_psum, L + 1)
                g = bank(5, 2, 8)
                dve.tensor_tensor(col(0, 8).rearrange("p (t h) -> p t h", t=TT), g[:, :, 0:4], spread(b_if[:, 0:4], 1, TT), ALU.add)
                dve.tensor_tensor(col(8, 8).rearrange("p (t h) -> p t h", t=TT), g[:, :, 4:8], spread(b_if[:, 4:8], 1, TT), ALU.add)\
                   .then_inc(S_.f_ready, 1)
                dve.wait_ge(S_.f_ln, L + 1)
                dve.scalar_tensor_tensor(col(16, 8), col(8, 8), 0.0, col(16, 8), ALU.min, ALU.subtract).then_inc(S_.logf_ready, 1)
                dve.wait_ge(S_.cum_psum, L + 1)
                c4 = lambda a: col(a, 8).rearrange("p (t h) -> p t h", t=TT)
                dve.tensor_copy(col(24, 8), ps[:, 5, 32:40])
                dve.tensor_copy(col(32, 8), ps[:, 5, 40:48])
                dve.tensor_tensor(col(40, 8), col(0, 8), ps[:, 5, 32:40], ALU.subtract)
                dve.drain()
                dg = ya
                for t in range(TT):
                    m = dve.tensor_tensor(dg[:, t, :].rearrange("p (h s) -> p h s", h=HM), spread(ident, 1, HM),
                                          spread(col(40 + 4 * t, 4), 2, P), ALU.mult)
                m.then_inc(S_.diag_ready, 1)
                dve.wait_ge(S_.rowr_psum, L + 1)
                dve.reduce_max(col(48, 4), bank(6, HM, P), AX_X)
                for t in range(TT):
                    dve.tensor_tensor(dm[:, t], bank(6 + t, HM, P), spread(K["tri"], 1, HM), ALU.add)
                dve.drain()
                for t in range(TT):
                    dve.reduce_max(col(52 + 4 * t, 4), dm[:, t], AX_X)
                dve.scalar_tensor_tensor(col(60, 4), col(48, 4), 0.0, col(32, 4), ALU.max, ALU.add)
                dve.drain()
                dve.tensor_copy(col(152, 4), col(24, 4))
                dve.tensor_tensor(col(156, 4), col(28, 4), col(60, 4), ALU.add)
                dve.tensor_tensor(col(64, 8), col(52, 8), col(24, 8), ALU.add)
                dve.drain()
                dve.tensor_tensor(col(64, 8), col(64, 8), col(152, 8), ALU.max)
                dve.tensor_tensor(col(92, 4), col(40, 4), col(32, 4), ALU.add)
                dve.drain()
                dve.tensor_tensor(col(72, 8), col(24, 8), col(64, 8), ALU.subtract)
                dve.tensor_tensor(col(80, 4), col(156, 4), col(68, 4), ALU.subtract)
                dve.tensor_scalar(col(84, 8), col(64, 8), -1.0, None, ALU.mult)
                dve.tensor_tensor(col(92, 4), col(92, 4), col(60, 4), ALU.subtract).then_inc(S_.dloc_ready, 1)
                dve.wait_ge(S_.dexp_ready, L + 1)
                for t in range(TT):
                    m = dve.scalar_tensor_tensor(dm[:, t].rearrange("p h n -> p (h n)"), ps[:, t, :], HDM ** -0.5,
                                                 dm[:, t].rearrange("p h n -> p (h n)"), ALU.mult, ALU.mult)
                m.then_inc(S_.s_ready, 1)
                dve.scalar_tensor_tensor(kw[:], bank(4, HM, HDM), HDM ** -0.5, spread(col(92, 4), 2, HDM), ALU.mult, ALU.mult)\
                   .then_inc(S_.kw_ready, 1)
                dve.wait_ge(S_.num_psum, L + 1)
                E1 = HDM + 1
                flat = ht[:].rearrange("p t (b h) e -> p t b (h e)", b=2)
                dve.tensor_copy(flat[:, 0], ps[:, 0:2, 0:2 * E1])
                for b in range(2):
                    dve.tensor_tensor(ht[:, 1, 2 * b:2 * b + 2, :], bank(2 + b, 2, E1), spread(col(80 + 2 * b, 2), 2, E1), ALU.mult)
                dve.drain()
                dve.tensor_tensor(flat[:, 1], flat[:, 1], ps[:, 4:6, 0:2 * E1], ALU.add)
                dve.drain()
                hv = ht[:].rearrange("p t h e -> p (t h) e")
                nq = hv[:, :, HDM:HDM + 1].rearrange("p a o -> p (a o)")
                h_ = hv[:, :, 0:HDM]
                dve.tensor_scalar(col(96, 8), nq, -1.0, None, ALU.mult)
                dve.drain()
                dve.tensor_tensor(col(96, 8), col(96, 8), nq, ALU.max)
                dve.drain()
                dve.tensor_tensor(col(96, 8), col(96, 8), col(84, 8), ALU.max)
                dve.drain()
                dve.reciprocal(col(96, 8), col(96, 8))
                dve.drain()
                dve.tensor_tensor(h_, h_, spread(col(96, 8), 2, HDM), ALU.mult)
                dve.drain()
                dve.reduce_sum(col(104, 8), h_, AX_X)
                dve.drain()
                dve.tensor_scalar(col(104, 8), col(104, 8), 1.0 / HDM, None, ALU.mult)
                dve.drain()
                dve.tensor_tensor(h_, h_, spread(col(104, 8), 2, HDM), ALU.subtract)
                dve.drain()
                sq = dm[:].rearrange("p t h n -> p (t h) n")
                dve.tensor_tensor(sq, h_, h_, ALU.mult)
                dve.drain()
                dve.reduce_sum(col(112, 8), sq, AX_X)
                dve.drain()
                dve.tensor_scalar(col(112, 8), col(112, 8), 1.0 / HDM, LN_EPS, ALU.mult, ALU.add).then_inc(S_.sqrt_in, 1)
                split(u + (10 + AHEAD))
                dve.wait_ge(S_.sqrt_out, L * 3 + 1)
                dve.reciprocal(col(112, 8), col(112, 8))
                dve.drain()
                dve.tensor_tensor(h_, h_, spread(col(112, 8), 2, HDM), ALU.mult)
                dve.drain()
                dve.tensor_tensor(h_, h_, zg[:].rearrange("p t (h e) -> p (t h) e", h=HM), ALU.mult).then_inc(S_.ym_ready, 1)
                y_parts(4, yM_lo, yM_hi, S_.yT_hi_ready, L * 4 + 2, S_.yT_lo_ready)
                dve.wait_ge(S_.bg_loaded, L * 16 + 16)
                gates = 0

                def merge(c):
                    dve.wait_ge(S_.gate_sig, L * 8 + 2 * c + 2)
                    q = slice((c % 2) * FFC, (c % 2 + 1) * FFC)
                    dve.tensor_tensor(ga[:], ga[:], ps[:, 0:2, q], ALU.mult)
                    dve.tensor_tensor(gm[:], gm[:], ps[:, 2:4, q], ALU.mult)
                    dve.drain()
                    dve.tensor_tensor(merged[:, :, c * FFC:(c + 1) * FFC], ga[:], gm[:], ALU.add).then_inc(S_.merged_ready, 1)
                    dve.drain()

                for m_, (kind, c) in enumerate(MERGE_UNITS):
                    if m_:
                        split(u + (10 + m_ + AHEAD))
                    if kind in ("ga", "gm"):
                        used(u + (10 + m_))
                        i = kind == "gm"
                        dve.tensor_tensor((ga, gm)[i][:], bank(GATE_BANKS[gates % 4], TT, FFC),
                                          spread(bg[:, int(i), c * FFC:(c + 1) * FFC], 1, TT), ALU.add).then_inc(S_.gate_lin, 1)
                        gates += 1
                        if (kind, c) in (("gm", 1), ("gm", 3)):
                            merge(c)
                    elif kind == "m":
                        used(u + (10 + m_))
                        merge(2 if c else 0)
                x_parts(L * 12 + 4)
                for n, (c0, w) in enumerate(WO_UNITS):
                    k = n + AHEAD
                    split(u + (22 + k), KC * WO_UNITS[k][1] if k < len(WO_UNITS) else UW)
                used(u + (MIX1_UNITS - 1))
                add_to_x()
                layer_norm(L * 3 + 2, L * 64 + 32)
                x_parts(L * 12 + 8)

            def router():
                dve.wait_ge(S_.router_loaded, 32)
                dve.tensor_copy(rw_hi[:], rw_raw[:])
                dve.drain()
                dve.tensor_tensor(rw_lo[:], rw_raw[:], rw_hi[:].bitcast(F32), ALU.subtract).then_inc(S_.rw_split, 1)
                dve.wait_ge(S_.logits_psum, 1)
                dve.tensor_tensor(lg[:], bank(4, TT, E_N), spread(rb[:], 1, TT), ALU.add)
                dve.drain()
                for t in range(TT):
                    other, own = spread(lg[:, t, :], 1, E_N), spread(lg[:, t, :], 2, E_N)
                    dve.tensor_tensor(cmp2[:, 0], other, own, ALU.is_gt)
                    dve.tensor_tensor(cmp2[:, 1], other, own, ALU.is_equal)
                    dve.drain()
                    dve.tensor_tensor(cmp2[:, 1], cmp2[:, 1], K["lower"].rearrange("p (e j) -> p e j", e=E_N), ALU.mult)
                    dve.drain()
                    dve.tensor_tensor(cmp2[:, 0], cmp2[:, 0], cmp2[:, 1], ALU.add)
                    dve.drain()
                    dve.reduce_sum(rt[:, 1, t, :], cmp2[:, 0], AX_X)
                    dve.reduce_max(rt[:, 2, t, 0:1], lg[:, t, :], AX_X)
                    dve.drain()
                    dve.tensor_scalar(rt[:, 1, t, :], rt[:, 1, t, :], 2.0, None, ALU.is_lt)
                    m = dve.tensor_scalar(rt[:, 0, t, :], lg[:, t, :], rt[:, 2, t, 0:1], None, ALU.subtract)
                m.then_inc(S_.rexp_in, 1)
                dve.memset(stat[:, 6:7], 0.0).then_inc(S_.chosen_ready, 1)
                dve.wait_ge(S_.rexp_out, 1)
                dve.tensor_tensor(rt[:, 0], rt[:, 0], rt[:, 1], ALU.mult)
                dve.drain()
                dve.reduce_sum(col(100, 2), rt[:, 0], AX_X)
                dve.drain()
                dve.reciprocal(col(100, 2), col(100, 2))
                dve.drain()
                dve.tensor_tensor(rt[:, 0], rt[:, 0], spread(col(100, 2), 2, E_N), ALU.mult)
                dve.drain()
                for b in range(2):
                    dve.tensor_copy(gate_of[:, :, b * E_N:(b + 1) * E_N], rt[:, 0])
                dve.wait_ge(S_.slots_psum, 1)
                dve.tensor_tensor(rt[:, 3], rt[:, 1], bank(5, TT, E_N), ALU.mult)
                dve.tensor_scalar(rt[:, 4], rt[:, 1], 4.0 * S, -4.0 * S, ALU.mult, ALU.add)
                dve.reduce_max(col(102), ps[:, 5, 16:24], AX_X)
                dve.drain()
                dve.tensor_tensor(slot_of[:, :, 0:E_N], rt[:, 3], rt[:, 4], ALU.add)
                dve.tensor_scalar(passes_sb[:], stat[0:1, 102:103], float(P), 1.0, ALU.is_gt, ALU.add).then_inc(S_.passes_ready, 1)
                dve.drain()
                dve.tensor_scalar(slot_of[:, :, E_N:2 * E_N], slot_of[:, :, 0:E_N], float(P), None, ALU.subtract)
                dve.memset(slot_of[:, :, 2 * E_N:], -1.0)
                dve.memset(gate_of[:, :, 2 * E_N:], 0.0)
                dve.tensor_scalar(y_sum[:], x[:], ALPHA, None, ALU.mult).then_inc(S_.y_added, 1)
                dve.drain()

            def experts(passes):
                def tokens_of(n):
                    at = n.value()
                    for t in range(TT):
                        s = slot_of[:, t, bass.ds(at, 1)]
                        dve.tensor_scalar(pick[:, t, :], K["iota"], s, None, ALU.is_equal)
                        m = dve.tensor_scalar(pick_gate[:, t, :], K["iota"], s, gate_of[:, t, bass.ds(at, 1)],
                                              ALU.is_equal, ALU.mult)
                    m.then_inc(S_.pick_ready, 1)

                def tokens(n):
                    dve.wait_ge(S_.xg_hi_ready, n.value(plus=1))
                    dve.tensor_tensor(xg_lo[:], bank(0, KC, P), xg_hi[:].bitcast(F32), ALU.subtract).then_inc(S_.xg_lo_ready, 1)

                def hidden(at, odd):
                    used(at + 1)
                    dve.tensor_tensor(hf[:, 0, 0:FFC], sa[:, odd, 0:FFC], ps[:, 2, 0:FFC], ALU.mult).then_inc(S_.he_ready, 1)

                def hidden_part(n):
                    dve.wait_ge(S_.heT_hi_ready, n.value(plus=1))
                    dve.tensor_tensor(hT_lo[:, 0, 0, :], ps[:, 7, 0:S], hT_hi[:, 0, 0, :].bitcast(F32), ALU.subtract)\
                       .then_inc(S_.heT_lo_ready, 1)

                def step(at, odd, n):
                    split(at + 1)
                    split(at + 2)
                    hidden_part(n + -1)
                    split(at + 3)
                    dve.wait_ge(S_.silue_ready, n.value(plus=2))
                    hidden(at, odd)

                tokens_of(Count(0))
                tokens(Count(0))
                with dve.Fori(0, passes * E_N) as e:
                    item = Count(0).loop(e, 1)
                    u, n = Count(MOE_UNIT0).loop(e, EXPERT_UNITS), Count(0).loop(e, MOE_STEPS)
                    split(u + 2)
                    dve.wait_ge(S_.silue_ready, n.value(plus=2))
                    hidden(u, 0)
                    dve.wait_ge(S_.put_psum, e + 1)
                    tokens_of(item + 1)
                    pairs = (MOE_STEPS - 1) // 2
                    with dve.Fori(0, pairs) as i:
                        for q in range(2):
                            step((u + (2 + STEP * q)).loop(i, 2 * STEP), (1 + q) % 2, (n + (1 + q)).loop(i, 2))
                    at, j = u + (2 + STEP * 2 * pairs), n + (MOE_STEPS - 1)
                    step(at, 1, j)
                    tokens(item + 1)
                    hidden_part(j)
                    split_next(u + EXPERT_UNITS)
                    dve.wait_ge(S_.eo_psum, e + 1)
                    dve.tensor_copy(eo[:, HALF:], ps[:, 5, :]).then_inc(S_.eo_ready, 1)
                    dve.wait_ge(S_.y_psum, e + 1)
                    dve.tensor_tensor(y_sum[:].rearrange("p t n -> p (t n)"), y_sum[:].rearrange("p t n -> p (t n)"),
                                      bank(0, TT * D), ALU.add).then_inc(S_.y_added, 1)
                dve.drain()
                dve.tensor_copy(x[:], y_sum[:])
                dve.drain()

            def mixer2(L, u):
                rms_norm(L * 5 + 1, L * 32 + 16, S_.xn_ready)
                dve.memset(avT[:, :, 0:CW - 1], 0.0)
                x_parts(L * 8 + 24)
                for n in (0, 1):
                    split(u + (n + AHEAD))
                dve.wait_ge(S_.proj2_out, L * 11 + 2)
                dve.tensor_tensor(avT[:, :, CW - 1:], avT[:, :, CW - 1:], agT[:], ALU.mult).then_inc(S_.glu_ready, 1)
                dve.drain()
                dve.wait_ge(S_.p2_cols_ready, L + 1)
                taps = [POOL_TAPS[-1] + 1]

                def convolve(n):
                    for k in range(taps[0], taps[0] + n):
                        for c in range(2):
                            w = cols2[:, 2 * k + c:2 * k + c + 1]
                            if k == POOL_TAPS[-1] + 1:
                                dve.tensor_scalar(cvT[:, c, :], avT[:, c, k:k + S], w, cols2[:, 62 + c:63 + c], ALU.mult, ALU.add)
                            else:
                                dve.scalar_tensor_tensor(cvT[:, c, :], avT[:, c, k:k + S], w, cvT[:, c, :], ALU.mult, ALU.add)
                        dve.drain()
                    taps[0] += n

                split(u + (2 + AHEAD))
                convolve(3)
                split(u + (3 + AHEAD))
                convolve(3)
                split(u + (4 + AHEAD))
                dve.wait_ge(S_.scores2, L * 2 + 1)
                for q in range(2):
                    dve.scalar_tensor_tensor(sb0[:, q::2, :], bank(4 + q, 2, P), HDB ** -0.5,
                                             spread(K["causal"][:, P:S], 1, 2), ALU.mult, ALU.add)
                dve.wait_ge(S_.scores2, L * 2 + 2)
                for q in range(2):
                    m = dve.scalar_tensor_tensor(sb1[:, q::2, :], bank(6 + q, 2, S), HDB ** -0.5,
                                                 spread(K["causal"], 1, 2), ALU.mult, ALU.add)
                m.then_inc(S_.scores2_in, 1)
                dve.drain()
                less_max(sb0[:], col(160, 4))
                split(u + (5 + AHEAD))
                less_max(sb1[:], col(164, 4)).then_inc(S_.smax2, 1)
                dve.wait_ge(S_.glog_psum, L + 1)
                dve.wait_ge(S_.p2_cols_ready, L + 1)
                for c in range(2):
                    m = dve.tensor_scalar(laT[:, c, :], ps[:, 7, c * S:(c + 1) * S], cols2[:, 68 + c:69 + c], None, ALU.add)
                m.then_inc(S_.glog_in, 1)
                for n in range(6, 11):
                    if n == 8:
                        dve.wait_ge(S_.expd2, L + 1)
                        for t, sc in enumerate((sb0, sb1)):
                            dve.reduce_sum(col(176 + 4 * t, 4), sc[:], AX_X)
                        dve.drain()
                        dve.reciprocal(col(176, 8), col(176, 8))
                        dve.drain()
                        dve.memset(stat[:, 0:1], 0.0).then_inc(S_.prob2, 2)
                    if n == 9:
                        dve.wait_ge(S_.gln_ready, L + 1)
                        dve.scalar_tensor_tensor(laT[:], laT[:], 0.0, egT[:], ALU.min, ALU.subtract)
                        dve.drain()
                        for c in range(2):
                            dve.tensor_tensor_scan(cumT[:, c, :], K["reset"], laT[:, c, :], 0.0, ALU.mult, ALU.add)
                        dve.drain()
                        ends = cumT[:].rearrange("p c (n i) -> p c n i", i=GCH)
                        gam = col(128, 16).rearrange("p (c n) -> p c n", c=2)
                        dve.tensor_copy(gam, ends[:, :, :, GCH - 1:GCH].rearrange("p c n o -> p c (n o)")).then_inc(S_.cum_ready, 1)
                        dve.wait_ge(S_.gexp_ready, L * 2 + 1)
                        for c in range(2):
                            m = dve.tensor_tensor(ends[:, c], spread(gam[:, c, :], 2, GCH), ends[:, c], ALU.subtract)
                        m.then_inc(S_.rest_ready, 1)
                        dve.tensor_tensor(qcT[:], qcT[:], egT[:], ALU.mult)
                        dve.tensor_tensor(laT[:], kcT[:], laT[:], ALU.mult)
                    split(u + (n + AHEAD))
                    if n < 8:
                        convolve((CW - taps[0] + 1) // 2 if n == 6 else CW - taps[0])
                dve.wait_ge(S_.gexp_ready, L * 2 + 2)
                dve.tensor_tensor(cumT[:], kcT[:], cumT[:], ALU.mult).then_inc(S_.qkg_ready, 1)
                dve.wait_ge(S_.pv2, L * HB + HB)
                yh = yb[:].rearrange("p t (h e) -> p t h e", h=HB)
                for t in range(TT):
                    dve.tensor_tensor(yh[:, t], bank(4 + t, HB, HDB), spread(col(176 + 4 * t, 4), 2, HDB), ALU.mult)
                dve.drain()
                yq = yb[:].rearrange("p t (h e) -> p (t h) e", h=HB)
                sq = sb0[:].rearrange("p h n -> p (h n)").rearrange("p (a e) -> p a e", e=HDB)
                dve.tensor_tensor(sq, yq, yq, ALU.mult)
                dve.drain()
                dve.reduce_sum(col(112, 8), sq, AX_X)
                dve.drain()
                dve.tensor_scalar(col(112, 8), col(112, 8), 1.0 / HDB, RMS_EPS, ALU.mult, ALU.add).then_inc(S_.sqrt2_in, 1)
                dve.wait_ge(S_.conv_part_ready, L + 1)
                dve.tensor_tensor(cvT[:], cvT[:], conv_part, ALU.add).then_inc(S_.conv_ready, 1)
                dve.wait_ge(S_.sqrt2_out, L * 5 + 2)
                dve.reciprocal(col(112, 8), col(112, 8))
                dve.drain()
                dve.tensor_tensor(yq, yq, spread(col(112, 8), 2, HDB), ALU.mult)
                dve.drain()
                dve.tensor_tensor(yb[:], yb[:], spread(gain_b[:], 1, TT), ALU.mult).then_inc(S_.yb_ready, 1)
                dve.wait_ge(S_.yT2_hi_ready, L * 4 + 1)
                dve.tensor_tensor(yA_lo[:, 2:4, :], bank(6, 2, S), yA_hi[:, 2:4, :].bitcast(F32), ALU.subtract)\
                   .then_inc(S_.yT2_lo_ready, 1)
                dve.wait_ge(S_.csum_psum, L + 1)
                for c in range(2):
                    m = dve.scalar_tensor_tensor(cvT[:, c, :], ps[:, 7, 0:S], -1.0 / S, cvT[:, c, :], ALU.mult, ALU.add)
                m.then_inc(S_.cent_ready, 1)
                dve.wait_ge(S_.at_psum, L + 1)
                for q in range(2):
                    m = dve.tensor_tensor(atT[:, q::2], bank(1 + q, 2, TT, P), spread(spread(K["glamask"], 1, TT), 1, 2), ALU.mult)
                m.then_inc(S_.at_ready, 1)
                for n in range(NCH - 1):
                    dve.wait_ge(S_.ds_psum, L * (NCH - 1) + (n + 1))
                    for c in range(2):
                        for half in range(2):
                            rows = slice(64 * half, 64 * half + 64)
                            add = bank(3 + n % 2, 2, S)[rows, c, half * GDV:(half + 1) * GDV]
                            if n == 0:
                                m = dve.tensor_copy(st8[rows, 1, c, :], add)
                            else:
                                m = dve.scalar_tensor_tensor(st8[rows, n + 1, c, :], st8[rows, n, c, :], dec[rows, c, n:n + 1],
                                                             add, ALU.mult, ALU.add)
                    m.then_inc(S_.state_ready, 1)
                    dve.drain()
                dve.wait_ge(S_.cvar_psum, L + 1)
                dve.tensor_scalar(agT[:, 0, :], ps[:, 7, S:2 * S], 1.0 / S, LN_EPS, ALU.mult, ALU.add).then_inc(S_.sqrt2_in, 1)
                dve.wait_ge(S_.sqrt2_out, L * 5 + 3)
                dve.reciprocal(agT[:, 0, :], agT[:, 0, :])
                dve.drain()
                dve.tensor_tensor(cvT[:], cvT[:], spread(agT[:, 0, :], 1, 2), ALU.mult).then_inc(S_.cnorm_ready, 1)
                dve.wait_ge(S_.yT2_hi_ready, L * 4 + 2)
                dve.tensor_tensor(yA_lo[:, 0:2, :], cvT[:], yA_hi[:, 0:2, :].bitcast(F32), ALU.subtract).then_inc(S_.yT2_lo_ready, 1)
                dve.wait_ge(S_.osum_psum, L + 1)
                dve.tensor_scalar(col(96, 8), ps[:, 0, 0:8], 1.0 / GDV, RMS_EPS, ALU.mult, ALU.add).then_inc(S_.sqrt2_in, 1)
                for h in range(GH):
                    at_h = 2 * (h % 2) + h // 2
                    dve.scalar_tensor_tensor(rT[:, h, :], bank(5, 4, S)[:, at_h, :], cols2[:, 70 + h:71 + h], rT[:, h, :],
                                             ALU.mult, ALU.mult)
                dve.wait_ge(S_.sqrt2_out, L * 5 + 4)
                dve.reciprocal(col(96, 8), col(96, 8))
                dve.drain()
                dve.tensor_tensor(rv[:].rearrange("p h (t n) -> p (h t) n", t=TT), spread(ident, 1, GH * TT),
                                  spread(col(96, 8), 2, P), ALU.mult).then_inc(S_.odiag_ready, 1)
                dve.wait_ge(S_.oscale_psum, L + 1)
                for q in range(2):
                    dve.tensor_tensor(oc[:, 2 * q:2 * q + 2, :], rT[:, 2 * q:2 * q + 2, :], bank(1, 4, S)[:, q::2, :], ALU.mult)\
                       .then_inc(S_.oc_ready, 1)
                for q in range(2):
                    dve.wait_ge(S_.yT2_hi_ready, L * 4 + 3 + q)
                    dve.tensor_tensor(yM_lo[:, 2 * q:2 * q + 2, :], oc[:, 2 * q:2 * q + 2, :],
                                      yM_hi[:, 2 * q:2 * q + 2, :].bitcast(F32), ALU.subtract).then_inc(S_.yT2_lo_ready, 1)
                for n in range(4):
                    split(u + (11 + n + AHEAD))
                used(u + 14)
                for t in range(TT):
                    dve.tensor_tensor(x[:, t, :], x[:, t, :], bank(2 * t, D), ALU.add)
                dve.drain()
                rms_norm(L * 5 + 5, L * 32 + 32, S_.xn_ready)
                dve.memset(u_a[:, :, :, 0:2], 0.0)
                dve.memset(u_g[:, :, :, 0:2], 0.0)
                dve.drain()
                x_parts(L * 8 + 28)

            def conv_ffn(L):
                def hidden(at, odd, dyn, after):
                    j = Count(dyn.const, dyn.terms[1:]).value() * 2

                    def columns(src, dst, first):
                        for k in range(3):
                            for c in range(2):
                                w = cols2[:, bass.ds(j + (74 + 44 * k + first + c), 1)]
                                if k == 0:
                                    b = cols2[:, bass.ds(j + (74 + 132 + first + c), 1)]
                                    m = dve.tensor_scalar(dst[:, c, :], src[:, odd, c, 0:S], w, b, ALU.mult, ALU.add)
                                else:
                                    m = dve.scalar_tensor_tensor(dst[:, c, :], src[:, odd, c, k:k + S], w, dst[:, c, :],
                                                                 ALU.mult, ALU.add)
                            if k < 2:
                                dve.drain()
                        return m

                    dve.wait_ge(S_.ua_ready, dyn.value(plus=1))
                    columns(u_a, c_a[:, odd], 0).then_inc(S_.ca_ready, 1)
                    split(after)
                    dve.wait_ge(S_.ug_ready, dyn.value(plus=1))
                    columns(u_g, c_g, 22)
                    dve.drain()
                    dve.wait_ge(S_.silu2_ready, dyn.value(plus=1))
                    dve.tensor_tensor(h2f[:, odd].rearrange("p (c n) -> p c n", c=2), c_a[:, odd], c_g[:], ALU.mult)\
                       .then_inc(S_.h2_ready, 1)
                return hidden

            dve.memset(zeros[:], 0.0)
            dve.memset(stat[:, 1:2], 0.0).then_inc(S_.h1_ready, 2)
            dve.memset(stat[:, 2:3], 0.0).then_inc(S_.h2_ready, 2)
            dve.memset(stat[:, 3:4], 0.0).then_inc(S_.lo_ready, RAW)
            dve.memset(stat[:, 4:5], 0.0).then_inc(S_.xn_ready, 1)
            for n in range(AHEAD):
                split(Count(n))
            with dve.Fori(0, 2) as L:
                mixer1(L, Count(0).loop(L, LAYER1_UNITS))
                with dve.If(L == 0):
                    feed_forward(Count(MIX1_UNITS), DENSE_STEPS, Count(0), hT_hi, hT_lo, F1, dense_hidden)
                    split_next(Count(LAYER1_UNITS))
                    dve.wait_ge(S_.sums_closed, 1)
                    add_to_x()
                with dve.Else():
                    router()
                    experts(dve.value_load(passes_sb[0:1, 0:1], min_val=1, max_val=2))
                layer_norm(L * 3 + 3, L * 64 + 64)
            dve.wait_ge(S_.const2_loaded, 16)
            passes = dve.value_load(passes_sb[0:1, 0:1], min_val=1, max_val=2)
            with dve.Fori(0, 2) as L:
                u = block2_units(passes).loop(L, LAYER2_UNITS)
                mixer2(L, u)
                at = u + MIX2_UNITS
                feed_forward(at, DENSE_STEPS, Count(0).loop(L, DENSE_STEPS), h2_hi, h2_lo, F2, conv_ffn(L))
                with dve.If(L == 0):
                    split_next(at + STEP * DENSE_STEPS)
                with dve.Else():
                    dve.nop()
                dve.wait_ge(S_.sums_closed, L + 2)
                for t in range(TT):
                    dve.tensor_tensor(x[:, t, :], x[:, t, :], bank(2 * t, D), ALU.add)
                dve.drain()
            rms_norm(11, 80, S_.result_ready)


_OUTS = [((1, S, D), "float32")]


def kernel(**inputs):
    import concourse.bacc as _bacc
    from concourse.bass_utils import run_bass_kernel_spmd as _run

    nc = _bacc.Bacc("TRN2", target_bir_lowering=False, num_devices=1)
    arrays = {name: np.ascontiguousarray(a) for name, a in inputs.items()}
    packed, onehot = constants()
    arrays.update({f"const{i}": a for i, a in enumerate(packed)})
    arrays["onehot"] = onehot
    A = {name: nc.dram_tensor(f"in_{name}", a.shape, mybir.dt.from_np(a.dtype), kind="ExternalInput").ap()
         for name, a in arrays.items()}
    out = nc.dram_tensor("out_0", *_OUTS[0][:1], F32, kind="ExternalOutput").ap()
    build(nc, A, out)
    r = _run(nc, [{f"in_{name}": a for name, a in arrays.items()}], core_ids=[0])
    return r.results[0]["out_0"]
```
